# Optimizing a Trainium2 kernel written in Bass

```python
import math
import jax
import jax.numpy as jnp
from jax import lax
import numpy as np
import jax, jax.numpy as jnp

D_MODEL = 1024
BATCH = 1
SEQ = 256
DEPTH = 1

HEAD_DIM = 64
CONV_CH = 256
CONV_WIDTH = 31
N_Q_HEADS = 12
N_KV_HEADS = 4
Q_PER_KV = N_Q_HEADS // N_KV_HEADS
NSA_WIDTH = N_Q_HEADS * HEAD_DIM
MIX_WIDTH = CONV_CH + NSA_WIDTH
KV_WIDTH = N_KV_HEADS * HEAD_DIM
CMP_LEN = 32
CMP_STRIDE = 16
CMP_HIDDEN = 256
SEL_BLOCK = 64
SEL_TOPK = 8
WINDOW = 512
Q_BLOCK = 64
N_BRANCH = 3
FORCED_BONUS = 1000.0
D_FF = -(-8 * D_MODEL // (3 * 256)) * 256
IN_COLS = 2 * CONV_CH + NSA_WIDTH + 6 * KV_WIDTH + N_BRANCH * N_Q_HEADS
EPS = 1e-6


def rms_norm(x, g):
    xf = x.astype(jnp.float32)
    y = xf * lax.rsqrt(jnp.mean(xf * xf, axis=-1, keepdims=True) + EPS)
    return (y * g.astype(jnp.float32)).astype(x.dtype)

def layer_norm(x, g, b):
    xf = x.astype(jnp.float32)
    mu = jnp.mean(xf, axis=-1, keepdims=True)
    var = jnp.mean(jnp.square(xf - mu), axis=-1, keepdims=True)
    y = (xf - mu) * lax.rsqrt(var + EPS)
    return (y * g.astype(jnp.float32) + b.astype(jnp.float32)).astype(x.dtype)

def alibi_slopes(n):
    def pow2_slopes(m):
        start = 2.0 ** (-8.0 / m)
        return [start ** (i + 1) for i in range(m)]
    if math.log2(n).is_integer():
        s = pow2_slopes(n)
    else:
        c = 2 ** math.floor(math.log2(n))
        s = pow2_slopes(c) + pow2_slopes(2 * c)[0::2][: n - c]
    return np.asarray(s, dtype=np.float32)

def masked_softmax(s, mask):
    s = jnp.where(mask, s.astype(jnp.float32), -jnp.inf)
    m = jnp.max(s, axis=-1, keepdims=True)
    m = jnp.where(jnp.isfinite(m), m, 0.0)
    p = jnp.exp(s - m)
    return p / jnp.maximum(jnp.sum(p, axis=-1, keepdims=True), 1e-30)

def conv_mixer(a, w_dw, b_dw, ln_g, ln_b):
    u, v = jnp.split(a, 2, axis=-1)
    y = u * jax.nn.sigmoid(v)
    y = lax.conv_general_dilated(
        y, w_dw[:, None, :], window_strides=(1,),
        padding=[(CONV_WIDTH - 1, 0)],
        dimension_numbers=("NWC", "WIO", "NWC"),
        feature_group_count=CONV_CH) + b_dw
    y = layer_norm(y, ln_g, ln_b)
    return jax.nn.silu(y)

def compress(kr, pe, w1, w2):
    b, t = kr.shape[:2]
    chunks = kr.reshape(b, t // CMP_STRIDE, CMP_STRIDE, N_KV_HEADS, HEAD_DIM)
    lo = jnp.einsum("bclgd,ldh->bcgh", chunks, w1[:CMP_STRIDE])
    hi = jnp.einsum("bclgd,ldh->bcgh", chunks, w1[CMP_STRIDE:])
    h = lo[:, :-1] + hi[:, 1:] + jnp.einsum("ld,ldh->h", pe, w1)
    return jnp.einsum("bngh,hd->bngd", jax.nn.silu(h), w2)

def nsa_attention(q, kc, vc, ks, vs, kw, vw, gates):
    b, t = q.shape[:2]
    n_cmp = kc.shape[1]
    n_sel = t // SEL_BLOCK
    k_top = min(SEL_TOPK, n_sel)
    scale = HEAD_DIM ** -0.5
    slopes = jnp.asarray(alibi_slopes(N_Q_HEADS)).reshape(N_KV_HEADS, Q_PER_KV)[None, :, :, None, None]
    cmp_idx = jnp.arange(n_cmp)
    cmp_start = cmp_idx * CMP_STRIDE
    cmp_center = cmp_start.astype(jnp.float32) + 0.5 * (CMP_LEN - 1)
    cmp_end = cmp_start + CMP_LEN - 1
    sel_start = jnp.arange(n_sel) * SEL_BLOCK
    overlap = ((cmp_start[:, None] < sel_start[None, :] + SEL_BLOCK)
               & (cmp_start[:, None] + CMP_LEN > sel_start[None, :])).astype(jnp.float32)
    ks_blk = ks.reshape(b, n_sel, SEL_BLOCK, N_KV_HEADS, HEAD_DIM).transpose(0, 3, 1, 2, 4)
    vs_blk = vs.reshape(b, n_sel, SEL_BLOCK, N_KV_HEADS, HEAD_DIM).transpose(0, 3, 1, 2, 4)
    pad = ((0, 0), (WINDOW, 0), (0, 0), (0, 0))
    kw_pad = jnp.pad(kw, pad)
    vw_pad = jnp.pad(vw, pad)
    b_idx = jnp.arange(b)[:, None, None, None]
    g_idx = jnp.arange(N_KV_HEADS)[None, :, None, None]
    offs = jnp.arange(SEL_BLOCK)
    win_offs = jnp.arange(WINDOW + Q_BLOCK) - WINDOW
    sel_j = jnp.arange(n_sel)

    def block(i):
        t0 = i * Q_BLOCK
        tq = t0 + jnp.arange(Q_BLOCK)
        tqf = tq.astype(jnp.float32)
        qb = lax.dynamic_slice_in_dim(q, t0, Q_BLOCK, axis=1) * scale
        gb = lax.dynamic_slice_in_dim(gates, t0, Q_BLOCK, axis=1)

        s_c = jnp.einsum("bqgrd,bngd->bgrqn", qb, kc) - slopes * (tqf[:, None] - cmp_center[None, :])
        p_c = masked_softmax(s_c, cmp_end[None, :] <= tq[:, None])
        o_c = jnp.einsum("bgrqn,bngd->bqgrd", p_c, vc)

        imp = jnp.einsum("bgrqn,nj->bgqj", p_c, overlap)
        cur = tq // SEL_BLOCK
        forced = ((sel_j[None, :] == 0) | (sel_j[None, :] == cur[:, None])
                  | (sel_j[None, :] == cur[:, None] - 1))
        imp = jnp.where(sel_j[None, :] <= cur[:, None],
                        imp + FORCED_BONUS * forced.astype(jnp.float32), -jnp.inf)
        top_s, top_i = lax.top_k(imp, k_top)

        kg = ks_blk[b_idx, g_idx, top_i]
        vg = vs_blk[b_idx, g_idx, top_i]
        pos = top_i[..., None] * SEL_BLOCK + offs
        mask_s = jnp.isfinite(top_s)[..., None] & (pos <= tq[None, None, :, None, None])
        dist_s = (tqf[None, None, :, None, None] - pos.astype(jnp.float32))[:, :, None]
        s_s = jnp.einsum("bqgrd,bgqksd->bgrqks", qb, kg) - slopes[..., None] * dist_s
        s_s = s_s.reshape(b, N_KV_HEADS, Q_PER_KV, Q_BLOCK, k_top * SEL_BLOCK)
        p_s = masked_softmax(s_s, mask_s.reshape(b, N_KV_HEADS, 1, Q_BLOCK, k_top * SEL_BLOCK))
        o_s = jnp.einsum("bgrqs,bgqsd->bqgrd", p_s,
                         vg.reshape(b, N_KV_HEADS, Q_BLOCK, k_top * SEL_BLOCK, HEAD_DIM))

        kwb = lax.dynamic_slice_in_dim(kw_pad, t0, WINDOW + Q_BLOCK, axis=1)
        vwb = lax.dynamic_slice_in_dim(vw_pad, t0, WINDOW + Q_BLOCK, axis=1)
        pos_w = t0 + win_offs
        dist_w = tq[:, None] - pos_w[None, :]
        mask_w = (dist_w >= 0) & (dist_w < WINDOW) & (pos_w[None, :] >= 0)
        s_w = jnp.einsum("bqgrd,bkgd->bgrqk", qb, kwb) - slopes * dist_w.astype(jnp.float32)
        p_w = masked_softmax(s_w, mask_w)
        o_w = jnp.einsum("bgrqk,bkgd->bqgrd", p_w, vwb)

        out = gb[..., 0:1] * o_c + gb[..., 1:2] * o_s + gb[..., 2:3] * o_w
        return out.astype(q.dtype)

    outs = lax.map(block, jnp.arange(t // Q_BLOCK))
    return jnp.moveaxis(outs, 0, 1).reshape(b, t, NSA_WIDTH)

def hybrid_layer(x, attn_norm, w_in, conv_w, conv_b, conv_ln_g, conv_ln_b,
                 cmp_k_pe, cmp_k_w1, cmp_k_w2, cmp_v_pe, cmp_v_w1, cmp_v_w2,
                 w_out, ffn_norm, w_gate_up, w_down):
    b, t, _ = x.shape
    h = rms_norm(x, attn_norm)
    z = h @ w_in
    splits = np.cumsum([2 * CONV_CH, NSA_WIDTH] + [KV_WIDTH] * 6).tolist()
    a_conv, q, kc_r, vc_r, ks, vs, kw, vw, g = jnp.split(z, splits, axis=-1)
    kv_shape = (b, t, N_KV_HEADS, HEAD_DIM)
    conv_out = conv_mixer(a_conv, conv_w, conv_b, conv_ln_g, conv_ln_b)
    kc = compress(kc_r.reshape(kv_shape), cmp_k_pe, cmp_k_w1, cmp_k_w2)
    vc = compress(vc_r.reshape(kv_shape), cmp_v_pe, cmp_v_w1, cmp_v_w2)
    gates = jax.nn.sigmoid(g).reshape(b, t, N_KV_HEADS, Q_PER_KV, N_BRANCH)
    nsa_out = nsa_attention(q.reshape(b, t, N_KV_HEADS, Q_PER_KV, HEAD_DIM), kc, vc,
                            ks.reshape(kv_shape), vs.reshape(kv_shape),
                            kw.reshape(kv_shape), vw.reshape(kv_shape), gates)
    mix = jnp.concatenate([conv_out, nsa_out.astype(conv_out.dtype)], axis=-1)
    x = x + mix @ w_out
    h = rms_norm(x, ffn_norm)
    gu = h @ w_gate_up
    gate, up = jnp.split(gu, 2, axis=-1)
    return x + (jax.nn.silu(gate) * up) @ w_down

def first_inputs(seed: int = 0) -> dict:
    key = jax.random.key(seed)
    ks = jax.random.split(key, 20)
    f32 = jnp.float32

    def nrm(k, shape, scale):
        return jax.random.normal(k, shape, f32) * scale

    return {
        "x": nrm(ks[0], (BATCH, SEQ, D_MODEL), 1.0),
        "attn_norm": 1.0 + nrm(ks[1], (DEPTH, D_MODEL), 0.05),
        "w_in": nrm(ks[2], (DEPTH, D_MODEL, IN_COLS), D_MODEL ** -0.5),
        "conv_w": nrm(ks[3], (DEPTH, CONV_WIDTH, CONV_CH), CONV_WIDTH ** -0.5),
        "conv_b": nrm(ks[4], (DEPTH, CONV_CH), 0.01),
        "conv_ln_g": 1.0 + nrm(ks[5], (DEPTH, CONV_CH), 0.05),
        "conv_ln_b": nrm(ks[6], (DEPTH, CONV_CH), 0.01),
        "cmp_k_pe": nrm(ks[7], (DEPTH, CMP_LEN, HEAD_DIM), 0.1),
        "cmp_k_w1": nrm(ks[8], (DEPTH, CMP_LEN, HEAD_DIM, CMP_HIDDEN), (CMP_LEN * HEAD_DIM) ** -0.5),
        "cmp_k_w2": nrm(ks[9], (DEPTH, CMP_HIDDEN, HEAD_DIM), CMP_HIDDEN ** -0.5),
        "cmp_v_pe": nrm(ks[10], (DEPTH, CMP_LEN, HEAD_DIM), 0.1),
        "cmp_v_w1": nrm(ks[11], (DEPTH, CMP_LEN, HEAD_DIM, CMP_HIDDEN), (CMP_LEN * HEAD_DIM) ** -0.5),
        "cmp_v_w2": nrm(ks[12], (DEPTH, CMP_HIDDEN, HEAD_DIM), CMP_HIDDEN ** -0.5),
        "w_out": nrm(ks[13], (DEPTH, MIX_WIDTH, D_MODEL), MIX_WIDTH ** -0.5),
        "ffn_norm": 1.0 + nrm(ks[14], (DEPTH, D_MODEL), 0.05),
        "w_gate_up": nrm(ks[15], (DEPTH, D_MODEL, 2 * D_FF), D_MODEL ** -0.5),
        "w_down": nrm(ks[16], (DEPTH, D_FF, D_MODEL), D_FF ** -0.5),
        "final_norm": 1.0 + nrm(ks[17], (D_MODEL,), 0.05),
    }

def first_block(x, attn_norm, w_in, conv_w, conv_b, conv_ln_g, conv_ln_b,
              cmp_k_pe, cmp_k_w1, cmp_k_w2, cmp_v_pe, cmp_v_w1, cmp_v_w2,
              w_out, ffn_norm, w_gate_up, w_down, final_norm):
    for l in range(DEPTH):
        x = hybrid_layer(x, attn_norm[l], w_in[l], conv_w[l], conv_b[l], conv_ln_g[l], conv_ln_b[l],
                         cmp_k_pe[l], cmp_k_w1[l], cmp_k_w2[l], cmp_v_pe[l], cmp_v_w1[l], cmp_v_w2[l],
                         w_out[l], ffn_norm[l], w_gate_up[l], w_down[l])
    return rms_norm(x, final_norm)


N_HEADS_A = 8
N_HEADS_B = 8
WIDTH_A = N_HEADS_A * HEAD_DIM
WIDTH_B = N_HEADS_B * HEAD_DIM
ROPE_DIM = HEAD_DIM // 4
ROPE_THETA = 500000.0
IDX_HEADS = 8
IDX_DIM = 64
TOPK_MAX = 256
BLOCK_Q = 128
D_FF_2 = 4 * D_MODEL
IN_SPLITS = (WIDTH_A, WIDTH_A, WIDTH_A,
             WIDTH_B, WIDTH_B, WIDTH_B,
             IDX_HEADS * IDX_DIM, IDX_DIM,
             IDX_HEADS,
             D_MODEL, D_MODEL)
IN_COLS_2 = sum(IN_SPLITS)


def rmsnorm(x, g):
    x32 = x.astype(jnp.float32)
    y = x32 * lax.rsqrt(jnp.mean(x32 * x32, axis=-1, keepdims=True) + EPS)
    return (y * g.astype(jnp.float32)).astype(x.dtype)

def rope_tables(seq_len):
    pos = jnp.arange(seq_len, dtype=jnp.float32)
    inv_freq = ROPE_THETA ** (-jnp.arange(0, ROPE_DIM, 2, dtype=jnp.float32) / ROPE_DIM)
    ang = pos[:, None] * inv_freq[None, :]
    return jnp.cos(ang), jnp.sin(ang)

def partial_rope(x, cos, sin):
    half = ROPE_DIM // 2
    x1 = x[..., :half]
    x2 = x[..., half:ROPE_DIM]
    cos = cos.astype(x.dtype)
    sin = sin.astype(x.dtype)
    return jnp.concatenate([x1 * cos - x2 * sin, x2 * cos + x1 * sin, x[..., ROPE_DIM:]], axis=-1)

def to_blocks(a, nblk):
    return a.reshape((a.shape[0], nblk, BLOCK_Q) + a.shape[2:]).swapaxes(0, 1)

def from_blocks(a):
    a = a.swapaxes(0, 1)
    return a.reshape((a.shape[0], a.shape[1] * a.shape[2]) + a.shape[3:])

def token_mixers(q_a, k_a, v_a, q_b, k_b, v_b, q_i, k_i, w_i):
    L = q_a.shape[1]
    nblk = L // BLOCK_Q
    topk = min(TOPK_MAX, L // 4)
    f32 = jnp.float32
    key_pos = jnp.arange(L, dtype=jnp.int32)
    scale = HEAD_DIM ** -0.5
    idx_scale = (IDX_DIM ** -0.5) * (IDX_HEADS ** -0.5)

    def block_fn(args):
        qa, qi, wi, qb, t0 = args
        t = t0 + jnp.arange(BLOCK_Q, dtype=jnp.int32)
        rel = jax.nn.relu(jnp.einsum('bqhd,bsd->bqhs', qi, k_i).astype(f32))
        isc = jnp.einsum('bqhs,bqh->bqs', rel, wi.astype(f32)) * idx_scale
        causal = key_pos[None, :] <= t[:, None]
        isc = jnp.where(causal[None], isc, -jnp.inf)
        _, sel = lax.top_k(isc, topk)
        valid = sel <= t[None, :, None]
        kg = jax.vmap(lambda kb, ib: kb[ib])(k_a, sel)
        vg = jax.vmap(lambda vb, ib: vb[ib])(v_a, sel)
        logit = jnp.einsum('bqhd,bqkhd->bqhk', qa, kg).astype(f32) * scale
        logit = jnp.where(valid[:, :, None, :], logit, -jnp.inf)
        p = jax.nn.softmax(logit, axis=-1).astype(vg.dtype)
        oa = jnp.einsum('bqhk,bqkhd->bqhd', p, vg)
        z = jnp.einsum('bqhd,bshd->bhqs', qb, k_b).astype(f32) * scale
        strict = (key_pos[None, :] < t[:, None])[None, None]
        log_1mb = jnp.where(strict, jax.nn.log_sigmoid(-z), 0.0)
        after = lax.cumsum(log_1mb, axis=3, reverse=True) - log_1mb
        att = jnp.where(strict, jnp.exp(jax.nn.log_sigmoid(z) + after), 0.0)
        ob = jnp.einsum('bhqs,bshd->bqhd', att.astype(v_b.dtype), v_b)
        return oa, ob

    starts = jnp.arange(nblk, dtype=jnp.int32) * BLOCK_Q
    oa, ob = lax.map(block_fn, (to_blocks(q_a, nblk), to_blocks(q_i, nblk),
                                to_blocks(w_i, nblk), to_blocks(q_b, nblk), starts))
    return from_blocks(oa), from_blocks(ob)

def second_inputs(seed: int = 0) -> dict:
    key = jax.random.key(seed)
    ks = jax.random.split(key, 16)
    f32 = jnp.float32
    nrm = lambda k, shape, fan_in: jax.random.normal(k, shape, f32) * (fan_in ** -0.5)
    gain = lambda k: 1.0 + 0.05 * jax.random.normal(k, (DEPTH, D_MODEL), f32)
    return {
        "x": jax.random.normal(ks[0], (BATCH, SEQ, D_MODEL), f32),
        "c": jax.random.normal(ks[1], (BATCH, D_MODEL), f32),
        "w_ada": nrm(ks[2], (DEPTH, D_MODEL, 6 * D_MODEL), D_MODEL),
        "b_ada": 0.01 * jax.random.normal(ks[3], (DEPTH, 6 * D_MODEL), f32),
        "g_pre_mix": gain(ks[4]),
        "w_in": nrm(ks[5], (DEPTH, D_MODEL, IN_COLS_2), D_MODEL),
        "w_up_a": nrm(ks[6], (DEPTH, WIDTH_A, D_MODEL), WIDTH_A),
        "w_up_b": nrm(ks[7], (DEPTH, WIDTH_B, D_MODEL), WIDTH_B),
        "w_out": nrm(ks[8], (DEPTH, D_MODEL, D_MODEL), D_MODEL),
        "g_post_mix": gain(ks[9]),
        "g_pre_ffn": gain(ks[10]),
        "w_ff1": nrm(ks[11], (DEPTH, D_MODEL, D_FF_2), D_MODEL),
        "w_ff2": nrm(ks[12], (DEPTH, D_FF_2, D_MODEL), D_FF_2),
        "g_post_ffn": gain(ks[13]),
    }

def second_block(x, c, w_ada, b_ada, g_pre_mix, w_in, w_up_a, w_up_b, w_out, g_post_mix,
              g_pre_ffn, w_ff1, w_ff2, g_post_ffn):
    B, L, D = x.shape
    cos, sin = rope_tables(L)
    cos_h, sin_h = cos[:, None, :], sin[:, None, :]
    split_at = list(np.cumsum(IN_SPLITS)[:-1])
    for l in range(DEPTH):
        mod = jax.nn.silu(c) @ w_ada[l] + b_ada[l]
        sh1, sc1, ga1, sh2, sc2, ga2 = [m[:, None, :] for m in jnp.split(mod, 6, axis=-1)]

        h = rmsnorm(x, g_pre_mix[l]) * (1.0 + sc1) + sh1
        proj = h @ w_in[l]
        qa, ka, va, qb, kb, vb, qi, ki, wi, gate_a, gate_b = jnp.split(proj, split_at, axis=-1)
        heads = lambda t, n: t.reshape(B, L, n, HEAD_DIM)
        qa = partial_rope(heads(qa, N_HEADS_A), cos_h, sin_h)
        ka = partial_rope(heads(ka, N_HEADS_A), cos_h, sin_h)
        va = heads(va, N_HEADS_A)
        qb, kb, vb = heads(qb, N_HEADS_B), heads(kb, N_HEADS_B), heads(vb, N_HEADS_B)
        qi = partial_rope(qi.reshape(B, L, IDX_HEADS, IDX_DIM), cos_h, sin_h)
        ki = partial_rope(ki, cos, sin)
        oa, ob = token_mixers(qa, ka, va, qb, kb, vb, qi, ki, wi)
        ya = oa.reshape(B, L, WIDTH_A) @ w_up_a[l]
        yb = ob.reshape(B, L, WIDTH_B) @ w_up_b[l]
        merged = jax.nn.sigmoid(gate_a) * ya + jax.nn.sigmoid(gate_b) * yb
        y = merged @ w_out[l]
        x = x + ga1 * rmsnorm(y, g_post_mix[l])

        h = rmsnorm(x, g_pre_ffn[l]) * (1.0 + sc2) + sh2
        u = jax.nn.relu(h @ w_ff1[l])
        y = (u * u) @ w_ff2[l]
        x = x + ga2 * rmsnorm(y, g_post_ffn[l])
    return x


def setup_inputs(seed=0):
    out = dict(first_inputs(seed))
    for name, value in second_inputs(seed + 1).items():
        if name != "x":
            out[name + "_2"] = value
    return out


def reference(
    x, attn_norm, w_in, conv_w, conv_b, conv_ln_g, conv_ln_b, cmp_k_pe, cmp_k_w1, cmp_k_w2,
    cmp_v_pe, cmp_v_w1, cmp_v_w2, w_out, ffn_norm, w_gate_up, w_down, final_norm, c_2, w_ada_2,
    b_ada_2, g_pre_mix_2, w_in_2, w_up_a_2, w_up_b_2, w_out_2, g_post_mix_2, g_pre_ffn_2,
    w_ff1_2, w_ff2_2, g_post_ffn_2,
):
    x = first_block(
        x, attn_norm, w_in, conv_w, conv_b, conv_ln_g, conv_ln_b, cmp_k_pe, cmp_k_w1, cmp_k_w2,
        cmp_v_pe, cmp_v_w1, cmp_v_w2, w_out, ffn_norm, w_gate_up, w_down, final_norm,
    )
    return second_block(
        x, c_2, w_ada_2, b_ada_2, g_pre_mix_2, w_in_2, w_up_a_2, w_up_b_2, w_out_2,
        g_post_mix_2, g_pre_ffn_2, w_ff1_2, w_ff2_2, g_post_ffn_2,
    )


_drawn_inputs = setup_inputs


def setup_inputs(seed=0):
    import zlib

    import numpy as np

    out = dict(_drawn_inputs(seed))
    spreads = {}
    factors = {'conv_b': 5.001, 'conv_ln_b': 6.7, 'cmp_k_pe': 8.0}
    for name, (base, spread) in spreads.items():
        noise = np.random.default_rng([zlib.crc32(name.encode()), seed]).standard_normal(out[name].shape)
        drawn = base * np.exp(spread * noise) if base else spread * noise
        out[name] = jnp.asarray(drawn.astype(out[name].dtype))
    for name, factor in factors.items():
        out[name] = (out[name] * factor).astype(out[name].dtype)
    return out
```

```python
import math
from contextlib import ExitStack

import numpy as np

import concourse.bass as bass
from concourse import mybir

F32 = mybir.dt.float32
F32R = mybir.dt.float32r
ALU = mybir.AluOpType
ACT = mybir.ActivationFunctionType
AX = mybir.AxisListType

P = 128
T = 256
D = 1024
DC = D // P
HD = 64
EPS = 1e-6
CONV_W = 31
NQ, NKV = 12, 4
NB_HEADS = 8
TOPK = T // 4
N_CMP = 15
CMP_SLOT = 16
FF1_STEPS = 11
FF2_STEPS = 16
NEG = -1.0e30
TAKEN = -3.0e38

TW = 2048
RAW, RING = 6, 3

def plan():
    tiles = [("s", n) for n in ("u", "v", "q0", "q1", "q2", "kc", "vc", "ks", "kw", "vs", "vw", "g")]
    tiles += [("s", f"out{i}") for i in range(3)]
    tiles += [("d", f"cmp{i}") for i in range(4)] + [("d", f"ada{i}") for i in range(24)]
    tiles += [("s", "out3"), ("s", "gate0"), ("s", "up0")]
    for i in range(1, FF1_STEPS):
        tiles += [("s", f"gate{i}"), ("s", f"up{i}"), ("s", f"down{i - 1}")]
    tiles += [("s", f"down{FF1_STEPS - 1}")]
    tiles += [("s", n) for n in ("idx", "qi0", "qi1", "qa0", "qa1", "ka0", "ka1", "qb0", "qb1", "kb0", "kb1",
                                 "va0", "va1", "vb0", "vb1")]
    tiles += [("s", f"sg{i}") for i in range(8)]
    tiles += [("s", n) for n in ("upa0", "upb0", "upa1", "upb1")] + [("s", f"o2{i}") for i in range(4)]
    tiles += [("s", "fa0")]
    for i in range(1, FF2_STEPS):
        tiles += [("s", f"fa{i}"), ("s", f"fb{i - 1}")]
    tiles += [("s", f"fb{FF2_STEPS - 1}")]
    return tiles


TILES = plan()
G_COLS = 36
IDX_COLS = 136

VEC_A = {}
for _name, _rows in (("attn_norm", 8), ("ffn_norm", 8), ("g_pre_mix", 8), ("g_pre_ffn", 8), ("c", 8), ("b_ada", 48),
                     ("conv_b", 2), ("ln_g", 2), ("ln_b", 2), ("g_post_mix", 8), ("g_post_ffn", 8), ("final", 8)):
    VEC_A[_name] = (sum(r for _, r in VEC_A.values()), _rows)
NA_ROWS = sum(r for _, r in VEC_A.values())
NB_ROWS = 2 * CONV_W + 32

CONST = {}
for _name, _w in (("ident", 128), ("causal", 256), ("tri", 128), ("negones", 128), ("strict", 128), ("mean", 128),
                  ("ones", 128)):
    CONST[_name] = (sum(w for _, w in CONST.values()), _w)
NCONST = sum(w for _, w in CONST.values())
NSHARED = 640


def slopes():
    def pow2(m):
        return [(2.0 ** (-8.0 / m)) ** (i + 1) for i in range(m)]
    return [float(s) for s in np.asarray(pow2(8) + pow2(16)[0::2][:NQ - 8], np.float32)]


def build(nc, x_in, wts, w_g, w_idx, rows_a, rows_b, cmp_w2, const_in, shared_1, shared_2, out):
    ctx = ExitStack()
    with ctx:
        def sb(name, shape, dt=F32):
            return ctx.enter_context(nc.sbuf_tensor(name, shape, dt))

        def sem(name):
            return ctx.enter_context(nc.semaphore(name))

        raw = sb("raw", [P, RAW, TW])
        w_hi = sb("w_hi", [P, RING, TW], F32R)
        w_lo = sb("w_lo", [P, RING, TW], F32R)
        x = sb("resid", [P, 2, D])
        h_hi = sb("h_hi", [P, DC, T], F32R)
        h_lo = sb("h_lo", [P, DC, T], F32R)
        mix_hi = sb("mix_hi", [P, DC, T], F32R)
        mix_lo = sb("mix_lo", [P, DC, T], F32R)
        const = sb("consts", [P, NCONST])
        shared = sb("shared", [P, NSHARED])
        vec = sb("vec", [P, NA_ROWS])
        vec_b = sb("vec_b", [P, NB_ROWS])
        z = sb("z", [P, 14, 2 * T])
        alibi = sb("alibi", [P, 4096])
        soft = sb("soft", [P, 1536])
        turned = sb("turned", [P, 768])
        misc = sb("misc", [P, 2048])
        small = sb("small", [P, 192])
        modT = sb("modT", [P, 48])
        ps = ctx.enter_context(nc.psum_tensor("ps", [P, 8, 512], F32))

        def cst(name):
            a, w = CONST[name]
            return const[:, a:a + w]

        def col(name, i):
            return vec[:, VEC_A[name][0] + i:VEC_A[name][0] + i + 1]

        ident = cst("ident")

        def zt(i):
            return z[:, i, :].rearrange("p (c t) -> p c t", c=2)
        U, V_, Q0, KC, VC, KS, KW, VS, VW = 0, 1, 2, 5, 6, 7, 8, 9, 10
        zflat = z[:, :, :].rearrange("p a b -> p (a b)")
        tail = zflat[:, 11 * 512:14 * 512]
        kr = [tail[:, 528 * i:528 * (i + 1)].rearrange("p (j n) -> p j n", j=8) for i in range(2)]
        hcmp = [tail[:, 1056:1312].rearrange("p (f n) -> p f n", f=2), misc[:, 1536:1792].rearrange("p (f n) -> p f n", f=2)]
        kcmp = tail[:, 1312:1376]
        vblk = misc[:, 0:768].rearrange("p (h d) -> p h d", h=NQ)
        pcT = misc[:, 768:1536].rearrange("p (c t) -> p c t", c=3)
        w2 = misc[:, 1792:2048].rearrange("p (a f d) -> p a f d", a=2, f=2)
        ypad = soft[:, 0:572].rearrange("p (c t) -> p c t", c=2)
        conv = soft[:, 572:1084].rearrange("p (c t) -> p c t", c=2)
        lnv = turned[:, 0:512].rearrange("p (a t) -> p a t", a=2)
        lnd = z[:, U, :].rearrange("p (c t) -> p c t", c=2)
        lnq = z[:, V_, :].rearrange("p (c t) -> p c t", c=2)
        scmp = turned[:, 0:384].rearrange("p (m h n) -> p m h n", m=2, h=NQ)
        pcmp = soft[:, 0:768].rearrange("p (m h n) -> p m h n", m=2, h=NQ)
        gates = small[:, 0:72].rearrange("p (m h b) -> p m h b", m=2, h=NQ)
        st24 = [small[:, 72 + 24 * i:96 + 24 * i].rearrange("p (m h) -> p m h", m=2) for i in range(2)]
        msum, rst, nwt, sqv = (small[:, 120 + 2 * i:122 + 2 * i] for i in range(4))
        nmax = small[:, 128:136].rearrange("p (a b) -> p a b", a=2)
        psum_p = small[:, 136:144].rearrange("p (a b) -> p a b", a=2)
        coef = small[:, 144:152].rearrange("p (a b) -> p a b", a=2)
        pebias = small[:, 152:156]
        part = small[:, 156:160]
        silu_c = small[:, 160:168]
        scl = small[:, 168:176]
        wi_s = small[:, 176:192].rearrange("p (m h) -> p m h", m=2)
        top8 = small[:, 72:80]
        xn = zflat[:, 0:2048].rearrange("p (m d) -> p m d", m=2)
        xn_scratch = zflat[:, 2048:3072]
        htmp = zflat[:, 3072:3072 + 512].rearrange("p (a t) -> p a t", a=2)
        rowb = zflat[:, 12 * 512:14 * 512]
        diag = zflat[:, 10 * 512:12 * 512].rearrange("p (k n) -> p k n", k=8)
        ff_act = [z[:, i, :] for i in range(3)]
        ff_hid = [z[:, 3 + i, :] for i in range(3)]
        hid_hi = [mix_hi[:, 2 * i:2 * i + 2, :] for i in range(3)]
        hid_lo = [mix_lo[:, 2 * i:2 * i + 2, :] for i in range(3)]
        QI, QA, KA, QB, KB, VA, VB = 0, 2, 4, 6, 8, 10, 12

        def wide(v):
            return v.rearrange("p m (h o) -> p m h o", o=1).to_broadcast([P, 2, NQ, CMP_SLOT])

        def xs_cmp(a):
            return turned[:, 384 * a:384 * a + 264]

        def cmp_hidden(a):
            return soft[:, 1100 + 120 * a:1220 + 120 * a].rearrange("p (f g n) -> p f g n", f=2, g=NKV)

        def merged(u):
            return zflat[:, 1024 * u:1024 * (u + 1)].rearrange("p (c t) -> p c t", c=4)
        def zgrp(i, g):
            return z[:, i + g // 2, (g % 2) * T:(g % 2 + 1) * T]
        sgate = alibi[:, :].rearrange("p (a k t) -> p a k t", a=2, k=8)
        kiT = turned[:, 0:256]
        rtmp = soft[:, 0:512]
        rtmp2 = soft[:, 512:768]
        isc = misc[:, 0:384]
        abias = misc[:, 384:768]
        relu_b = [soft[:, 768 + 384 * i:1152 + 384 * i] for i in range(2)]
        sA = [soft[:, 384 * i:384 * (i + 1)] for i in range(2)]
        pTA = turned[:, 0:384]
        zm = [soft[:, 768 + 384 * i:1152 + 384 * i] for i in range(2)]
        eb = turned[:, 384:768]
        spb = misc[:, 768:1152]
        attb = misc[:, 1152:1536]

        s_raw = [sem(f"raw{i}_landed") for i in range(RAW)]
        s_x, s_const, s_rows, s_shared, s_w2, s_out = (sem(n) for n in (
            "x_landed", "const_landed", "rows_landed", "shared_landed", "w2_landed", "out_written"))
        hi_ready = sem("hi_ready")
        w_ready = sem("w_ready")
        pe_tile = sem("pe_tile")
        direct_done = sem("direct_done")
        z_evac = sem("z_evac")
        vec_ps, vec_ready = sem("vec_ps"), sem("vec_ready")
        ms_ready, sq_ready = sem("ms_ready"), sem("sq_ready")
        xn_ready, xT_ready, hhi_ready, h_ready = sem("xn_ready"), sem("xT_ready"), sem("hhi_ready"), sem("h_ready")
        dstep, astep, gstep = sem("dve_step"), sem("act_step"), sem("pool_step")
        zeroed, alibi_ready = sem("zeroed"), sem("alibi_ready")
        conv_ready, conv_mean, convd_ready, conv_var = (sem(n) for n in ("conv_ready", "conv_mean", "convd_ready", "conv_var"))
        lnv_ready, lnsq_ready, lnn_ready, chi_ready, clo_ready = (sem(n) for n in (
            "lnv_ready", "lnsq_ready", "lnn_ready", "conv_hi_ready", "conv_lo_ready"))
        kr_ready, cmp_ps, cmp_sb, cmp_sum, cmp_h, cmp2_ps, cmp2_sb, vblk_ready = (sem(n) for n in (
            "kr_ready", "cmp_ps", "cmp_sb", "cmp_sum", "cmp_h", "cmp2_ps", "cmp_keys_ready", "cmp_values_ready"))
        sc_ps, sc_sb, pc_exp, pc_ready, pcT_ps, pcT_ready = (sem(n) for n in (
            "cmp_scores_ps", "cmp_scores_sb", "cmp_probs_exp", "cmp_probs_ready", "cmp_probsT_ps", "cmp_probsT_ready"))
        s_ps, s_sb, p_exp, p_ready, pT_ps, pT_ready, o_ps, o_hi, o_lo = (sem(n) for n in (
            "scores_ps", "scores_sb", "probs_exp", "probs_ready", "probsT_ps", "probsT_ready", "o_ps", "o_hi", "o_lo"))
        mod_ps, mod_ready, silu_c_ready = sem("mod_ps"), sem("mod_ready"), sem("silu_c_ready")
        acc_ps, x_new = sem("acc_ps"), sem("x_new")
        silu_done, hid_done, hidhi_done, hidlo_done = (sem(n) for n in ("silu_done", "hid_done", "hid_hi_done", "hid_lo_done"))
        relu2_done, hid2_done, hid2hi_done, hid2lo_done = (sem(n) for n in ("relu2_done", "hid2_done", "hid2_hi_done", "hid2_lo_done"))
        diag_ready, row_ps, row_ready = sem("diag_ready"), sem("row_ps"), sem("row_ready")
        rot_ps, rot_done, ix_ps, relu_done, ix_acc = (sem(n) for n in ("rot_ps", "rot_done", "ix_ps", "relu_done", "ix_acc"))
        bias_ready = sem("bias_ready")
        b_z, b_zm, b_abs, b_ln, b_sp, b_c, b_cm, b_att = (sem(n) for n in (
            "b_scores_ps", "b_masked", "b_abs", "b_ln", "b_softplus", "b_sum_ps", "b_sum_masked", "b_att"))
        up_ps, up_a, m_sum, m_hi, m_lo = (sem(n) for n in ("up_ps", "up_used", "merged", "merged_hi", "merged_lo"))
        sqy, y_res = sem("y_squares"), sem("y_residual")

        n_of = {name: n for n, (_, name) in enumerate(TILES)}
        s_idx, d_idx = {}, {}
        for kind, name in TILES:
            (s_idx if kind == "s" else d_idx)[name] = len(s_idx) if kind == "s" else len(d_idx)
        s_name = {v: k for k, v in s_idx.items()}
        NSPLIT = len(s_idx)
        FF1_LOOP, FF2_LOOP, LOOPED, TURNS = s_idx["gate2"], s_idx["fa2"], 24, 4
        ff1_tiles, ff2_tiles = range(FF1_LOOP, FF1_LOOP + LOOPED), range(FF2_LOOP, FF2_LOOP + LOOPED)

        def tile_width(name):
            return {"g": DC * G_COLS, "idx": DC * IDX_COLS}.get(name, TW)

        def raw_of(name):
            return raw[:, n_of[name] % RAW, 0:tile_width(name)]

        def landed(eng, name):
            n = n_of[name]
            eng.wait_ge(s_raw[n % RAW], 16 * (n // RAW + 1))

        def hi_of(name):
            return w_hi[:, s_idx[name] % RING, 0:tile_width(name)]

        def lo_of(name):
            return w_lo[:, s_idx[name] % RING, 0:tile_width(name)]

        block = ctx.enter_context(nc.Block())

        @block.sync
        def _(sp):
            for m in range(2):
                sp.dma_start(x[:, m, :], x_in[m * P:(m + 1) * P, :]).then_inc(s_x, 16)
            sp.dma_start(const[:, :], const_in).then_inc(s_const, 16)
            sp.dma_start(raw[0:NA_ROWS, 5, 0:P], rows_a).then_inc(s_rows, 16)
            sp.dma_start(raw[0:NB_ROWS, 5, P:2 * P], rows_b).then_inc(s_rows, 16)

            def load(name):
                n = n_of[name]
                if n >= RAW:
                    kind, old = TILES[n - RAW]
                    if kind == "s":
                        sp.wait_ge(w_ready, s_idx[old] + 1)
                    else:
                        sp.wait_ge(direct_done, d_idx[old] + 1)
                if n == RAW - 1:
                    sp.wait_ge(vec_ps, 1)
                src = {"g": w_g, "idx": w_idx}.get(name)
                if src is None:
                    src = wts[n - (n > n_of["g"]) - (n > n_of["idx"]), :, :]
                sp.dma_start(raw_of(name), src).then_inc(s_raw[n % RAW], 16)

            def load_loop(first):
                n0, s0 = n_of[s_name[first]], first
                w0 = n0 - (n0 > n_of["g"]) - (n0 > n_of["idx"])
                with sp.Fori(0, TURNS) as i:
                    for j in range(RAW):
                        sp.wait_ge(w_ready, i * RAW + (s0 + j - RAW + 1))
                        src = wts[bass.ds(i * RAW + (w0 + j), 1), :, :].rearrange("a p w -> (a p) w")
                        sp.dma_start(raw[:, (n0 + j) % RAW, :], src).then_inc(s_raw[(n0 + j) % RAW], 16)

            for kind, name in TILES:
                if kind == "s" and s_idx[name] in ff1_tiles:
                    if s_idx[name] == FF1_LOOP:
                        load_loop(FF1_LOOP)
                elif kind == "s" and s_idx[name] in ff2_tiles:
                    if s_idx[name] == FF2_LOOP:
                        load_loop(FF2_LOOP)
                else:
                    load(name)
                if name == "u":
                    sp.dma_start(shared[:, :], shared_1).then_inc(s_shared, 16)
                    sp.dma_start(w2.rearrange("p a f d -> p (a f d)"), cmp_w2).then_inc(s_w2, 16)
                if name == "down0":
                    sp.wait_ge(x_new, 4)
                    sp.dma_start(shared[:, :], shared_2).then_inc(s_shared, 16)
            sp.wait_ge(y_res, 8)
            for m in range(2):
                sp.dma_start(out[m * P:(m + 1) * P, :], x[:, m, :]).then_inc(s_out, 16)
            sp.wait_ge(s_out, 32)

        @block.gpsimd
        def _(pool):
            nc.gpsimd.memset(ypad[:, :, 0:CONV_W - 1], 0.0).then_inc(zeroed, 1)
            nc.gpsimd.memset(vblk, 0.0).then_inc(zeroed, 1)
            for i in range(2):
                nc.gpsimd.memset(hcmp[i], 0.0).then_inc(zeroed, 1)
            pool.wait_ge(s_shared, 16)
            for h, s in enumerate(slopes()):
                nc.gpsimd.tensor_scalar(alibi[:, T * h:T * (h + 1)], shared[:, 0:T], s, None, ALU.mult).then_inc(alibi_ready, 1)
            pool.wait_ge(vec_ready, 2)
            pool.wait_ge(zeroed, 4)
            pool.wait_ge(alibi_ready, NQ)
            copies = 0
            for i, src in enumerate((KC, VC)):
                pool.wait_ge(z_evac, src + 1)
                for g in range(NKV):
                    view = zt(src)[(g % 2) * HD:(g % 2 + 1) * HD, g // 2, :].rearrange("p (c j l) -> p l j c", c=16, j=8)
                    for l in range(2):
                        if copies:
                            pool.wait_ge(kr_ready, copies)
                        copies += 1
                        nc.gpsimd.tensor_copy(kr[i][l * HD:(l + 1) * HD, :, g * 16:(g + 1) * 16], view[:, l]).then_inc(kr_ready, 1)
                for half in range(2):
                    a = 2 * CONV_W + 16 * i + 8 * half
                    pool.wait_ge(kr_ready, copies)
                    copies += 1
                    nc.gpsimd.tensor_copy(kr[i][:, :, 64 + half:65 + half],
                                          vec_b[:, a:a + 8].rearrange("p (j o) -> p j o", o=1)).then_inc(kr_ready, 1)

        @block.tensor
        def _(pe):
            def mm3(o, lh, ll, rh, rl, start, stop):
                nc.tensor.matmul(o, lh, rh, start=start, stop=False)
                nc.tensor.matmul(o, lh, rl, start=False, stop=False)
                return nc.tensor.matmul(o, ll, rh, start=False, stop=stop)

            def w3(slot, k, n=TW):
                return (w_hi[:, slot, 0:n].rearrange("p (k c) -> p k c", k=k), w_lo[:, slot, 0:n].rearrange("p (k c) -> p k c", k=k))

            def feature_tile(slot, bank, hi, lo):
                wh, wl = w3(slot, DC)
                for c in range(2):
                    cs = slice(c * P, (c + 1) * P)
                    for k in range(DC):
                        i = mm3(ps[:, bank, c * T:(c + 1) * T], wh[:, k, cs], wl[:, k, cs], hi[:, k, :], lo[:, k, :],
                                k == 0, k == DC - 1)
                return i

            def token_tile(slot, bank, hi, lo, a, n, cols):
                wh, wl = w3(slot, DC, DC * cols)
                for m in range(2):
                    ms = slice(m * P, (m + 1) * P)
                    for k in range(DC):
                        i = mm3(ps[:, bank, m * T:m * T + n], hi[:, k, ms], lo[:, k, ms], wh[:, k, a:a + n], wl[:, k, a:a + n],
                                k == 0, k == DC - 1)
                return i

            def acc_tile(slot, hi, lo, k0, first, last):
                wh, wl = w3(slot, 2)
                for kk in range(2):
                    for m in range(2):
                        ms = slice(m * P, (m + 1) * P)
                        for n in range(2):
                            ns = slice(n * 512, (n + 1) * 512)
                            i = mm3(ps[:, 2 * m + n, :], hi[:, k0 + kk, ms], lo[:, k0 + kk, ms], wh[:, kk, ns], wl[:, kk, ns],
                                    first and kk == 0, last and kk == 1)
                return i

            def norm_turn(t):
                pe.wait_ge(xn_ready, 2 * (t + 1))
                for k in range(DC):
                    for m in range(2):
                        o = ps[:, 4 + k // 2, (k % 2) * T + m * P:(k % 2) * T + (m + 1) * P]
                        i = nc.tensor.transpose(o, xn[:, m, k * P:(k + 1) * P], ident)
                    if k % 2:
                        i.then_inc(xT_ready, 1)

            def spread(t):
                pe.wait_ge(diag_ready, t + 1)
                for n in range(2):
                    i = nc.tensor.matmul(ps[:, 4 + n, :], cst("ones"), diag[:, 4 * n:4 * n + 4, :].rearrange("p k n -> p (k n)"),
                                         start=True, stop=True)
                i.then_inc(row_ps, 1)

            pe.wait_ge(s_const, 16)
            pe.wait_ge(s_rows, 32)
            nc.tensor.transpose(ps[:, 0, 0:NA_ROWS], raw[0:NA_ROWS, 5, 0:P], ident[0:NA_ROWS, 0:NA_ROWS])
            nc.tensor.transpose(ps[:, 0, P:P + NB_ROWS], raw[0:NB_ROWS, 5, P:2 * P], ident[0:NB_ROWS, 0:NB_ROWS]).then_inc(vec_ps, 1)
            norm_turn(0)

            pe.wait_ge(h_ready, DC)
            pe.wait_ge(vec_ready, 2)

            def project_1(s):
                pe.wait_ge(w_ready, s + 1)
                if s >= 3:
                    pe.wait_ge(z_evac, s - 2)
                return s % RING, s % 3
            for s in range(3):
                feature_tile(*project_1(s), h_hi, h_lo).then_inc(pe_tile, 1)
            with pe.Fori(0, 2) as i:
                for j in range(3):
                    pe.wait_ge(w_ready, i * 3 + (3 + j + 1))
                    pe.wait_ge(z_evac, i * 3 + (3 + j - 2))
                    feature_tile(j, j, h_hi, h_lo).then_inc(pe_tile, 1)
            pe.wait_ge(conv_ready, 1)
            for c in range(2):
                i = nc.tensor.matmul(ps[:, 3, 0:T], cst("mean"), conv[:, c, :], start=(c == 0), stop=(c == 1))
            i.then_inc(conv_mean, 1)
            for s in (9, 10):
                slot, bank = project_1(s)
                token_tile(slot, bank, h_hi, h_lo, 0, T, T).then_inc(pe_tile, 1)
            slot, bank = project_1(11)
            token_tile(slot, bank, h_hi, h_lo, 0, G_COLS, G_COLS).then_inc(pe_tile, 1)
            pe.wait_ge(convd_ready, 1)
            for c in range(2):
                i = nc.tensor.matmul(ps[:, 3, T:2 * T], cst("mean"), lnq[:, c, :], start=(c == 0), stop=(c == 1))
            i.then_inc(conv_var, 1)

            for a in range(2):
                pe.wait_ge(kr_ready, 10 * (a + 1))
                for half in range(2):
                    name = f"cmp{2 * a + half}"
                    landed(pe, name)
                    wc = raw_of(name).rearrange("p (j h) -> p j h", j=8)
                    for f in range(2):
                        for j in range(8):
                            i = nc.tensor.matmul(ps[:, 4 + a, (2 * half + f) * 66:(2 * half + f + 1) * 66], wc[:, j, f * P:(f + 1) * P],
                                                 kr[a][:, j, :], start=(j == 0), stop=(j == 7))
                    i.then_inc(direct_done, 1)
            pe.wait_ge(s_w2, 16)
            pe.wait_ge(cmp_h, 2)
            for f in range(2):
                i = nc.tensor.matmul(ps[0:HD, 6, 0:P], w2[:, 0, f, :], hcmp[0][:, f, :], start=(f == 0), stop=(f == 1))
            i.then_inc(cmp2_ps, 1)
            pe.wait_ge(cmp_h, 4)
            for f in range(2):
                i = nc.tensor.matmul(ps[:, 7, 0:HD], hcmp[1][:, f, :], w2[:, 1, f, :], start=(f == 0), stop=(f == 1))
            i.then_inc(cmp2_ps, 1)

            def head_at(h):
                pair, in_pair = h // 6, h % 6
                return 3 * pair + in_pair % 3, HD * (in_pair // 3), pair

            def qT(h):
                j, b, _ = head_at(h)
                return z[b:b + HD, Q0 + j // 2, (j % 2) * T:(j % 2 + 1) * T]

            pe.wait_ge(z_evac, 12)
            pe.wait_ge(cmp2_sb, 2)
            for m in range(2):
                for h in range(NQ):
                    _, b, _ = head_at(h)
                    g = h // 3
                    at = ((2 * m + h // 6) * 3 + h % 3) * CMP_SLOT
                    i = nc.tensor.matmul(ps[:, 4 + b // HD, at:at + CMP_SLOT], qT(h)[:, m * P:(m + 1) * P],
                                         kcmp[b:b + HD, g * CMP_SLOT:(g + 1) * CMP_SLOT], start=True, stop=True)
            i.then_inc(sc_ps, 1)

            order = [6 * p + r + 3 * e for p in range(2) for r in range(3) for e in range(2)]

            def scores(n):
                h = order[n]
                _, b, pair = head_at(h)
                for br, k_tile in enumerate((KS, KW)):
                    bank = 2 * (n % 2) + br
                    kT = z[b:b + HD, k_tile, pair * T:(pair + 1) * T]
                    nc.tensor.matmul(ps[:, bank, 0:P], qT(h)[:, 0:P], kT[:, 0:P], start=True, stop=True)
                    i = nc.tensor.matmul(ps[:, bank, P:P + T], qT(h)[:, P:T], kT, start=True, stop=True)
                i.then_inc(s_ps, 1)

            scores(0)
            pe.wait_ge(pc_ready, 1)
            for c in range(3):
                for m in range(2):
                    i = nc.tensor.transpose(ps[:, 4 + c // 2, (c % 2) * T + m * P:(c % 2) * T + (m + 1) * P],
                                            pcmp[:, m, 4 * c:4 * c + 4, :].rearrange("p h n -> p (h n)"), ident)
            i.then_inc(pcT_ps, 1)

            def ada(t):
                name = f"ada{t}"
                landed(pe, name)
                wa = raw_of(name).rearrange("p (k c) -> p k c", k=DC)
                for c in range(2):
                    for k in range(DC):
                        i = nc.tensor.matmul(ps[:, 7, 2 * T - 48 + 2 * t + c:2 * T - 47 + 2 * t + c], wa[:, k, c * P:(c + 1) * P],
                                             silu_c[:, k:k + 1], start=(k == 0), stop=(k == DC - 1))
                i.then_inc(direct_done, 1)

            pe.wait_ge(silu_c_ready, 1)
            pe.wait_ge(vblk_ready, NQ)
            pe.wait_ge(pcT_ready, 3)
            for n in range(NQ):
                h = order[n]
                j, b, _ = head_at(h)
                g = h // 3
                if n + 1 < NQ:
                    if n >= 1:
                        pe.wait_ge(s_sb, 4 * n)
                    scores(n + 1)
                pe.wait_ge(p_ready, 4 * (n + 1))
                if n >= 1:
                    pe.wait_ge(pT_ready, 2 * n)
                for br in range(2):
                    for c in range(3):
                        i = nc.tensor.transpose(ps[:, 4 + br, c * P:(c + 1) * P],
                                                soft[:, (2 * (n % 2) + br) * 384 + c * P:(2 * (n % 2) + br) * 384 + (c + 1) * P], ident)
                i.then_inc(pT_ps, 1)
                ada(2 * n)
                ada(2 * n + 1)
                if n % 2 == 0 and n >= 2:
                    pe.wait_ge(o_lo, n // 2)
                nc.tensor.matmul(ps[b:b + HD, 6, 0:T], vblk[:, h, :], pcT[:, h // 4, :], start=True, stop=False)
                pe.wait_ge(pT_ready, 2 * (n + 1))
                for br, v_tile in enumerate((VS, VW)):
                    for kt in range(2):
                        lhs = z[:, v_tile, kt * T + g * HD:kt * T + (g + 1) * HD]
                        pt = turned[:, br * 384:br * 384 + T] if kt == 0 else turned[:, br * 384 + T:(br + 1) * 384]
                        i = nc.tensor.matmul(ps[b:b + HD, 6, kt * P:T], lhs, pt, start=False, stop=(br == 1 and kt == 1))
                i.then_inc(o_ps, 1)

            pe.wait_ge(clo_ready, 2)
            for i4 in range(4):
                s = s_idx[f"out{i4}"]
                pe.wait_ge(w_ready, s + 1)
                if i4 == 0:
                    pe.wait_ge(s_sb, 4 * NQ)
                if i4 >= 1:
                    pe.wait_ge(o_lo, 2 * i4)
                i = acc_tile(s % RING, mix_hi, mix_lo, 2 * i4, i4 == 0, i4 == 3)
                i.then_inc(pe_tile, 1)
            norm_turn(1)

            pe.wait_ge(h_ready, 2 * DC)

            def down(slot, buf, first, last):
                return acc_tile(slot, hid_hi[buf], hid_lo[buf], 0, first, last)

            def ff1_step(st, i=0, first=False):
                s0 = s_idx[f"gate{st}"]
                for c in range(2):
                    pe.wait_ge(w_ready, i * 6 + (s0 + c + 1))
                    if c == 0 and st >= 2:
                        pe.wait_ge(hid_done, i * 2 + (st - 1))
                    feature_tile((s0 + c) % RING, 4 + 2 * (st % 2) + c, h_hi, h_lo).then_inc(pe_tile, 1)
                if st >= 1:
                    pe.wait_ge(w_ready, i * 6 + (s0 + 3))
                    pe.wait_ge(hidlo_done, i * 2 + st)
                    down((s0 + 2) % RING, (st - 1) % 2, first, False).then_inc(pe_tile, 1)

            ff1_step(0)
            pe.wait_ge(x_new, 4)
            ff1_step(1, first=True)
            with pe.Fori(0, TURNS) as i:
                ff1_step(2, i)
                ff1_step(3, i)
            ff1_step(10)
            s = s_idx["down10"]
            pe.wait_ge(w_ready, s + 1)
            pe.wait_ge(hidlo_done, FF1_STEPS)
            down(s % RING, 0, False, True).then_inc(pe_tile, 1)
            spread(0)
            norm_turn(2)

            pe.wait_ge(h_ready, 3 * DC)

            def evac_no(s):
                return 12 + s - s_idx["idx"]

            def project_2(name):
                s = s_idx[name]
                pe.wait_ge(w_ready, s + 1)
                pe.wait_ge(z_evac, evac_no(s) - 2)
                return s % RING, s % 3

            slot, bank = project_2("idx")
            wh, wl = w3(slot, DC, DC * IDX_COLS)
            for k in range(DC):
                mm3(ps[:, bank, 0:T], wh[:, k, 0:P], wl[:, k, 0:P], h_hi[:, k, :], h_lo[:, k, :], k == 0, k == DC - 1)
            for m in range(2):
                ms = slice(m * P, (m + 1) * P)
                for k in range(DC):
                    i = mm3(ps[:, bank, T + m * 8:T + (m + 1) * 8], h_hi[:, k, ms], h_lo[:, k, ms], wh[:, k, P:P + 8], wl[:, k, P:P + 8],
                            k == 0, k == DC - 1)
            i.then_inc(pe_tile, 1)

            def feature_2(name):
                feature_tile(*project_2(name), h_hi, h_lo).then_inc(pe_tile, 1)

            rots = [0]

            def swap(src, n, name):
                pe.wait_ge(z_evac, evac_no(s_idx[name]) + 1)
                if rots[0]:
                    pe.wait_ge(rot_done, rots[0])
                nc.tensor.matmul(ps[:, 3, 0:n], shared[:, 512:640], src, start=True, stop=True).then_inc(rot_ps, 1)
                rots[0] += 1

            def index_scores(h):
                b, j = HD * (h % 2), h // 2
                if h == 0:
                    pe.wait_ge(rot_done, 3)
                if h >= 4:
                    pe.wait_ge(relu_done, h - 3)
                q = z[b:b + HD, QI + j // 2, (j % 2) * T:(j % 2 + 1) * T]
                nc.tensor.matmul(ps[:, 4 + h % 4, 0:P], q[:, 0:P], kiT[b:b + HD, 0:P], start=True, stop=True)
                nc.tensor.matmul(ps[:, 4 + h % 4, P:P + T], q[:, P:T], kiT[b:b + HD, :], start=True, stop=True).then_inc(ix_ps, 1)

            pe.wait_ge(s_shared, 32)
            feature_2("qi0")
            feature_2("qi1")
            swap(kiT, T, "idx")
            feature_2("qa0")
            swap(z[:, QI, :], 512, "qi0")
            swap(z[:, QI + 1, :], 512, "qi1")
            feature_2("qa1")
            for h in range(4):
                index_scores(h)
            swap(z[:, QA, :], 512, "qa0")
            feature_2("ka0")
            for h in range(4, 8):
                index_scores(h)
            swap(z[:, QA + 1, :], 512, "qa1")
            feature_2("ka1")
            swap(z[:, KA, :], 512, "ka0")
            feature_2("qb0")
            swap(z[:, KA + 1, :], 512, "ka1")
            for name in ("qb1", "kb0", "kb1"):
                feature_2(name)
            for name in ("va0", "va1", "vb0", "vb1"):
                token_tile(*project_2(name), h_hi, h_lo, 0, T, T).then_inc(pe_tile, 1)
            for i8 in range(8):
                feature_2(f"sg{i8}")

            def zhead(base, h):
                b, j = HD * (h % 2), h // 2
                return z[b:b + HD, base + j // 2, (j % 2) * T:(j % 2 + 1) * T]

            def scores_a(h):
                if h == 0:
                    pe.wait_ge(z_evac, 12 + s_idx["sg7"] - s_idx["idx"] + 1)
                if h >= 2:
                    pe.wait_ge(s_sb, 4 * NQ + 2 * (h - 1))
                q, k = zhead(QA, h), zhead(KA, h)
                nc.tensor.matmul(ps[:, h % 2, 0:P], q[:, 0:P], k[:, 0:P], start=True, stop=True)
                nc.tensor.matmul(ps[:, h % 2, P:P + T], q[:, P:T], k, start=True, stop=True).then_inc(s_ps, 1)

            def scores_b(h):
                if h >= 2:
                    pe.wait_ge(b_zm, h - 1)
                q, k = zhead(QB, h), zhead(KB, h)
                nc.tensor.matmul(ps[:, 3 + h % 2, 0:T], k[:, 0:P], q, start=True, stop=True)
                nc.tensor.matmul(ps[:, 3 + h % 2, T:T + P], k[:, P:T], q[:, P:T], start=True, stop=True).then_inc(b_z, 1)

            pe.wait_ge(rot_done, 7)
            scores_a(0)
            scores_b(0)
            for h in range(NB_HEADS):
                b, j = HD * (h % 2), h // 2
                if h + 1 < NB_HEADS:
                    scores_a(h + 1)
                    scores_b(h + 1)
                pe.wait_ge(p_ready, 4 * NQ + 2 * (h + 1))
                if h >= 1:
                    pe.wait_ge(pT_ready, 2 * NQ + h)
                for c in range(3):
                    i = nc.tensor.transpose(ps[:, 2, c * P:(c + 1) * P], sA[h % 2][:, c * P:(c + 1) * P], ident)
                i.then_inc(pT_ps, 1)
                pe.wait_ge(b_sp, h + 1)
                if h >= 1:
                    pe.wait_ge(b_cm, 2 * h)
                q, k = zhead(QB, h), zhead(KB, h)
                nc.tensor.matmul(ps[:, 5, 0:T], k[:, 0:P], q, start=True, stop=False)
                nc.tensor.matmul(ps[:, 5, 0:T], cst("tri"), spb[:, 0:T], start=False, stop=False)
                nc.tensor.matmul(ps[:, 5, P:T], cst("negones"), spb[:, T:T + P], start=False, stop=True)
                nc.tensor.matmul(ps[:, 5, T:T + P], k[:, P:T], q[:, P:T], start=True, stop=False)
                nc.tensor.matmul(ps[:, 5, T:T + P], cst("tri"), spb[:, T:T + P], start=False, stop=True).then_inc(b_c, 1)
                if h % 2 == 0 and h >= 2:
                    pe.wait_ge(o_lo, 6 + h)
                va = z[:, VA + h // 4, :].rearrange("p (m d) -> p m d", m=2)[:, :, (h % 4) * HD:(h % 4 + 1) * HD]
                vb = z[:, VB + h // 4, :].rearrange("p (m d) -> p m d", m=2)[:, :, (h % 4) * HD:(h % 4 + 1) * HD]
                pe.wait_ge(pT_ready, 2 * NQ + h + 1)
                nc.tensor.matmul(ps[b:b + HD, 6, 0:T], va[:, 0, :], pTA[:, 0:T], start=True, stop=False)
                nc.tensor.matmul(ps[b:b + HD, 6, P:T], va[:, 1, :], pTA[:, T:T + P], start=False, stop=True).then_inc(o_ps, 1)
                pe.wait_ge(b_att, h + 1)
                nc.tensor.matmul(ps[b:b + HD, 7, 0:T], vb[:, 0, :], attb[:, 0:T], start=True, stop=False)
                nc.tensor.matmul(ps[b:b + HD, 7, P:T], vb[:, 1, :], attb[:, T:T + P], start=False, stop=True).then_inc(o_ps, 1)

            for u, name in enumerate(("upa0", "upb0", "upa1", "upb1")):
                s = s_idx[name]
                pe.wait_ge(w_ready, s + 1)
                pe.wait_ge(o_lo, 14)
                wh, wl = w3(s % RING, 4)
                for c in range(4):
                    for k in range(4):
                        kk = 4 * (u % 2) + k
                        cs = slice(c * P, (c + 1) * P)
                        i = mm3(ps[:, 2 * u + c // 2, (c % 2) * T:(c % 2 + 1) * T], wh[:, k, cs], wl[:, k, cs], mix_hi[:, kk, :], mix_lo[:, kk, :],
                                k == 0, k == 3)
                i.then_inc(pe_tile, 1)
            for i4 in range(4):
                s = s_idx[f"o2{i4}"]
                pe.wait_ge(w_ready, s + 1)
                pe.wait_ge(m_lo, i4 // 2 + 1)
                acc_tile(s % RING, h_hi, h_lo, 2 * i4, i4 == 0, i4 == 3).then_inc(pe_tile, 1)
            pe.wait_ge(m_sum, 2)
            spread(1)
            pe.wait_ge(row_ready, 2)
            norm_turn(3)

            pe.wait_ge(h_ready, 4 * DC)

            def ff2_step(st, i=0, first=False):
                s0 = s_idx[f"fa{st}"]
                pe.wait_ge(w_ready, i * 6 + (s0 + 1))
                if st >= 3:
                    pe.wait_ge(relu2_done, i * 3 + (st - 2))
                feature_tile(s0 % RING, 4 + st % 3, h_hi, h_lo).then_inc(pe_tile, 1)
                if st >= 1:
                    pe.wait_ge(w_ready, i * 6 + (s0 + 2))
                    pe.wait_ge(hid2lo_done, i * 3 + st)
                    down((s0 + 1) % RING, (st - 1) % 3, first, False).then_inc(pe_tile, 1)

            ff2_step(0)
            ff2_step(1, first=True)
            ff2_step(2)
            ff2_step(3)
            ff2_step(4)
            with pe.Fori(1, TURNS) as i:
                ff2_step(2, i)
                ff2_step(3, i)
                ff2_step(4, i)
            ff2_step(14)
            ff2_step(15)
            s = s_idx["fb15"]
            pe.wait_ge(w_ready, s + 1)
            pe.wait_ge(hid2lo_done, FF2_STEPS)
            down(s % RING, 15 % 3, False, True).then_inc(pe_tile, 1)
            spread(2)

        @block.scalar
        def _(act):
            def split(s, name, i=0):
                n = n_of[name]
                act.wait_ge(s_raw[n % RAW], i * 16 + 16 * (n // RAW + 1))
                if s >= RING:
                    act.wait_ge(pe_tile, i * 6 + (s - RING + 1))
                w = tile_width(name)
                nc.scalar.copy(w_hi[:, s % RING, 0:w], raw[:, n % RAW, 0:w]).then_inc(hi_ready, 1)

            def after(s, i=0):
                if s + RING < NSPLIT:
                    split(s + RING, s_name[s + RING], i)

            steps = [0]

            def link(ins):
                steps[0] += 1
                ins.then_inc(astep, 1)
                act.wait_ge(astep, steps[0])

            def root(t):
                act.wait_ge(ms_ready, t + 1)
                nc.scalar.activation(sqv, msum, ACT.Sqrt).then_inc(sq_ready, 1)

            def norm_hi(t, scale, bias=None):
                for k in range(DC):
                    act.wait_ge(xT_ready, 4 * t + k // 2 + 1)
                    src = ps[:, 4 + k // 2, (k % 2) * T:(k % 2 + 1) * T]
                    nc.scalar.activation(h_hi[:, k, :], src, ACT.Identity, scale=scale(k),
                                         bias=bias(k) if bias else 0.0).then_inc(hhi_ready, 1)

            for s in range(RING):
                split(s, s_name[s])
            root(0)
            act.wait_ge(vec_ready, 1)
            norm_hi(0, lambda k: col("attn_norm", k))

            for s in range(12):
                act.wait_ge(pe_tile, s + 1)
                bank, name = s % 3, s_name[s]
                if name == "g":
                    nc.scalar.activation(gates, ps[:, bank, :].rearrange("p (m c) -> p m c", m=2)[:, :, 0:G_COLS].rearrange(
                        "p m (h b) -> p m h b", b=3), ACT.Sigmoid).then_inc(z_evac, 1)
                elif name == "v":
                    nc.scalar.activation(z[:, s, :], ps[:, bank, :], ACT.Sigmoid).then_inc(z_evac, 1)
                elif name[0] == "q":
                    nc.scalar.mul(z[:, s, :], ps[:, bank, :], HD ** -0.5).then_inc(z_evac, 1)
                else:
                    nc.scalar.copy(z[:, s, :], ps[:, bank, :]).then_inc(z_evac, 1)
                after(s)
            act.wait_ge(lnv_ready, 1)
            nc.scalar.activation(lnv[:, 1, :], lnv[:, 0, :], ACT.Sqrt).then_inc(lnsq_ready, 1)
            act.wait_ge(lnn_ready, 1)
            for c in range(2):
                link(nc.scalar.activation(conv[:, c, :], lnd[:, c, :], ACT.Silu, scale=col("ln_g", c), bias=col("ln_b", c)))
                nc.scalar.copy(mix_hi[:, c, :], conv[:, c, :]).then_inc(chi_ready, 1)
            for a in range(2):
                act.wait_ge(direct_done, 2 * (a + 1))
                nc.scalar.copy(xs_cmp(a), ps[:, 4 + a, 0:264]).then_inc(cmp_sb, 1)
            for a in range(2):
                act.wait_ge(cmp_sum, a + 1)
                for f in range(2):
                    dst = hcmp[a][:, f, :].rearrange("p (g n) -> p g n", g=NKV)[:, :, 0:N_CMP]
                    nc.scalar.activation(dst, cmp_hidden(a)[:, f], ACT.Silu, bias=pebias[:, 2 * a + f:2 * a + f + 1]).then_inc(cmp_h, 1)
            nc.scalar.activation(silu_c, vec[:, VEC_A["c"][0]:VEC_A["c"][0] + 8], ACT.Silu).then_inc(silu_c_ready, 1)
            act.wait_ge(cmp2_ps, 1)
            for b in range(2):
                nc.scalar.copy(kcmp[b * HD:(b + 1) * HD, :].rearrange("p (g n) -> p g n", g=NKV),
                               ps[0:HD, 6, 0:P].rearrange("p (g n) -> p g n", g=NKV)[:, :, 0:CMP_SLOT]).then_inc(cmp2_sb, 1)
            act.wait_ge(sc_sb, 1)
            nc.scalar.activation(scmp, scmp, ACT.Exp).then_inc(pc_exp, 1)
            for n in range(NQ):
                act.wait_ge(s_sb, 4 * (n + 1))
                for br in range(2):
                    for m in range(2):
                        o = soft[:, (2 * (n % 2) + br) * 384 + m * P:(2 * (n % 2) + br) * 384 + P + m * T]
                        c = 2 * br + m
                        nc.scalar.activation(o, o, ACT.Exp, scale=-1.0, bias=nmax[:, n % 2, c:c + 1],
                                             accum_out=psum_p[:, n % 2, c:c + 1]).then_inc(p_exp, 1)
                if n % 2:
                    j = n // 2
                    act.wait_ge(o_ps, n + 1)
                    nc.scalar.copy(mix_hi[:, 2 + j, :], ps[:, 6, 0:T]).then_inc(o_hi, 1)
            for i4 in range(4):
                after(s_idx[f"out{i4}"])
            root(1)
            norm_hi(1, lambda k: col("ffn_norm", k))

            def ff1_step(st, i=0):
                s0 = s_idx[f"gate{st}"]
                act.wait_ge(pe_tile, i * 6 + (s0 + 1))
                if st >= 2:
                    act.wait_ge(hid_done, i * 2 + (st - 1))
                nc.scalar.activation(ff_act[st % 2], ps[:, 4 + 2 * (st % 2), :], ACT.Silu).then_inc(silu_done, 1)
                after(s0, i)
                after(s0 + 1, i)
                act.wait_ge(hid_done, i * 2 + (st + 1))
                if st >= 2:
                    act.wait_ge(pe_tile, i * 6 + (s0 - 1 + 1))
                nc.scalar.copy(hid_hi[st % 2], ff_hid[st % 2].rearrange("p (c t) -> p c t", c=2)).then_inc(hidhi_done, 1)
                if st >= 1:
                    after(s0 + 2, i)

            ff1_step(0)
            ff1_step(1)
            with act.Fori(0, TURNS) as i:
                ff1_step(2, i)
                ff1_step(3, i)
            ff1_step(10)
            after(s_idx["down10"])
            root(2)
            root(3)
            norm_hi(2, lambda k: scl[:, k:k + 1], lambda k: modT[:, k:k + 1])

            relus = [0]

            def relu_index(h):
                act.wait_ge(ix_ps, h + 1)
                if h >= 2:
                    act.wait_ge(ix_acc, 2 * (h - 1))
                nc.scalar.activation(relu_b[h % 2], ps[:, 4 + h % 4, 0:384], ACT.Relu).then_inc(relu_done, 1)

            for s in range(s_idx["idx"], s_idx["sg7"] + 1):
                name = s_name[s]
                act.wait_ge(pe_tile, s + 1)
                bank = s % 3
                if name == "idx":
                    link(nc.scalar.copy(kiT, ps[:, bank, 0:T]))
                    nc.scalar.copy(wi_s, ps[:, bank, T:T + 16].rearrange("p (m h) -> p m h", m=2)).then_inc(z_evac, 1)
                elif name[:2] == "sg":
                    i8 = int(name[2])
                    dst = sgate[:, i8 // 4, 2 * (i8 % 4):2 * (i8 % 4) + 2, :].rearrange("p c t -> p (c t)")
                    nc.scalar.activation(dst, ps[:, bank, :], ACT.Sigmoid).then_inc(z_evac, 1)
                else:
                    at = {"qi": QI, "qa": QA, "ka": KA, "qb": QB, "kb": KB, "va": VA, "vb": VB}[name[:2]] + int(name[2])
                    scale = HD ** -0.5 if name[:2] in ("qa", "qb") else 1.0
                    nc.scalar.mul(z[:, at, :], ps[:, bank, :], scale).then_inc(z_evac, 1)
                after(s)
                if name in ("qa1", "ka0"):
                    for h in range(4):
                        relu_index(h + 4 * (name == "ka0"))

            def attn_a(h):
                act.wait_ge(s_sb, 4 * NQ + 2 * (h + 1))
                for m in range(2):
                    o = sA[h % 2][:, m * P:P + m * T]
                    nc.scalar.activation(o, o, ACT.Exp, scale=-1.0, bias=nmax[:, h % 2, m:m + 1], accum_out=psum_p[:, h % 2, m:m + 1]).then_inc(p_exp, 1)

            def attn_b1(h):
                act.wait_ge(b_abs, h + 1)
                link(nc.scalar.activation(eb, eb, ACT.Exp))
                nc.scalar.activation(eb, eb, ACT.Ln, bias=1.0).then_inc(b_ln, 1)

            for h in range(NB_HEADS):
                attn_a(h)
                attn_b1(h)
                act.wait_ge(b_cm, 2 * (h + 1))
                nc.scalar.activation(attb, attb, ACT.Exp).then_inc(b_att, 1)
                if h % 2:
                    j = h // 2
                    act.wait_ge(o_ps, NQ + 2 * (h + 1))
                    nc.scalar.copy(mix_hi[:, j, :], ps[:, 6, 0:T]).then_inc(o_hi, 1)
                    nc.scalar.copy(mix_hi[:, 4 + j, :], ps[:, 7, 0:T]).then_inc(o_hi, 1)
            for u in range(2):
                after(s_idx[f"upa{u}"])
                after(s_idx[f"upb{u}"])
                act.wait_ge(m_sum, u + 1)
                nc.scalar.copy(h_hi[:, 4 * u:4 * u + 4, :], merged(u)).then_inc(m_hi, 1)
            for i4 in range(4):
                after(s_idx[f"o2{i4}"])
            act.wait_ge(pe_tile, s_idx["o23"] + 1)
            for q in range(4):
                nc.scalar.activation(xn_scratch[:, 0:512], ps[:, q, :], ACT.Square, accum_out=part[:, q:q + 1]).then_inc(sqy, 1)
                act.wait_ge(sqy, q + 1)
            root(4)
            root(5)
            norm_hi(3, lambda k: scl[:, k:k + 1], lambda k: modT[:, 24 + k:25 + k])

            def ff2_step(st, i=0):
                s0 = s_idx[f"fa{st}"]
                act.wait_ge(pe_tile, i * 6 + (s0 + 1))
                if st >= 3:
                    act.wait_ge(hid2_done, i * 3 + (st - 2))
                nc.scalar.activation(ff_act[st % 3], ps[:, 4 + st % 3, :], ACT.Relu).then_inc(relu2_done, 1)
                after(s0, i)
                act.wait_ge(hid2_done, i * 3 + (st + 1))
                if st >= 3:
                    act.wait_ge(pe_tile, i * 6 + (s0 - 4 + 1))
                nc.scalar.copy(hid_hi[st % 3], ff_hid[st % 3].rearrange("p (c t) -> p c t", c=2)).then_inc(hid2hi_done, 1)
                if st >= 1:
                    after(s0 + 1, i)

            for st in range(5):
                ff2_step(st)
            with act.Fori(1, TURNS) as i:
                ff2_step(2, i)
                ff2_step(3, i)
                ff2_step(4, i)
            ff2_step(14)
            ff2_step(15)
            act.wait_ge(pe_tile, s_idx["fb15"] + 1)
            for q in range(4):
                nc.scalar.activation(xn_scratch[:, 0:512], ps[:, q, :], ACT.Square, accum_out=part[:, q:q + 1]).then_inc(sqy, 1)
                act.wait_ge(sqy, 4 + q + 1)
            root(6)

        @block.vector
        def _(dve):
            V = nc.vector
            steps = [0]

            def link(ins):
                steps[0] += 1
                ins.then_inc(dstep, 1)
                dve.wait_ge(dstep, steps[0])

            def split(s, name, i=0):
                dve.wait_ge(hi_ready, i * 6 + (s + 1))
                w = tile_width(name)
                V.tensor_tensor(w_lo[:, s % RING, 0:w], raw[:, n_of[name] % RAW, 0:w],
                                w_hi[:, s % RING, 0:w].bitcast(F32), ALU.subtract).then_inc(w_ready, 1)

            def after(s, i=0):
                if s + RING < NSPLIT:
                    split(s + RING, s_name[s + RING], i)

            roots = [0]

            def rstd():
                V.tensor_scalar(msum, msum, EPS, None, ALU.add).then_inc(ms_ready, 1)
                roots[0] += 1
                dve.wait_ge(sq_ready, roots[0])
                link(V.reciprocal(rst, sqv))
                newton(rst, msum, nwt)

            def newton(r, v, t):
                link(V.tensor_tensor(t, r, r, ALU.mult))
                link(V.tensor_tensor(t, t, v, ALU.mult))
                link(V.tensor_scalar(t, t, -0.5, 1.5, ALU.mult, ALU.add))
                link(V.tensor_tensor(r, r, t, ALU.mult))

            def norm_x():
                for m in range(2):
                    link(V.tensor_tensor_reduce(xn_scratch, x[:, m, :], x[:, m, :], 1.0 / D, 0.0, ALU.mult, ALU.add, msum[:, m:m + 1]))
                rstd()

            def norm_scale():
                for m in range(2):
                    V.tensor_scalar(xn[:, m, :], x[:, m, :], rst[:, m:m + 1], None, ALU.mult).then_inc(xn_ready, 1)

            def norm_lo(t, scale, bias=None):
                for k in range(DC):
                    src = ps[:, 4 + k // 2, (k % 2) * T:(k % 2 + 1) * T]
                    dve.wait_ge(hhi_ready, 8 * t + 2 * (k // 2) + 2)
                    hi = h_hi[:, k, :].bitcast(F32)
                    if bias is None:
                        V.scalar_tensor_tensor(h_lo[:, k, :], src, scale(k), hi, ALU.mult, ALU.subtract).then_inc(h_ready, 1)
                    else:
                        link(V.tensor_scalar(htmp[:, k % 2, :], src, scale(k), bias(k), ALU.mult, ALU.add))
                        V.tensor_tensor(h_lo[:, k, :], htmp[:, k % 2, :], hi, ALU.subtract).then_inc(h_ready, 1)

            def diagonals(v):
                for k in range(DC):
                    i = V.tensor_scalar(diag[:, k, :], ident, v[:, k:k + 1], None, ALU.mult)
                i.then_inc(diag_ready, 1)

            def row(t):
                dve.wait_ge(row_ps, t + 1)
                V.tensor_copy(rowb, ps[:, 4:6, :].rearrange("p a n -> p (a n)")).then_inc(row_ready, 1)
                dve.wait_ge(row_ready, t + 1)

            dve.wait_ge(s_x, 32)
            norm_x()
            norm_scale()
            for s in range(RING):
                split(s, s_name[s])
            dve.wait_ge(vec_ps, 1)
            V.tensor_copy(vec[:, :], ps[:, 0, 0:NA_ROWS]).then_inc(vec_ready, 1)
            V.tensor_copy(vec_b[:, :], ps[:, 0, P:P + NB_ROWS]).then_inc(vec_ready, 1)
            dve.wait_ge(vec_ready, 2)
            norm_lo(0, lambda k: col("attn_norm", k))

            taps = [(w, c) for w in range(CONV_W) for c in range(2)]
            base = steps[0]
            for s in range(12):
                if s == 1:
                    dve.wait_ge(z_evac, 2)
                    dve.wait_ge(zeroed, 1)
                    link(V.tensor_tensor(ypad[:, :, CONV_W - 1:], zt(U), zt(V_), ALU.mult))
                after(s)
                if s >= 1:
                    for w, c in taps[8 * (s - 1):8 * s]:
                        src, wcol = ypad[:, c, w:w + T], vec_b[:, 2 * w + c:2 * w + c + 1]
                        if w == 0:
                            i = V.tensor_scalar(conv[:, c, :], src, wcol, col("conv_b", c), ALU.mult, ALU.add)
                        else:
                            if c == 0 or w > 0:
                                dve.wait_ge(dstep, steps[0] - 1)
                            i = V.scalar_tensor_tensor(conv[:, c, :], src, wcol, conv[:, c, :], ALU.mult, ALU.add)
                        if (w, c) == taps[-1]:
                            i.then_inc(conv_ready, 1)
                        else:
                            steps[0] += 1
                            i.then_inc(dstep, 1)
                if s == 8:
                    dve.wait_ge(dstep, steps[0])
                    dve.wait_ge(conv_ready, 1)
                    dve.wait_ge(conv_mean, 1)
                    link(V.tensor_tensor(lnd, conv, ps[:, 3:4, 0:T].to_broadcast([P, 2, T]), ALU.subtract))
                    V.tensor_tensor(lnq, lnd, lnd, ALU.mult).then_inc(convd_ready, 1)
            dve.wait_ge(conv_var, 1)
            V.tensor_scalar(lnv[:, 0, :], ps[:, 3, T:2 * T], EPS, None, ALU.add).then_inc(lnv_ready, 1)
            dve.wait_ge(lnsq_ready, 1)
            link(V.reciprocal(lnq[:, 0, :], lnv[:, 1, :]))
            newton(lnq[:, 0, :], lnv[:, 0, :], lnq[:, 1, :])
            V.tensor_tensor(lnd, lnd, lnq[:, 0:1, :].to_broadcast([P, 2, T]), ALU.mult).then_inc(lnn_ready, 1)
            for c in range(2):
                dve.wait_ge(chi_ready, c + 1)
                V.tensor_tensor(mix_lo[:, c, :], conv[:, c, :], mix_hi[:, c, :].bitcast(F32), ALU.subtract).then_inc(clo_ready, 1)

            for a in range(2):
                dve.wait_ge(cmp_sb, a + 1)
                v = xs_cmp(a).rearrange("p (l f n) -> p l f n", l=2, f=2)
                link(V.tensor_tensor(pebias[:, 2 * a:2 * a + 2].rearrange("p (f o) -> p f o", o=1), v[:, 0, :, 64:65], v[:, 1, :, 65:66], ALU.add))
                for f in range(2):
                    lo = v[:, 0, f, 0:64].rearrange("p (g c) -> p g c", g=NKV)[:, :, 0:15]
                    hi = v[:, 1, f, 0:64].rearrange("p (g c) -> p g c", g=NKV)[:, :, 1:16]
                    i = V.tensor_tensor(cmp_hidden(a)[:, f], lo, hi, ALU.add)
                    if f == 0:
                        link(i)
                i.then_inc(cmp_sum, 1)
            dve.wait_ge(zeroed, 2)
            dve.wait_ge(cmp2_ps, 2)
            for h in range(NQ):
                g = h // 3
                V.tensor_copy(vblk[32 * (h % 4):32 * (h % 4 + 1), h, :], ps[32 * g:32 * (g + 1), 7, 0:HD]).then_inc(vblk_ready, 1)
            dve.wait_ge(sc_ps, 1)
            for e in range(2):
                half = lambda a: a.rearrange("p (a e n) -> p a e n", a=4, e=2)[:, :, e, :]
                link(V.tensor_tensor(half(turned[:, 0:384]), ps[:, 4 + e, 0:192].rearrange("p (a n) -> p a n", a=4),
                                     half(shared[:, 256:640]), ALU.add))
            mx, sm = st24
            link(V.tensor_reduce(mx, scmp, AX.X, ALU.max))
            link(V.tensor_scalar(mx, mx, -1.0e20, None, ALU.max))
            V.tensor_tensor(scmp, scmp, wide(mx), ALU.subtract).then_inc(sc_sb, 1)
            link(V.memset(soft[:, 0:768], 0.0))
            dve.wait_ge(pc_exp, 1)
            link(V.tensor_reduce(sm, scmp, AX.X, ALU.add))
            link(V.tensor_scalar(sm, sm, 1.0e-30, None, ALU.max))
            link(V.reciprocal(mx, sm))
            dve.wait_ge(z_evac, 12)
            link(V.tensor_tensor(mx, mx, gates[:, :, :, 0], ALU.mult))
            V.tensor_tensor(pcmp[:, :, :, 0:CMP_SLOT], scmp, wide(mx), ALU.mult).then_inc(pc_ready, 1)
            dve.wait_ge(pcT_ps, 1)
            for c in range(3):
                V.tensor_copy(pcT[:, c, :], ps[:, 4 + c // 2, (c % 2) * T:(c % 2 + 1) * T]).then_inc(pcT_ready, 1)

            order = [6 * p + r + 3 * e for p in range(2) for r in range(3) for e in range(2)]

            def masked(n):
                h = order[n]
                dve.wait_ge(s_ps, n + 1)
                dve.wait_ge(alibi_ready, NQ)
                for br in range(2):
                    for m in range(2):
                        at = (2 * (n % 2) + br) * 384
                        c = 2 * br + m
                        bias = alibi[:, T * h:T * (h + 1)] if m else alibi[:, T * h + P:T * (h + 1)]
                        V.tensor_tensor_reduce(soft[:, at + m * P:at + P + m * T], ps[:, 2 * (n % 2) + br, m * P:P + m * T], bias,
                                               -1.0, 3.0e38, ALU.add, ALU.min, nmax[:, n % 2, c:c + 1]).then_inc(s_sb, 1)

            masked(0)
            for n in range(NQ):
                h = order[n]
                if n + 1 < NQ:
                    if n >= 1:
                        dve.wait_ge(pT_ps, n)
                    masked(n + 1)
                dve.wait_ge(p_exp, 4 * (n + 1))
                link(V.reciprocal(coef[:, n % 2, :], psum_p[:, n % 2, :]))
                cf = coef[:, n % 2, :].rearrange("p (b m) -> p b m", b=2)
                gt = gates[:, :, h, 1:3].rearrange("p m b -> p b m")
                link(V.tensor_tensor(cf, cf, gt, ALU.mult))
                for br in range(2):
                    for m in range(2):
                        o = soft[:, (2 * (n % 2) + br) * 384 + m * P:(2 * (n % 2) + br) * 384 + P + m * T]
                        V.tensor_scalar(o, o, coef[:, n % 2, 2 * br + m:2 * br + m + 1], None, ALU.mult).then_inc(p_ready, 1)
                dve.wait_ge(pT_ps, n + 1)
                if n >= 1:
                    dve.wait_ge(o_ps, n)
                for br in range(2):
                    V.tensor_copy(turned[:, 384 * br:384 * (br + 1)], ps[:, 4 + br, 0:384]).then_inc(pT_ready, 1)
                if n % 2:
                    j = n // 2
                    dve.wait_ge(o_hi, j + 1)
                    V.tensor_tensor(mix_lo[:, 2 + j, :], ps[:, 6, 0:T], mix_hi[:, 2 + j, :].bitcast(F32), ALU.subtract).then_inc(o_lo, 1)
            dve.wait_ge(direct_done, 28)
            link(V.tensor_tensor(modT[:, :], ps[:, 7, 2 * T - 48:2 * T], vec[:, VEC_A["b_ada"][0]:VEC_A["b_ada"][0] + 48], ALU.add))
            for i4 in range(4):
                after(s_idx[f"out{i4}"])
            dve.wait_ge(pe_tile, s_idx["out3"] + 1)
            for q in range(4):
                xs = x[:, q // 2, (q % 2) * 512:(q % 2 + 1) * 512]
                V.tensor_tensor(xs, xs, ps[:, q, :], ALU.add).then_inc(x_new, 1)
            dve.wait_ge(x_new, 4)
            norm_x()
            norm_scale()
            norm_lo(1, lambda k: col("ffn_norm", k))

            def ff1_step(st, i=0):
                s0 = s_idx[f"gate{st}"]
                after(s0, i)
                dve.wait_ge(pe_tile, i * 6 + (s0 + 2))
                dve.wait_ge(silu_done, i * 2 + (st + 1))
                if st >= 2:
                    dve.wait_ge(hidlo_done, i * 2 + (st - 1))
                V.tensor_tensor(ff_hid[st % 2], ff_act[st % 2], ps[:, 5 + 2 * (st % 2), :], ALU.mult).then_inc(hid_done, 1)
                after(s0 + 1, i)
                dve.wait_ge(hidhi_done, i * 2 + (st + 1))
                V.tensor_tensor(hid_lo[st % 2], ff_hid[st % 2].rearrange("p (c t) -> p c t", c=2),
                                hid_hi[st % 2].bitcast(F32), ALU.subtract).then_inc(hidlo_done, 1)
                if st >= 1:
                    after(s0 + 2, i)

            ff1_step(0)
            ff1_step(1)
            with dve.Fori(0, TURNS) as i:
                ff1_step(2, i)
                ff1_step(3, i)
            ff1_step(10)
            after(s_idx["down10"])
            diagonals(vec[:, VEC_A["final"][0]:VEC_A["final"][0] + 8])
            dve.wait_ge(pe_tile, s_idx["down10"] + 1)
            for q in range(4):
                xs = x[:, q // 2, (q % 2) * 512:(q % 2 + 1) * 512]
                V.tensor_tensor(xs, xs, ps[:, q, :], ALU.add).then_inc(x_new, 1)
            dve.wait_ge(x_new, 8)
            norm_x()
            row(0)
            for m in range(2):
                V.scalar_tensor_tensor(x[:, m, :], x[:, m, :], rst[:, m:m + 1], rowb, ALU.mult, ALU.mult).then_inc(x_new, 1)
            dve.wait_ge(x_new, 10)

            def modulated(g, i):
                link(V.tensor_scalar(scl, modT[:, i:i + 8], 1.0, None, ALU.add))
                link(V.tensor_tensor(scl, scl, vec[:, VEC_A[g][0]:VEC_A[g][0] + 8], ALU.mult))

            norm_x()
            modulated("g_pre_mix", 8)
            norm_scale()
            norm_lo(2, lambda k: scl[:, k:k + 1], lambda k: modT[:, k:k + 1])

            cos, sin = shared[:, 0:T], shared[:, T:2 * T]
            rots = [0]

            def rotate(view, groups):
                n = groups * T
                dve.wait_ge(rot_ps, rots[0] + 1)
                t = rtmp[:, 0:n].rearrange("p (g t) -> p g t", g=groups)
                s = ps[:, 3, 0:n].rearrange("p (g t) -> p g t", g=groups)
                v = view.rearrange("p (g t) -> p g t", g=groups)
                bc = lambda a: a.rearrange("p (g t) -> p g t", g=1).to_broadcast([P, groups, T])
                link(V.tensor_tensor(t, s, bc(sin), ALU.mult))
                link(V.tensor_tensor(v, v, bc(cos), ALU.mult))
                V.tensor_tensor(v, v, t, ALU.add).then_inc(rot_done, 1)
                rots[0] += 1

            def index_sum(h):
                dve.wait_ge(relu_done, h + 1)
                if h >= 1:
                    dve.wait_ge(ix_acc, 2 * h)
                for m in range(2):
                    o = isc[:, m * P:P + m * T]
                    base_ = (cst("causal") if m else cst("causal")[:, P:T]) if h == 0 else o
                    V.scalar_tensor_tensor(o, relu_b[h % 2][:, m * P:P + m * T], wi_s[:, m, h:h + 1], base_,
                                           ALU.mult, ALU.add).then_inc(ix_acc, 1)

            def take8(m):
                o = isc[:, m * P:P + m * T]
                link(V.max(top8, o))
                link(V.match_replace(o, top8, o, TAKEN))

            takes = [m for _ in range(TOPK // 8) for m in range(2)]
            for s in range(s_idx["idx"], s_idx["sg7"] + 1):
                name = s_name[s]
                after(s)
                if name == "qa0":
                    rotate(kiT, 1)
                    rotate(z[:, QI, :], 2)
                    rotate(z[:, QI + 1, :], 2)
                if name == "qa1":
                    for h in range(4):
                        index_sum(h)
                    rotate(z[:, QA, :], 2)
                if name == "ka0":
                    for h in range(4, 8):
                        index_sum(h)
                    rotate(z[:, QA + 1, :], 2)
                    dve.wait_ge(ix_acc, 16)
                if name == "ka1":
                    rotate(z[:, KA, :], 2)
                if name == "qb0":
                    rotate(z[:, KA + 1, :], 2)
                if s > s_idx["ka0"] and takes:
                    for m in takes[:2]:
                        take8(m)
                    takes = takes[2:]
            assert not takes
            link(V.tensor_scalar(abias, isc, TAKEN, NEG, ALU.not_equal, ALU.mult))
            for m in range(2):
                o = abias[:, m * P:P + m * T]
                V.tensor_tensor(o, o, cst("causal") if m else cst("causal")[:, P:T], ALU.add).then_inc(bias_ready, 1)
            dve.wait_ge(bias_ready, 2)

            def a_masked(h):
                dve.wait_ge(s_ps, NQ + h + 1)
                for m in range(2):
                    V.tensor_tensor_reduce(sA[h % 2][:, m * P:P + m * T], ps[:, h % 2, m * P:P + m * T], abias[:, m * P:P + m * T],
                                           -1.0, 3.0e38, ALU.add, ALU.min, nmax[:, h % 2, m:m + 1]).then_inc(s_sb, 1)

            def diag_masked(dst, bank, inc):
                two = lambda a: a.rearrange("p (k n) -> p k n", n=P)[:, 0:3:2, :]
                link(V.tensor_tensor(two(dst), two(ps[:, bank, 0:384]), cst("strict").rearrange("p (o n) -> p o n", o=1).to_broadcast([P, 2, P]), ALU.add))
                V.tensor_copy(dst[:, P:T], ps[:, bank, P:T]).then_inc(inc, 1)

            def b_front(h):
                dve.wait_ge(b_z, h + 1)
                diag_masked(zm[h % 2], 3 + h % 2, b_zm)
                dve.wait_ge(b_zm, h + 1)
                if h >= 1:
                    dve.wait_ge(b_sp, h)
                V.scalar_tensor_tensor(eb, zm[h % 2], -1.0, zm[h % 2], ALU.mult, ALU.min).then_inc(b_abs, 1)

            a_masked(0)
            for h in range(NB_HEADS):
                b_front(h)
                if h + 1 < NB_HEADS:
                    if h >= 1:
                        dve.wait_ge(pT_ps, NQ + h)
                    a_masked(h + 1)
                dve.wait_ge(b_ln, h + 1)
                if h >= 1:
                    dve.wait_ge(b_c, h)
                V.scalar_tensor_tensor(spb, zm[h % 2], 0.0, eb, ALU.max, ALU.add).then_inc(b_sp, 1)
                dve.wait_ge(p_exp, 4 * NQ + 2 * (h + 1))
                link(V.reciprocal(coef[:, h % 2, 0:2], psum_p[:, h % 2, 0:2]))
                for m in range(2):
                    o = sA[h % 2][:, m * P:P + m * T]
                    V.tensor_scalar(o, o, coef[:, h % 2, m:m + 1], None, ALU.mult).then_inc(p_ready, 1)
                dve.wait_ge(pT_ps, NQ + h + 1)
                if h >= 1:
                    dve.wait_ge(o_ps, NQ + 2 * h)
                V.tensor_copy(pTA, ps[:, 2, 0:384]).then_inc(pT_ready, 1)
                dve.wait_ge(b_c, h + 1)
                two = lambda a: a.rearrange("p (k n) -> p k n", n=P)[:, 0:3:2, :]
                V.tensor_tensor(two(attb), two(ps[:, 5, 0:384]), cst("strict").rearrange("p (o n) -> p o n", o=1).to_broadcast([P, 2, P]),
                                ALU.add).then_inc(b_cm, 1)
                V.tensor_copy(attb[:, P:T], ps[:, 5, P:T]).then_inc(b_cm, 1)
                if h % 2:
                    j = h // 2
                    for e in range(2):
                        dve.wait_ge(o_hi, 6 + 2 * j + e + 1)
                        V.tensor_tensor(mix_lo[:, 4 * e + j, :], ps[:, 6 + e, 0:T], mix_hi[:, 4 * e + j, :].bitcast(F32), ALU.subtract).then_inc(o_lo, 1)

            for u in range(2):
                after(s_idx[f"upa{u}"])
                dve.wait_ge(pe_tile, s_idx[f"upa{u}"] + 1)
                ga, gb = sgate[:, 0, 4 * u:4 * u + 4, :], sgate[:, 1, 4 * u:4 * u + 4, :]
                pa = ps[:, 4 * u:4 * u + 2, :].rearrange("p a (c t) -> p (a c) t", c=2)
                pb = ps[:, 4 * u + 2:4 * u + 4, :].rearrange("p a (c t) -> p (a c) t", c=2)
                V.tensor_tensor(ga, pa, ga, ALU.mult).then_inc(up_a, 1)
                after(s_idx[f"upb{u}"])
                dve.wait_ge(pe_tile, s_idx[f"upb{u}"] + 1)
                link(V.tensor_tensor(gb, pb, gb, ALU.mult))
                dve.wait_ge(up_a, u + 1)
                V.tensor_tensor(merged(u), ga, gb, ALU.add).then_inc(m_sum, 1)
                dve.wait_ge(m_hi, u + 1)
                V.tensor_tensor(h_lo[:, 4 * u:4 * u + 4, :], merged(u), h_hi[:, 4 * u:4 * u + 4, :].bitcast(F32), ALU.subtract).then_inc(m_lo, 1)
            for i4 in range(4):
                after(s_idx[f"o2{i4}"])

            def post_norm(t, g, i, target):
                link(V.tensor_tensor(scl, modT[:, i:i + 8], vec[:, VEC_A[g][0]:VEC_A[g][0] + 8], ALU.mult))
                diagonals(scl)
                dve.wait_ge(sqy, 4 * t)
                halves = part.rearrange("p (m n) -> p m n", m=2)
                link(V.tensor_reduce(msum, halves, AX.X, ALU.add))
                link(V.tensor_scalar(msum, msum, 1.0 / D, None, ALU.mult))
                rstd()
                row(t)
                for q in range(4):
                    xs = x[:, q // 2, (q % 2) * 512:(q % 2 + 1) * 512]
                    t_ = xn_scratch[:, 512 * (q % 2):512 * (q % 2 + 1)]
                    link(V.scalar_tensor_tensor(t_, ps[:, q, :], rst[:, q // 2:q // 2 + 1], rowb[:, (q % 2) * 512:(q % 2 + 1) * 512], ALU.mult, ALU.mult))
                    V.tensor_tensor(xs, xs, t_, ALU.add).then_inc(y_res, 1)
                dve.wait_ge(y_res, 4 * t)

            post_norm(1, "g_post_mix", 16, None)
            norm_x()
            modulated("g_pre_ffn", 32)
            norm_scale()
            norm_lo(3, lambda k: scl[:, k:k + 1], lambda k: modT[:, 24 + k:25 + k])

            def ff2_step(st, i=0):
                s0 = s_idx[f"fa{st}"]
                after(s0, i)
                dve.wait_ge(relu2_done, i * 3 + (st + 1))
                if st >= 3:
                    dve.wait_ge(hid2lo_done, i * 3 + (st - 2))
                V.tensor_tensor(ff_hid[st % 3], ff_act[st % 3], ff_act[st % 3], ALU.mult).then_inc(hid2_done, 1)
                dve.wait_ge(hid2hi_done, i * 3 + (st + 1))
                V.tensor_tensor(hid_lo[st % 3], ff_hid[st % 3].rearrange("p (c t) -> p c t", c=2),
                                hid_hi[st % 3].bitcast(F32), ALU.subtract).then_inc(hid2lo_done, 1)
                if st >= 1:
                    after(s0 + 1, i)

            for st in range(5):
                ff2_step(st)
            with dve.Fori(1, TURNS) as i:
                ff2_step(2, i)
                ff2_step(3, i)
                ff2_step(4, i)
            ff2_step(14)
            ff2_step(15)
            post_norm(2, "g_post_ffn", 40, None)


def _cols(w):
    k, n = w.shape[0] // 128, w.shape[1] // 256
    return w.reshape(k, 128, n, 256).transpose(2, 1, 0, 3).reshape(n, 128, k * 256)


def _rows(w):
    return w.reshape(-1, 2, 128, 1024).transpose(0, 2, 1, 3).reshape(-1, 128, 2048)


def _narrow(w):
    return np.ascontiguousarray(w.reshape(8, 128, -1).transpose(1, 0, 2).reshape(128, -1))


def _pair_heads(w, axis):
    s = w.shape
    shape = s[:axis] + (2, 2, 3, 64) + s[axis + 1:]
    order = list(range(len(shape)))
    order[axis + 1], order[axis + 2] = axis + 2, axis + 1
    return w.reshape(shape).transpose(order).reshape(s)


def _layout(a):
    f = lambda n: np.asarray(a[n])[0]
    w_in, w_out, gu, down = f("w_in"), f("w_out"), f("w_gate_up"), f("w_down")
    q = _pair_heads(w_in[:, 512:1280], 1)
    kv = lambda i: w_in[:, 1280 + 256 * i:1536 + 256 * i]
    first = [w_in[:, 0:512], q, kv(0), kv(1), kv(2), kv(4), kv(3), kv(5)]
    w_g = _narrow(w_in[:, 2816:2852])
    cmp1 = [f(n).reshape(2, 8, 128, 256).transpose(0, 2, 1, 3).reshape(2, 128, 2048) for n in ("cmp_k_w1", "cmp_v_w1")]
    out1 = np.concatenate([w_out[:256], _pair_heads(w_out[256:], 0)], 0)
    gate, up, dn = _cols(gu[:, :2816]), _cols(gu[:, 2816:]), _rows(down)
    ffn1 = [gate[0:1], up[0:1]]
    for i in range(1, FF1_STEPS):
        ffn1 += [gate[i:i + 1], up[i:i + 1], dn[i - 1:i]]
    ffn1 += [dn[-1:]]
    w2 = f("w_in_2")
    qa, ka, va, qb, kb, vb, qi = (w2[:, 512 * i:512 * (i + 1)] for i in range(7))
    ki, wi, sg = w2[:, 3584:3648], w2[:, 3648:3656], w2[:, 3656:]
    w_idx = _narrow(np.concatenate([ki, ki, wi], 1))
    ups = [f(n).reshape(4, 128, 2, 512).transpose(2, 1, 0, 3).reshape(2, 128, 2048) for n in ("w_up_a_2", "w_up_b_2")]
    fa, fb = _cols(f("w_ff1_2")), _rows(f("w_ff2_2"))
    ffn2 = [fa[0:1]]
    for i in range(1, FF2_STEPS):
        ffn2 += [fa[i:i + 1], fb[i - 1:i]]
    ffn2 += [fb[-1:]]
    stream = [_cols(np.concatenate(first, 1)), _rows(out1)[0:3], *cmp1, _cols(f("w_ada_2")), _rows(out1)[3:4], *ffn1,
              _cols(np.concatenate([qi, qa, ka, qb, kb, va, vb, sg], 1)),
              ups[0][0:1], ups[1][0:1], ups[0][1:2], ups[1][1:2], _rows(f("w_out_2")), *ffn2]
    wts = np.concatenate(stream, 0)
    vecs = {"attn_norm": f("attn_norm"), "ffn_norm": f("ffn_norm"), "g_pre_mix": f("g_pre_mix_2"), "g_pre_ffn": f("g_pre_ffn_2"),
            "c": f("c_2"), "b_ada": f("b_ada_2"), "conv_b": f("conv_b"), "ln_g": f("conv_ln_g"), "ln_b": f("conv_ln_b"),
            "g_post_mix": f("g_post_mix_2"), "g_post_ffn": f("g_post_ffn_2"), "final": np.asarray(a["final_norm"])}
    rows_a = np.concatenate([vecs[n].reshape(-1, 128) for n in VEC_A], 0)
    rows_b = np.concatenate([f("conv_w").reshape(-1, 128), f("cmp_k_pe").reshape(-1, 128), f("cmp_v_pe").reshape(-1, 128)], 0)
    w2c = np.concatenate([f(n).reshape(2, 128, 64).transpose(1, 0, 2).reshape(128, 128) for n in ("cmp_k_w2", "cmp_v_w2")], 1)
    return {"x": np.asarray(a["x"])[0], "wts": wts, "w_g": w_g, "w_idx": w_idx, "rows_a": rows_a, "rows_b": rows_b, "cmp_w2": w2c}


def _constants():
    p, t = np.arange(128), np.arange(256)
    c = {"ident": np.eye(128), "tri": -(p[:, None] >= p[None, :]).astype(np.float32), "negones": -np.ones((128, 128)),
         "strict": np.where(p[:, None] < p[None, :], 0.0, NEG), "mean": np.full((128, 128), 1.0 / 256), "ones": np.ones((128, 128))}
    dist = t[None, :] - (p[:, None] + 128)
    c["causal"] = np.where(dist <= 0, 0.0, NEG)
    const = np.concatenate([c[n] for n in CONST], 1).astype(np.float32)
    sl = np.asarray(slopes())
    tt = np.arange(256).reshape(2, 128)
    n = np.arange(16)
    center, end = n * 16 + 15.5, n * 16 + 31
    valid = (end[None, None, :] <= tt[:, :, None]) & (n < 15)
    cb = np.where(valid[:, :, None, :], -sl[None, None, :, None] * (tt[:, :, None, None] - center), NEG)
    shared_1 = np.concatenate([np.where(dist <= 0, dist, -1.0e33), cb.transpose(1, 0, 2, 3).reshape(128, -1)], 1).astype(np.float32)
    ang = np.arange(256, dtype=np.float32)[:, None] * (500000.0 ** (-np.arange(0, 16, 2, dtype=np.float32) / 16)).astype(np.float32)
    cos, sin, swap = np.ones((128, 256)), np.zeros((128, 256)), np.zeros((128, 128))
    for b in (0, 64):
        for i in range(8):
            cos[b + i] = cos[b + 8 + i] = np.cos(ang[:, i])
            sin[b + i] = sin[b + 8 + i] = np.sin(ang[:, i])
            swap[b + 8 + i, b + i] = -1.0
            swap[b + i, b + 8 + i] = 1.0
    shared_2 = np.concatenate([cos, sin, swap], 1).astype(np.float32)
    return {"const": const, "shared_1": shared_1, "shared_2": shared_2}


def kernel(**inputs):
    import concourse.bacc as _bacc
    from concourse.bass_utils import run_bass_kernel_spmd as _run

    nc = _bacc.Bacc("TRN2", target_bir_lowering=False, num_devices=1)
    arrays = {n: np.ascontiguousarray(v) for n, v in {**_layout(inputs), **_constants()}.items()}
    ap = {n: nc.dram_tensor(n, v.shape, mybir.dt.from_np(v.dtype), kind="ExternalInput").ap() for n, v in arrays.items()}
    out = nc.dram_tensor("out", (T, D), F32, kind="ExternalOutput").ap()
    build(nc, ap["x"], ap["wts"], ap["w_g"], ap["w_idx"], ap["rows_a"], ap["rows_b"], ap["cmp_w2"], ap["const"],
          ap["shared_1"], ap["shared_2"], out)
    r = _run(nc, [arrays], core_ids=[0])
    return r.results[0]["out"].reshape(1, T, D)
```

```python
import math
from contextlib import ExitStack

import numpy as np

import concourse.bass as bass
from concourse import mybir

F32 = mybir.dt.float32
F32R = mybir.dt.float32r
ALU = mybir.AluOpType
ACT = mybir.ActivationFunctionType
AX = mybir.AxisListType

P = 128
T = 256
D = 1024
DC = D // P
HD = 64
EPS = 1e-6
CONV_W = 31
NQ, NKV = 12, 4
NB_HEADS = 8
TOPK = T // 4
N_CMP = 15
CMP_SLOT = 16
FF1_STEPS = 11
FF2_STEPS = 16
NEG = -1.0e30
TAKEN = -3.0e38

TW = 2048
RAW, RING = 3, 3
TURN = 6

def plan():
    tiles = [("s", n) for n in ("u", "v", "kc", "vc", "q0", "q1", "q2", "ks", "kw", "g", "vs")]
    tiles += [("d", f"cmp{i}") for i in range(4)] + [("s", "vw")]
    tiles += [("s", f"out{i}") for i in range(3)]
    tiles += [("s", "out3"), ("s", "gate0"), ("s", "up0")]
    for i in range(1, FF1_STEPS):
        tiles += [("s", f"gate{i}"), ("s", f"up{i}"), ("s", f"down{i - 1}")]
    tiles += [("s", f"down{FF1_STEPS - 1}")]
    tiles += [("s", n) for n in ("idx", "qi0", "qi1", "qa0", "qa1", "ka0", "ka1", "qb0", "qb1", "kb0", "kb1",
                                 "va0", "va1", "vb0", "vb1")]
    tiles += [("s", f"sg{i}") for i in range(8)]
    tiles += [("s", n) for n in ("upa0", "upb0", "upa1", "upb1")] + [("s", f"o2{i}") for i in range(4)]
    tiles += [("s", "fa0")]
    for i in range(1, FF2_STEPS):
        tiles += [("s", f"fa{i}"), ("s", f"fb{i - 1}")]
    tiles += [("s", f"fb{FF2_STEPS - 1}")]
    return tiles


TILES = plan()
G_COLS = 36
IDX_COLS = 136

VEC_A = {}
for _name, _rows in (("attn_norm", 8), ("ffn_norm", 8), ("g_pre_mix", 8), ("g_pre_ffn", 8), ("c", 8), ("b_ada", 48),
                     ("conv_b", 2), ("ln_g", 2), ("ln_b", 2), ("g_post_mix", 8), ("g_post_ffn", 8), ("final", 8)):
    VEC_A[_name] = (sum(r for _, r in VEC_A.values()), _rows)
NA_ROWS = sum(r for _, r in VEC_A.values())
NB_ROWS = 2 * CONV_W + 32

CONST = {}
for _name, _w in (("ident", 128), ("causal", 256), ("tri", 128), ("negones", 128), ("strict", 128), ("mean", 128),
                  ("ones", 128)):
    CONST[_name] = (sum(w for _, w in CONST.values()), _w)
NCONST = sum(w for _, w in CONST.values())
NSHARED = 640


def slopes():
    def pow2(m):
        return [(2.0 ** (-8.0 / m)) ** (i + 1) for i in range(m)]
    return [float(s) for s in np.asarray(pow2(8) + pow2(16)[0::2][:NQ - 8], np.float32)]


def build(nc, x_in, wts, w_ada, w_g, w_idx, rows_a, rows_b, cmp_w2, const_in, shared_1, shared_2, out):
    ctx = ExitStack()
    with ctx:
        def sb(name, shape, dt=F32):
            return ctx.enter_context(nc.sbuf_tensor(name, shape, dt))

        def sem(name):
            return ctx.enter_context(nc.semaphore(name))

        raw = sb("raw", [P, RAW, TW])
        w_hi = sb("w_hi", [P, RING, TW], F32R)
        w_lo = sb("w_lo", [P, RING, TW], F32R)
        x = sb("resid", [P, 2, D])
        h_hi = sb("h_hi", [P, DC, T], F32R)
        h_lo = sb("h_lo", [P, DC, T], F32R)
        mix_hi = sb("mix_hi", [P, DC, T], F32R)
        mix_lo = sb("mix_lo", [P, DC, T], F32R)
        const = sb("consts", [P, NCONST])
        shared = sb("shared", [P, NSHARED])
        vec = sb("vec", [P, NA_ROWS])
        vec_b = sb("vec_b", [P, NB_ROWS])
        z = sb("z", [P, 14, 2 * T])
        alibi = sb("alibi", [P, 4096])
        soft = sb("soft", [P, 1536])
        turned = sb("turned", [P, 768])
        misc = sb("misc", [P, 2048])
        small = sb("small", [P, 192])
        modT = sb("modT", [P, 48])
        ada = sb("ada", [P, 2, TW])
        mod_tail = sb("mod_tail", [P, TW])
        ps = ctx.enter_context(nc.psum_tensor("ps", [P, 8, 512], F32))

        def cst(name):
            a, w = CONST[name]
            return const[:, a:a + w]

        def col(name, i):
            return vec[:, VEC_A[name][0] + i:VEC_A[name][0] + i + 1]

        ident = cst("ident")

        def zt(i):
            return z[:, i, :].rearrange("p (c t) -> p c t", c=2)
        U, V_, Q0, KC, VC, KS, KW, VS, VW = 0, 1, 2, 5, 6, 7, 8, 9, 10
        z_at = {"u": U, "v": V_, "q0": Q0, "q1": Q0 + 1, "q2": Q0 + 2, "kc": KC, "vc": VC, "ks": KS, "kw": KW, "vs": VS, "vw": VW}
        zflat = z[:, :, :].rearrange("p a b -> p (a b)")
        tail = zflat[:, 11 * 512:14 * 512]
        kr = [tail[:, 528 * i:528 * (i + 1)].rearrange("p (j n) -> p j n", j=8) for i in range(2)]
        hcmp = [tail[:, 1056:1312].rearrange("p (f n) -> p f n", f=2), misc[:, 1536:1792].rearrange("p (f n) -> p f n", f=2)]
        kcmp = tail[:, 1312:1376]
        vblk = misc[:, 0:768].rearrange("p (h d) -> p h d", h=NQ)
        pcT = misc[:, 768:1536].rearrange("p (c t) -> p c t", c=3)
        w2 = misc[:, 1792:2048].rearrange("p (a f d) -> p a f d", a=2, f=2)
        early = ada[:, :, :].rearrange("p a w -> p (a w)")
        ypad = early[:, 0:572].rearrange("p (c t) -> p c t", c=2)
        conv = early[:, 572:1084].rearrange("p (c t) -> p c t", c=2)
        lnv = early[:, 1084:1596].rearrange("p (a t) -> p a t", a=2)
        lnd = z[:, U, :].rearrange("p (c t) -> p c t", c=2)
        lnq = z[:, V_, :].rearrange("p (c t) -> p c t", c=2)
        scmp_flat = early[:, 2364:2748]
        scmp = scmp_flat.rearrange("p (m h n) -> p m h n", m=2, h=NQ)
        pcmp = early[:, 2748:3516].rearrange("p (m h n) -> p m h n", m=2, h=NQ)
        gates = small[:, 0:72].rearrange("p (m h b) -> p m h b", m=2, h=NQ)
        st24 = [small[:, 72 + 24 * i:96 + 24 * i].rearrange("p (m h) -> p m h", m=2) for i in range(2)]
        msum, rst, nwt, sqv = (small[:, 120 + 2 * i:122 + 2 * i] for i in range(4))
        nmax = small[:, 128:136].rearrange("p (a b) -> p a b", a=2)
        psum_p = small[:, 136:144].rearrange("p (a b) -> p a b", a=2)
        coef = small[:, 144:152].rearrange("p (a b) -> p a b", a=2)
        pebias = small[:, 152:156]
        part = small[:, 156:160]
        silu_c = small[:, 160:168]
        scl = small[:, 168:176]
        wi_s = small[:, 176:192].rearrange("p (m h) -> p m h", m=2)
        top8 = small[:, 72:80]
        xn = zflat[:, 0:2048].rearrange("p (m d) -> p m d", m=2)
        xn_scratch = zflat[:, 2048:3072]
        htmp = zflat[:, 3072:3072 + 512].rearrange("p (a t) -> p a t", a=2)
        rowb = zflat[:, 12 * 512:14 * 512]
        diag = zflat[:, 10 * 512:12 * 512].rearrange("p (k n) -> p k n", k=8)
        ff_act = [z[:, i, :] for i in range(3)]
        ff_hid = [z[:, 3 + i, :] for i in range(3)]
        hid_hi = [mix_hi[:, 2 * i:2 * i + 2, :] for i in range(3)]
        hid_lo = [mix_lo[:, 2 * i:2 * i + 2, :] for i in range(3)]
        mod_part = alibi
        QI, QA, KA, QB, KB, VA, VB = 0, 2, 4, 6, 8, 10, 12

        def wide(v):
            return v.rearrange("p m (h o) -> p m h o", o=1).to_broadcast([P, 2, NQ, CMP_SLOT])

        def xs_cmp(a):
            return early[:, 1596 + 264 * a:1860 + 264 * a]

        def cmp_hidden(a):
            return early[:, 2124 + 120 * a:2244 + 120 * a].rearrange("p (f g n) -> p f g n", f=2, g=NKV)

        def merged(u):
            return zflat[:, 1024 * u:1024 * (u + 1)].rearrange("p (c t) -> p c t", c=4)
        def zgrp(i, g):
            return z[:, i + g // 2, (g % 2) * T:(g % 2 + 1) * T]
        sgate = alibi[:, :].rearrange("p (a k t) -> p a k t", a=2, k=8)
        kiT = turned[:, 0:256]
        rtmp = soft[:, 0:512]
        rtmp2 = soft[:, 512:768]
        isc = misc[:, 0:384]
        abias = misc[:, 384:768]
        relu_b = [soft[:, 768 + 384 * i:1152 + 384 * i] for i in range(2)]
        sA = [soft[:, 384 * i:384 * (i + 1)] for i in range(2)]
        pTA = turned[:, 0:384]
        zm = [soft[:, 768 + 384 * i:1152 + 384 * i] for i in range(2)]
        eb = turned[:, 384:768]
        spb = misc[:, 768:1152]
        attb = misc[:, 1152:1536]

        s_raw = [sem(f"raw{i}_landed") for i in range(RAW)]
        s_ada = [sem(f"ada{i}_landed") for i in range(2)]
        ada_used, mod_ps, mod_ready, mod_zeroed = (sem(n) for n in ("ada_used", "mod_ps", "mod_ready", "mod_zeroed"))
        s_x, s_const, s_rows, s_shared, s_w2, s_out = (sem(n) for n in (
            "x_landed", "const_landed", "rows_landed", "shared_landed", "w2_landed", "out_written"))
        hi_ready = sem("hi_ready")
        w_ready = sem("w_ready")
        pe_tile = sem("pe_tile")
        direct_done = sem("direct_done")
        z_evac = sem("z_evac")
        vec_ps, vec_ready = sem("vec_ps"), sem("vec_ready")
        ms_ready, sq_ready = sem("ms_ready"), sem("sq_ready")
        xn_ready, xT_ready, hhi_ready, h_ready = sem("xn_ready"), sem("xT_ready"), sem("hhi_ready"), sem("h_ready")
        dstep, astep, gstep = sem("dve_step"), sem("act_step"), sem("pool_step")
        zeroed, alibi_ready = sem("zeroed"), sem("alibi_ready")
        conv_ready, conv_mean, convd_ready, conv_var = (sem(n) for n in ("conv_ready", "conv_mean", "convd_ready", "conv_var"))
        lnv_ready, lnsq_ready, lnn_ready, chi_ready, clo_ready = (sem(n) for n in (
            "lnv_ready", "lnsq_ready", "lnn_ready", "conv_hi_ready", "conv_lo_ready"))
        kr_ready, cmp_ps, cmp_sb, cmp_sum, cmp_h, cmp2_ps, cmp2_sb, vblk_ready = (sem(n) for n in (
            "kr_ready", "cmp_ps", "cmp_sb", "cmp_sum", "cmp_h", "cmp2_ps", "cmp_keys_ready", "cmp_values_ready"))
        sc_ps, sc_sb, pc_exp, pc_ready, pcT_ps, pcT_ready = (sem(n) for n in (
            "cmp_scores_ps", "cmp_scores_sb", "cmp_probs_exp", "cmp_probs_ready", "cmp_probsT_ps", "cmp_probsT_ready"))
        s_ps, s_sb, p_exp, p_ready, pT_ps, pT_ready, pTw_ready, o_ps, o_hi, o_lo = (sem(n) for n in (
            "scores_ps", "scores_sb", "probs_exp", "probs_ready", "probsT_ps", "probsT_ready", "window_probsT_ready", "o_ps", "o_hi", "o_lo"))
        silu_c_ready = sem("silu_c_ready")
        acc_ps, x_new = sem("acc_ps"), sem("x_new")
        silu_done, hid_done, hidhi_done, hidlo_done = (sem(n) for n in ("silu_done", "hid_done", "hid_hi_done", "hid_lo_done"))
        relu2_done, hid2_done, hid2hi_done, hid2lo_done = (sem(n) for n in ("relu2_done", "hid2_done", "hid2_hi_done", "hid2_lo_done"))
        diag_ready, row_ps, row_ready = sem("diag_ready"), sem("row_ps"), sem("row_ready")
        rot_ps, rot_done, ix_ps, relu_done, ix_acc = (sem(n) for n in ("rot_ps", "rot_done", "ix_ps", "relu_done", "ix_acc"))
        bias_ready, gates_open = sem("bias_ready"), sem("gates_open")
        b_z, b_zm, b_abs, b_ln, b_sp, b_c, b_cm, b_att = (sem(n) for n in (
            "b_scores_ps", "b_masked", "b_abs", "b_ln", "b_softplus", "b_sum_ps", "b_sum_masked", "b_att"))
        up_ps, up_a, m_sum, m_hi, m_lo = (sem(n) for n in ("up_ps", "up_used", "merged", "merged_hi", "merged_lo"))
        sqy, y_res = sem("y_squares"), sem("y_residual")

        n_of = {name: n for n, (_, name) in enumerate(TILES)}
        s_idx, d_idx = {}, {}
        for kind, name in TILES:
            (s_idx if kind == "s" else d_idx)[name] = len(s_idx) if kind == "s" else len(d_idx)
        s_name = {v: k for k, v in s_idx.items()}
        NSPLIT = len(s_idx)
        FF1_LOOP, FF2_LOOP, LOOPED, TURNS = s_idx["gate2"], s_idx["fa2"], 24, 4
        ff1_tiles, ff2_tiles = range(FF1_LOOP, FF1_LOOP + LOOPED), range(FF2_LOOP, FF2_LOOP + LOOPED)

        def tile_width(name):
            return {"g": DC * G_COLS, "idx": DC * IDX_COLS}.get(name, TW)

        def raw_of(name):
            return raw[:, n_of[name] % RAW, 0:tile_width(name)]

        def landed(eng, name):
            n = n_of[name]
            eng.wait_ge(s_raw[n % RAW], 16 * (n // RAW + 1))

        def hi_of(name):
            return w_hi[:, s_idx[name] % RING, 0:tile_width(name)]

        def lo_of(name):
            return w_lo[:, s_idx[name] % RING, 0:tile_width(name)]

        block = ctx.enter_context(nc.Block())

        @block.sync
        def _(sp):
            for m in range(2):
                sp.dma_start(x[:, m, :], x_in[m * P:(m + 1) * P, :]).then_inc(s_x, 16)
            sp.dma_start(const[:, :], const_in).then_inc(s_const, 16)
            sp.dma_start(raw[0:NA_ROWS, RAW - 1, 0:P], rows_a).then_inc(s_rows, 16)
            sp.dma_start(raw[0:NB_ROWS, RAW - 1, P:2 * P], rows_b).then_inc(s_rows, 16)

            def load(name):
                n = n_of[name]
                if n >= RAW:
                    kind, old = TILES[n - RAW]
                    if kind == "s":
                        sp.wait_ge(w_ready, s_idx[old] + 1)
                    else:
                        sp.wait_ge(direct_done, d_idx[old] + 1)
                if n == RAW - 1:
                    sp.wait_ge(vec_ps, 1)
                src = {"g": w_g, "idx": w_idx}.get(name)
                if src is None:
                    src = wts[n - (n > n_of["g"]) - (n > n_of["idx"]), :, :]
                sp.dma_start(raw_of(name), src).then_inc(s_raw[n % RAW], 16)

            def load_loop(first):
                n0, s0 = n_of[s_name[first]], first
                w0 = n0 - (n0 > n_of["g"]) - (n0 > n_of["idx"])
                with sp.Fori(0, TURNS) as i:
                    for j in range(TURN):
                        sp.wait_ge(w_ready, i * TURN + (s0 + j - RAW + 1))
                        src = wts[bass.ds(i * TURN + (w0 + j), 1), :, :].rearrange("a p w -> (a p) w")
                        sp.dma_start(raw[:, (n0 + j) % RAW, :], src).then_inc(s_raw[(n0 + j) % RAW], 16)

            for kind, name in TILES:
                if kind == "s" and s_idx[name] in ff1_tiles:
                    if s_idx[name] == FF1_LOOP:
                        load_loop(FF1_LOOP)
                elif kind == "s" and s_idx[name] in ff2_tiles:
                    if s_idx[name] == FF2_LOOP:
                        load_loop(FF2_LOOP)
                else:
                    load(name)
                if name == "u":
                    sp.dma_start(shared[:, :], shared_1).then_inc(s_shared, 16)
                    sp.dma_start(w2.rearrange("p a f d -> p (a f d)"), cmp_w2).then_inc(s_w2, 16)
                if name == "down0":
                    sp.wait_ge(x_new, 4)
                    sp.dma_start(shared[:, :], shared_2).then_inc(s_shared, 16)
            sp.wait_ge(y_res, 8)
            for m in range(2):
                sp.dma_start(out[m * P:(m + 1) * P, :], x[:, m, :]).then_inc(s_out, 16)
            sp.wait_ge(s_out, 32)

        @block.gpsimd
        def _(pool):
            nc.gpsimd.memset(ypad[:, :, 0:CONV_W - 1], 0.0).then_inc(zeroed, 1)
            nc.gpsimd.memset(vblk, 0.0).then_inc(zeroed, 1)
            for i in range(2):
                nc.gpsimd.memset(hcmp[i], 0.0).then_inc(zeroed, 1)
            nc.gpsimd.memset(pcmp, 0.0).then_inc(zeroed, 1)
            pool.wait_ge(s_shared, 16)
            for h, s in enumerate(slopes()):
                nc.gpsimd.tensor_scalar(alibi[:, T * h:T * (h + 1)], shared[:, 0:T], s, None, ALU.mult).then_inc(alibi_ready, 1)
            pool.wait_ge(vec_ready, 2)
            pool.wait_ge(zeroed, 5)
            pool.wait_ge(alibi_ready, NQ)
            copies = 0
            for i, (src, name) in enumerate(((KC, "kc"), (VC, "vc"))):
                pool.wait_ge(z_evac, s_idx[name] + 1)
                for g in range(NKV):
                    view = zt(src)[(g % 2) * HD:(g % 2 + 1) * HD, g // 2, :].rearrange("p (c j l) -> p l j c", c=16, j=8)
                    for l in range(2):
                        if copies:
                            pool.wait_ge(kr_ready, copies)
                        copies += 1
                        nc.gpsimd.tensor_copy(kr[i][l * HD:(l + 1) * HD, :, g * 16:(g + 1) * 16], view[:, l]).then_inc(kr_ready, 1)
                for half in range(2):
                    a = 2 * CONV_W + 16 * i + 8 * half
                    pool.wait_ge(kr_ready, copies)
                    copies += 1
                    nc.gpsimd.tensor_copy(kr[i][:, :, 64 + half:65 + half],
                                          vec_b[:, a:a + 8].rearrange("p (j o) -> p j o", o=1)).then_inc(kr_ready, 1)
            pool.wait_ge(s_sb, 4 * NQ)
            nc.gpsimd.memset(mod_part[:, :], 0.0).then_inc(mod_zeroed, 1)

        @block.tensor
        def _(pe):
            def mm3(o, lh, ll, rh, rl, start, stop):
                nc.tensor.matmul(o, lh, rh, start=start, stop=False)
                nc.tensor.matmul(o, lh, rl, start=False, stop=False)
                return nc.tensor.matmul(o, ll, rh, start=False, stop=stop)

            def w3(slot, k, n=TW):
                return (w_hi[:, slot, 0:n].rearrange("p (k c) -> p k c", k=k), w_lo[:, slot, 0:n].rearrange("p (k c) -> p k c", k=k))

            def feature_tile(slot, bank, hi, lo):
                wh, wl = w3(slot, DC)
                for c in range(2):
                    cs = slice(c * P, (c + 1) * P)
                    for k in range(DC):
                        i = mm3(ps[:, bank, c * T:(c + 1) * T], wh[:, k, cs], wl[:, k, cs], hi[:, k, :], lo[:, k, :],
                                k == 0, k == DC - 1)
                return i

            def token_tile(slot, bank, hi, lo, a, n, cols):
                wh, wl = w3(slot, DC, DC * cols)
                for m in range(2):
                    ms = slice(m * P, (m + 1) * P)
                    for k in range(DC):
                        i = mm3(ps[:, bank, m * T:m * T + n], hi[:, k, ms], lo[:, k, ms], wh[:, k, a:a + n], wl[:, k, a:a + n],
                                k == 0, k == DC - 1)
                return i

            def acc_tile(slot, hi, lo, k0, first, last):
                wh, wl = w3(slot, 2)
                for kk in range(2):
                    for m in range(2):
                        ms = slice(m * P, (m + 1) * P)
                        for n in range(2):
                            ns = slice(n * 512, (n + 1) * 512)
                            i = mm3(ps[:, 2 * m + n, :], hi[:, k0 + kk, ms], lo[:, k0 + kk, ms], wh[:, kk, ns], wl[:, kk, ns],
                                    first and kk == 0, last and kk == 1)
                return i

            def norm_turn(t):
                pe.wait_ge(xn_ready, 2 * (t + 1))
                for k in range(DC):
                    for m in range(2):
                        o = ps[:, 4 + k // 2, (k % 2) * T + m * P:(k % 2) * T + (m + 1) * P]
                        i = nc.tensor.transpose(o, xn[:, m, k * P:(k + 1) * P], ident)
                    if k % 2:
                        i.then_inc(xT_ready, 1)

            def spread(t):
                pe.wait_ge(diag_ready, t + 1)
                for n in range(2):
                    i = nc.tensor.matmul(ps[:, 4 + n, :], cst("ones"), diag[:, 4 * n:4 * n + 4, :].rearrange("p k n -> p (k n)"),
                                         start=True, stop=True)
                i.then_inc(row_ps, 1)

            pe.wait_ge(s_const, 16)
            pe.wait_ge(s_rows, 32)
            nc.tensor.transpose(ps[:, 0, 0:NA_ROWS], raw[0:NA_ROWS, RAW - 1, 0:P], ident[0:NA_ROWS, 0:NA_ROWS])
            nc.tensor.transpose(ps[:, 0, P:P + NB_ROWS], raw[0:NB_ROWS, RAW - 1, P:2 * P], ident[0:NB_ROWS, 0:NB_ROWS]).then_inc(vec_ps, 1)
            norm_turn(0)

            pe.wait_ge(h_ready, DC)
            pe.wait_ge(vec_ready, 2)

            def project_1(s):
                pe.wait_ge(w_ready, s + 1)
                if s >= 3:
                    pe.wait_ge(z_evac, s - 2)
                return s % RING, s % 3
            for s in range(3):
                feature_tile(*project_1(s), h_hi, h_lo).then_inc(pe_tile, 1)
            with pe.Fori(0, 2) as i:
                for j in range(3):
                    pe.wait_ge(w_ready, i * 3 + (3 + j + 1))
                    pe.wait_ge(z_evac, i * 3 + (3 + j - 2))
                    feature_tile(j, j, h_hi, h_lo).then_inc(pe_tile, 1)
            def compress(a):
                pe.wait_ge(kr_ready, 10 * (a + 1))
                for half in range(2):
                    name = f"cmp{2 * a + half}"
                    landed(pe, name)
                    wc = raw_of(name).rearrange("p (j h) -> p j h", j=8)
                    for f in range(2):
                        for j in range(8):
                            i = nc.tensor.matmul(ps[:, 4 + a, (2 * half + f) * 66:(2 * half + f + 1) * 66], wc[:, j, f * P:(f + 1) * P],
                                                 kr[a][:, j, :], start=(j == 0), stop=(j == 7))
                    i.then_inc(direct_done, 1)

            compress(0)
            pe.wait_ge(conv_ready, 1)
            for c in range(2):
                i = nc.tensor.matmul(ps[:, 3, 0:T], cst("mean"), conv[:, c, :], start=(c == 0), stop=(c == 1))
            i.then_inc(conv_mean, 1)
            compress(1)
            pe.wait_ge(convd_ready, 1)
            for c in range(2):
                i = nc.tensor.matmul(ps[:, 3, T:2 * T], cst("mean"), lnq[:, c, :], start=(c == 0), stop=(c == 1))
            i.then_inc(conv_var, 1)
            slot, bank = project_1(s_idx["g"])
            token_tile(slot, bank, h_hi, h_lo, 0, G_COLS, G_COLS).then_inc(pe_tile, 1)
            pe.wait_ge(s_w2, 16)
            pe.wait_ge(cmp_h, 2)
            for f in range(2):
                i = nc.tensor.matmul(ps[0:HD, 6, 0:P], w2[:, 0, f, :], hcmp[0][:, f, :], start=(f == 0), stop=(f == 1))
            i.then_inc(cmp2_ps, 1)
            pe.wait_ge(cmp_h, 4)
            for f in range(2):
                i = nc.tensor.matmul(ps[:, 7, 0:HD], hcmp[1][:, f, :], w2[:, 1, f, :], start=(f == 0), stop=(f == 1))
            i.then_inc(cmp2_ps, 1)
            slot, bank = project_1(s_idx["vs"])
            token_tile(slot, bank, h_hi, h_lo, 0, T, T).then_inc(pe_tile, 1)

            def head_at(h):
                pair, in_pair = h // 6, h % 6
                return 3 * pair + in_pair % 3, HD * (in_pair // 3), pair

            def qT(h):
                j, b, _ = head_at(h)
                return z[b:b + HD, Q0 + j // 2, (j % 2) * T:(j % 2 + 1) * T]

            pe.wait_ge(cmp2_sb, 2)
            for m in range(2):
                for h in range(NQ):
                    _, b, _ = head_at(h)
                    g = h // 3
                    at = ((2 * m + h // 6) * 3 + h % 3) * CMP_SLOT
                    i = nc.tensor.matmul(ps[:, 4 + b // HD, at:at + CMP_SLOT], qT(h)[:, m * P:(m + 1) * P],
                                         kcmp[b:b + HD, g * CMP_SLOT:(g + 1) * CMP_SLOT], start=True, stop=True)
            i.then_inc(sc_ps, 1)
            slot, bank = project_1(s_idx["vw"])
            token_tile(slot, bank, h_hi, h_lo, 0, T, T).then_inc(pe_tile, 1)

            order = [6 * p + r + 3 * e for p in range(2) for r in range(3) for e in range(2)]

            def scores(n):
                h = order[n]
                _, b, pair = head_at(h)
                for br, k_tile in enumerate((KS, KW)):
                    bank = 2 * (n % 2) + br
                    kT = z[b:b + HD, k_tile, pair * T:(pair + 1) * T]
                    nc.tensor.matmul(ps[:, bank, 0:P], qT(h)[:, 0:P], kT[:, 0:P], start=True, stop=True)
                    i = nc.tensor.matmul(ps[:, bank, P:P + T], qT(h)[:, P:T], kT, start=True, stop=True)
                i.then_inc(s_ps, 1)

            pe.wait_ge(z_evac, s_idx["vw"])
            scores(0)
            pe.wait_ge(z_evac, s_idx["vw"] + 1)
            pe.wait_ge(lnv_ready, 1)
            scores(1)
            pe.wait_ge(pc_ready, 1)
            for c in range(3):
                for m in range(2):
                    i = nc.tensor.transpose(ps[:, 4 + c // 2, (c % 2) * T + m * P:(c % 2) * T + (m + 1) * P],
                                            pcmp[:, m, 4 * c:4 * c + 4, :].rearrange("p h n -> p (h n)"), ident)
            i.then_inc(pcT_ps, 1)

            pe.wait_ge(vblk_ready, NQ)
            pe.wait_ge(pcT_ready, 3)
            for n in range(NQ):
                h = order[n]
                j, b, _ = head_at(h)
                g = h // 3
                for br in range(2):
                    pe.wait_ge(p_ready, 4 * n + 2 * (br + 1))
                    if n >= 1:
                        pe.wait_ge((pT_ready, pTw_ready)[br], n)
                    for c in range(3):
                        i = nc.tensor.transpose(ps[:, 4 + br, c * P:(c + 1) * P],
                                                soft[:, (2 * (n % 2) + br) * 384 + c * P:(2 * (n % 2) + br) * 384 + (c + 1) * P], ident)
                    i.then_inc(pT_ps, 1)
                if n + 2 < NQ:
                    pe.wait_ge(s_sb, 4 * (n + 1))
                    scores(n + 2)
                if n % 2 == 0 and n >= 2:
                    pe.wait_ge(o_lo, n // 2)
                nc.tensor.matmul(ps[b:b + HD, 6, 0:T], vblk[:, h, :], pcT[:, h // 4, :], start=True, stop=False)
                for br, v_tile in enumerate((VS, VW)):
                    pe.wait_ge((pT_ready, pTw_ready)[br], n + 1)
                    for kt in range(2):
                        lhs = z[:, v_tile, kt * T + g * HD:kt * T + (g + 1) * HD]
                        pt = turned[:, br * 384:br * 384 + T] if kt == 0 else turned[:, br * 384 + T:(br + 1) * 384]
                        i = nc.tensor.matmul(ps[b:b + HD, 6, kt * P:T], lhs, pt, start=False, stop=(br == 1 and kt == 1))
                i.then_inc(o_ps, 1)

            pe.wait_ge(clo_ready, 2)
            for i4 in range(4):
                s = s_idx[f"out{i4}"]
                pe.wait_ge(w_ready, s + 1)
                if i4 == 0:
                    pe.wait_ge(s_sb, 4 * NQ)
                if i4 >= 1:
                    pe.wait_ge(o_lo, 2 * i4)
                i = acc_tile(s % RING, mix_hi, mix_lo, 2 * i4, i4 == 0, i4 == 3)
                i.then_inc(pe_tile, 1)
            norm_turn(1)

            pe.wait_ge(h_ready, 2 * DC)

            def down(slot, buf, first, last):
                return acc_tile(slot, hid_hi[buf], hid_lo[buf], 0, first, last)

            def ff1_step(st, i=0, first=False):
                s0 = s_idx[f"gate{st}"]
                for c in range(2):
                    pe.wait_ge(w_ready, i * 6 + (s0 + c + 1))
                    if c == 0 and st >= 2:
                        pe.wait_ge(hid_done, i * 2 + (st - 1))
                    feature_tile((s0 + c) % RING, 4 + 2 * (st % 2) + c, h_hi, h_lo).then_inc(pe_tile, 1)
                if st >= 1:
                    pe.wait_ge(w_ready, i * 6 + (s0 + 3))
                    pe.wait_ge(hidlo_done, i * 2 + st)
                    down((s0 + 2) % RING, (st - 1) % 2, first, False).then_inc(pe_tile, 1)

            ff1_step(0)
            pe.wait_ge(x_new, 4)
            ff1_step(1, first=True)
            with pe.Fori(0, TURNS) as i:
                ff1_step(2, i)
                ff1_step(3, i)
            ff1_step(10)
            s = s_idx["down10"]
            pe.wait_ge(w_ready, s + 1)
            pe.wait_ge(hidlo_done, FF1_STEPS)
            down(s % RING, 0, False, True).then_inc(pe_tile, 1)
            spread(0)

            def mod_columns(src, first, n):
                for c in range(n):
                    i = nc.tensor.matmul(ps[:, 6, first + c:first + c + 1], src[:, c * P:(c + 1) * P], cst("ones")[:, 0:1],
                                         start=True, stop=True)
                i.then_inc(mod_ps, 1)

            pe.wait_ge(ada_used, 1 + 16)
            pe.wait_ge(hidlo_done, FF1_STEPS)
            mod_columns(mod_part, 0, 32)
            norm_turn(2)

            pe.wait_ge(h_ready, 3 * DC)

            def evac_no(s):
                return 12 + s - s_idx["idx"]

            def project_2(name):
                s = s_idx[name]
                pe.wait_ge(w_ready, s + 1)
                pe.wait_ge(z_evac, evac_no(s) - 2)
                return s % RING, s % 3

            slot, bank = project_2("idx")
            wh, wl = w3(slot, DC, DC * IDX_COLS)
            for k in range(DC):
                mm3(ps[:, bank, 0:T], wh[:, k, 0:P], wl[:, k, 0:P], h_hi[:, k, :], h_lo[:, k, :], k == 0, k == DC - 1)
            for m in range(2):
                ms = slice(m * P, (m + 1) * P)
                for k in range(DC):
                    i = mm3(ps[:, bank, T + m * 8:T + (m + 1) * 8], h_hi[:, k, ms], h_lo[:, k, ms], wh[:, k, P:P + 8], wl[:, k, P:P + 8],
                            k == 0, k == DC - 1)
            i.then_inc(pe_tile, 1)

            def feature_2(name):
                feature_tile(*project_2(name), h_hi, h_lo).then_inc(pe_tile, 1)

            rots = [0]

            def swap(src, n, name):
                pe.wait_ge(z_evac, evac_no(s_idx[name]) + 1)
                if rots[0]:
                    pe.wait_ge(rot_done, rots[0])
                nc.tensor.matmul(ps[:, 3, 0:n], shared[:, 512:640], src, start=True, stop=True).then_inc(rot_ps, 1)
                rots[0] += 1

            def index_scores(h):
                b, j = HD * (h % 2), h // 2
                if h == 0:
                    pe.wait_ge(rot_done, 3)
                if h >= 4:
                    pe.wait_ge(relu_done, h - 3)
                q = z[b:b + HD, QI + j // 2, (j % 2) * T:(j % 2 + 1) * T]
                nc.tensor.matmul(ps[:, 4 + h % 4, 0:P], q[:, 0:P], kiT[b:b + HD, 0:P], start=True, stop=True)
                nc.tensor.matmul(ps[:, 4 + h % 4, P:P + T], q[:, P:T], kiT[b:b + HD, :], start=True, stop=True).then_inc(ix_ps, 1)

            pe.wait_ge(s_shared, 32)
            feature_2("qi0")
            feature_2("qi1")
            swap(kiT, T, "idx")
            feature_2("qa0")
            swap(z[:, QI, :], 512, "qi0")
            swap(z[:, QI + 1, :], 512, "qi1")
            feature_2("qa1")
            for h in range(4):
                index_scores(h)
            swap(z[:, QA, :], 512, "qa0")
            feature_2("ka0")
            for h in range(4, 8):
                index_scores(h)
            swap(z[:, QA + 1, :], 512, "qa1")
            feature_2("ka1")
            swap(z[:, KA, :], 512, "ka0")
            feature_2("qb0")
            swap(z[:, KA + 1, :], 512, "ka1")
            for name in ("qb1", "kb0", "kb1"):
                feature_2(name)
            for name in ("va0", "va1", "vb0", "vb1"):
                token_tile(*project_2(name), h_hi, h_lo, 0, T, T).then_inc(pe_tile, 1)
            def gate_half(h, c):
                s = s_idx[f"sg{h}"]
                if c == 0:
                    pe.wait_ge(w_ready, s + 1)
                    pe.wait_ge(z_evac, evac_no(s))
                wh, wl = w3(s % RING, DC)
                cs = slice(c * P, (c + 1) * P)
                for k in range(DC):
                    i = mm3(ps[:, 7, c * T:(c + 1) * T], wh[:, k, cs], wl[:, k, cs], h_hi[:, k, :], h_lo[:, k, :], k == 0, k == DC - 1)
                if c:
                    i.then_inc(pe_tile, 1)

            def zhead(base, h):
                b, j = HD * (h % 2), h // 2
                return z[b:b + HD, base + j // 2, (j % 2) * T:(j % 2 + 1) * T]

            def scores_a(h):
                if h == 0:
                    pe.wait_ge(z_evac, evac_no(s_idx["vb1"]) + 1)
                if h >= 2:
                    pe.wait_ge(s_sb, 4 * NQ + 2 * (h - 1))
                q, k = zhead(QA, h), zhead(KA, h)
                nc.tensor.matmul(ps[:, h % 2, 0:P], q[:, 0:P], k[:, 0:P], start=True, stop=True)
                nc.tensor.matmul(ps[:, h % 2, P:P + T], q[:, P:T], k, start=True, stop=True).then_inc(s_ps, 1)

            def scores_b(h):
                if h >= 2:
                    pe.wait_ge(b_zm, h - 1)
                q, k = zhead(QB, h), zhead(KB, h)
                nc.tensor.matmul(ps[:, 3 + h % 2, 0:T], k[:, 0:P], q, start=True, stop=True)
                nc.tensor.matmul(ps[:, 3 + h % 2, T:T + P], k[:, P:T], q[:, P:T], start=True, stop=True).then_inc(b_z, 1)

            pe.wait_ge(rot_done, 7)
            for h in range(2):
                scores_a(h)
                scores_b(h)
            for h in range(NB_HEADS):
                b, j = HD * (h % 2), h // 2
                pe.wait_ge(p_ready, 4 * NQ + 2 * (h + 1))
                if h >= 1:
                    pe.wait_ge(pT_ready, NQ + h)
                for c in range(3):
                    i = nc.tensor.transpose(ps[:, 2, c * P:(c + 1) * P], sA[h % 2][:, c * P:(c + 1) * P], ident)
                i.then_inc(pT_ps, 1)
                pe.wait_ge(b_sp, h + 1)
                if h >= 1:
                    pe.wait_ge(b_cm, 2 * h)
                q, k = zhead(QB, h), zhead(KB, h)
                nc.tensor.matmul(ps[:, 5, 0:T], k[:, 0:P], q, start=True, stop=False)
                nc.tensor.matmul(ps[:, 5, 0:T], cst("tri"), spb[:, 0:T], start=False, stop=False)
                nc.tensor.matmul(ps[:, 5, P:T], cst("negones"), spb[:, T:T + P], start=False, stop=True)
                nc.tensor.matmul(ps[:, 5, T:T + P], k[:, P:T], q[:, P:T], start=True, stop=False)
                nc.tensor.matmul(ps[:, 5, T:T + P], cst("tri"), spb[:, T:T + P], start=False, stop=True).then_inc(b_c, 1)
                if h + 2 < NB_HEADS:
                    scores_a(h + 2)
                    scores_b(h + 2)
                gate_half(h, 0)
                gate_half(h, 1)
                if h % 2 == 0 and h >= 2:
                    pe.wait_ge(o_lo, 6 + h // 2)
                va = z[:, VA + h // 4, :].rearrange("p (m d) -> p m d", m=2)[:, :, (h % 4) * HD:(h % 4 + 1) * HD]
                vb = z[:, VB + h // 4, :].rearrange("p (m d) -> p m d", m=2)[:, :, (h % 4) * HD:(h % 4 + 1) * HD]
                pe.wait_ge(pT_ready, NQ + h + 1)
                nc.tensor.matmul(ps[b:b + HD, 6, 0:T], va[:, 0, :], pTA[:, 0:T], start=True, stop=False)
                nc.tensor.matmul(ps[b:b + HD, 6, P:T], va[:, 1, :], pTA[:, T:T + P], start=False, stop=True).then_inc(o_ps, 1)
                pe.wait_ge(b_att, h + 1)
                nc.tensor.matmul(ps[b:b + HD, 6, T:2 * T], vb[:, 0, :], attb[:, 0:T], start=True, stop=False)
                nc.tensor.matmul(ps[b:b + HD, 6, T + P:2 * T], vb[:, 1, :], attb[:, T:T + P], start=False, stop=True).then_inc(o_ps, 1)

            for u, name in enumerate(("upa0", "upb0", "upa1", "upb1")):
                s = s_idx[name]
                pe.wait_ge(w_ready, s + 1)
                pe.wait_ge(o_lo, 10)
                wh, wl = w3(s % RING, 4)
                for c in range(4):
                    for k in range(4):
                        kk = 4 * (u % 2) + k
                        cs = slice(c * P, (c + 1) * P)
                        i = mm3(ps[:, 2 * u + c // 2, (c % 2) * T:(c % 2 + 1) * T], wh[:, k, cs], wl[:, k, cs], mix_hi[:, kk, :], mix_lo[:, kk, :],
                                k == 0, k == 3)
                i.then_inc(pe_tile, 1)
            for i4 in range(4):
                s = s_idx[f"o2{i4}"]
                pe.wait_ge(w_ready, s + 1)
                pe.wait_ge(m_lo, i4 // 2 + 1)
                acc_tile(s % RING, h_hi, h_lo, 2 * i4, i4 == 0, i4 == 3).then_inc(pe_tile, 1)
            pe.wait_ge(m_sum, 2)
            pe.wait_ge(ada_used, 1 + 24)
            mod_columns(mod_tail, 32, 16)
            spread(1)
            pe.wait_ge(row_ready, 2)
            norm_turn(3)

            pe.wait_ge(h_ready, 4 * DC)

            def ff2_step(st, i=0, first=False):
                s0 = s_idx[f"fa{st}"]
                pe.wait_ge(w_ready, i * 6 + (s0 + 1))
                if st >= 3:
                    pe.wait_ge(relu2_done, i * 3 + (st - 2))
                feature_tile(s0 % RING, 4 + st % 3, h_hi, h_lo).then_inc(pe_tile, 1)
                if st >= 1:
                    pe.wait_ge(w_ready, i * 6 + (s0 + 2))
                    pe.wait_ge(hid2lo_done, i * 3 + st)
                    down((s0 + 1) % RING, (st - 1) % 3, first, False).then_inc(pe_tile, 1)

            ff2_step(0)
            ff2_step(1, first=True)
            ff2_step(2)
            ff2_step(3)
            ff2_step(4)
            with pe.Fori(1, TURNS) as i:
                ff2_step(2, i)
                ff2_step(3, i)
                ff2_step(4, i)
            ff2_step(14)
            ff2_step(15)
            s = s_idx["fb15"]
            pe.wait_ge(w_ready, s + 1)
            pe.wait_ge(hid2lo_done, FF2_STEPS)
            down(s % RING, 15 % 3, False, True).then_inc(pe_tile, 1)
            spread(2)

        @block.scalar
        def _(act):
            def load_ada(t, i=0):
                act.wait_ge(ada_used, i * 4 + max(t, 1))
                src = w_ada[bass.ds(i * 4 + t, 1), :, :].rearrange("a p w -> (a p) w")
                act.dma_start(ada[:, t % 2, :], src).then_inc(s_ada[t % 2], 16)

            def split(s, name, i=0):
                n = n_of[name]
                act.wait_ge(s_raw[n % RAW], i * (16 * TURN // RAW) + 16 * (n // RAW + 1))
                if s >= RING:
                    act.wait_ge(pe_tile, i * 6 + (s - RING + 1))
                w = tile_width(name)
                nc.scalar.copy(w_hi[:, s % RING, 0:w], raw[:, n % RAW, 0:w]).then_inc(hi_ready, 1)

            def after(s, i=0):
                if s + RING < NSPLIT:
                    split(s + RING, s_name[s + RING], i)

            steps = [0]

            def link(ins):
                steps[0] += 1
                ins.then_inc(astep, 1)
                act.wait_ge(astep, steps[0])

            def root(t):
                act.wait_ge(ms_ready, t + 1)
                nc.scalar.activation(sqv, msum, ACT.Sqrt).then_inc(sq_ready, 1)

            def norm_hi(t, scale, bias=None):
                for k in range(DC):
                    act.wait_ge(xT_ready, 4 * t + k // 2 + 1)
                    src = ps[:, 4 + k // 2, (k % 2) * T:(k % 2 + 1) * T]
                    nc.scalar.activation(h_hi[:, k, :], src, ACT.Identity, scale=scale(k),
                                         bias=bias(k) if bias else 0.0).then_inc(hhi_ready, 1)

            for s in range(RING):
                split(s, s_name[s])
            root(0)
            nc.scalar.preload_act_table_set("sigmoid_and_others")
            act.wait_ge(vec_ready, 1)
            norm_hi(0, lambda k: col("attn_norm", k))

            def copy_out(s):
                act.wait_ge(pe_tile, s + 1)
                bank, name = s % 3, s_name[s]
                if name == "g":
                    nc.scalar.activation(gates, ps[:, bank, :].rearrange("p (m c) -> p m c", m=2)[:, :, 0:G_COLS].rearrange(
                        "p m (h b) -> p m h b", b=3), ACT.Sigmoid).then_inc(z_evac, 1)
                elif name == "v":
                    nc.scalar.activation(z[:, V_, :], ps[:, bank, :], ACT.Sigmoid).then_inc(z_evac, 1)
                elif name[0] == "q":
                    nc.scalar.mul(z[:, z_at[name], :], ps[:, bank, :], HD ** -0.5).then_inc(z_evac, 1)
                else:
                    nc.scalar.copy(z[:, z_at[name], :], ps[:, bank, :]).then_inc(z_evac, 1)

            for s in range(9):
                copy_out(s)
                if s < 8:
                    after(s)
            act.wait_ge(direct_done, 2)
            nc.scalar.copy(xs_cmp(0), ps[:, 4, 0:264]).then_inc(cmp_sb, 1)
            after(8)
            act.wait_ge(direct_done, 4)
            nc.scalar.copy(xs_cmp(1), ps[:, 5, 0:264]).then_inc(cmp_sb, 1)
            for a in range(2):
                act.wait_ge(cmp_sum, a + 1)
                for f in range(2):
                    dst = hcmp[a][:, f, :].rearrange("p (g n) -> p g n", g=NKV)[:, :, 0:N_CMP]
                    nc.scalar.activation(dst, cmp_hidden(a)[:, f], ACT.Silu, bias=pebias[:, 2 * a + f:2 * a + f + 1]).then_inc(cmp_h, 1)
            nc.scalar.activation(silu_c, vec[:, VEC_A["c"][0]:VEC_A["c"][0] + 8], ACT.Silu).then_inc(silu_c_ready, 1)
            copy_out(s_idx["g"])
            act.wait_ge(cmp2_ps, 1)
            for b in range(2):
                nc.scalar.copy(kcmp[b * HD:(b + 1) * HD, :].rearrange("p (g n) -> p g n", g=NKV),
                               ps[0:HD, 6, 0:P].rearrange("p (g n) -> p g n", g=NKV)[:, :, 0:CMP_SLOT]).then_inc(cmp2_sb, 1)
            act.wait_ge(lnv_ready, 1)
            nc.scalar.activation(lnv[:, 1, :], lnv[:, 0, :], ACT.Sqrt).then_inc(lnsq_ready, 1)
            after(9)
            copy_out(s_idx["vs"])
            act.wait_ge(lnn_ready, 1)
            for c in range(2):
                link(nc.scalar.activation(conv[:, c, :], lnd[:, c, :], ACT.Silu, scale=col("ln_g", c), bias=col("ln_b", c)))
                nc.scalar.copy(mix_hi[:, c, :], conv[:, c, :]).then_inc(chi_ready, 1)
            act.wait_ge(sc_sb, 1)
            nc.scalar.activation(scmp, scmp, ACT.Exp).then_inc(pc_exp, 1)
            after(10)
            copy_out(s_idx["vw"])

            def attn(n):
                act.wait_ge(s_sb, 4 * (n + 1))
                for br in range(2):
                    for m in range(2):
                        o = soft[:, (2 * (n % 2) + br) * 384 + m * P:(2 * (n % 2) + br) * 384 + P + m * T]
                        c = 2 * br + m
                        nc.scalar.activation(o, o, ACT.Exp, scale=-1.0, bias=nmax[:, n % 2, c:c + 1],
                                             accum_out=psum_p[:, n % 2, c:c + 1]).then_inc(p_exp, 1)

            attn(0)
            attn(1)
            after(11)
            for n in range(NQ):
                act.wait_ge(pT_ps, 2 * (n + 1))
                if n >= 1:
                    act.wait_ge(o_ps, n)
                nc.scalar.copy(turned[:, 384:768], ps[:, 5, 0:384]).then_inc(pTw_ready, 1)
                if n + 2 < NQ:
                    attn(n + 2)
                if n % 2:
                    j = n // 2
                    act.wait_ge(o_ps, n + 1)
                    nc.scalar.copy(mix_hi[:, 2 + j, :], ps[:, 6, 0:T]).then_inc(o_hi, 1)
            nc.scalar.preload_act_table_set("sqrt_and_others")
            for i4 in range(4):
                after(s_idx[f"out{i4}"])
            root(1)
            nc.scalar.preload_act_table_set("silu_and_others")
            norm_hi(1, lambda k: col("ffn_norm", k))

            def ff1_step(st, i=0):
                s0 = s_idx[f"gate{st}"]
                if 2 <= st <= 9:
                    load_ada(2 * (st - 2), i)
                    load_ada(2 * (st - 2) + 1, i)
                act.wait_ge(pe_tile, i * 6 + (s0 + 1))
                if st >= 2:
                    act.wait_ge(hid_done, i * 2 + (st - 1))
                nc.scalar.activation(ff_act[st % 2], ps[:, 4 + 2 * (st % 2), :], ACT.Silu).then_inc(silu_done, 1)
                after(s0, i)
                after(s0 + 1, i)
                act.wait_ge(hid_done, i * 2 + (st + 1))
                if st >= 2:
                    act.wait_ge(pe_tile, i * 6 + (s0 - 1 + 1))
                nc.scalar.copy(hid_hi[st % 2], ff_hid[st % 2].rearrange("p (c t) -> p c t", c=2)).then_inc(hidhi_done, 1)
                if st >= 1:
                    after(s0 + 2, i)

            ff1_step(0)
            ff1_step(1)
            with act.Fori(0, TURNS) as i:
                ff1_step(2, i)
                ff1_step(3, i)
            ff1_step(10)
            after(s_idx["down10"])
            nc.scalar.preload_act_table_set("sqrt_and_others")
            root(2)
            root(3)
            nc.scalar.preload_act_table_set("natural_log_exp_and_others")
            norm_hi(2, lambda k: scl[:, k:k + 1], lambda k: modT[:, k:k + 1])

            relus = [0]

            def relu_index(h):
                act.wait_ge(ix_ps, h + 1)
                if h >= 2:
                    act.wait_ge(ix_acc, 2 * (h - 1))
                nc.scalar.activation(relu_b[h % 2], ps[:, 4 + h % 4, 0:384], ACT.Relu).then_inc(relu_done, 1)

            def keep_gates(h):
                s = s_idx[f"sg{h}"]
                act.wait_ge(pe_tile, s + 1)
                dst = sgate[:, h // 4, 2 * (h % 4):2 * (h % 4) + 2, :].rearrange("p c t -> p (c t)")
                nc.scalar.copy(dst, ps[:, 7, :]).then_inc(z_evac, 1)
                after(s)

            for s in range(s_idx["idx"], s_idx["vb1"] + 1):
                name = s_name[s]
                act.wait_ge(pe_tile, s + 1)
                bank = s % 3
                if name == "idx":
                    load_ada(16)
                    load_ada(17)
                if name == "idx":
                    link(nc.scalar.copy(kiT, ps[:, bank, 0:T]))
                    nc.scalar.copy(wi_s, ps[:, bank, T:T + 16].rearrange("p (m h) -> p m h", m=2)).then_inc(z_evac, 1)
                else:
                    at = {"qi": QI, "qa": QA, "ka": KA, "qb": QB, "kb": KB, "va": VA, "vb": VB}[name[:2]] + int(name[2])
                    scale = HD ** -0.5 if name[:2] in ("qa", "qb") else 1.0
                    nc.scalar.mul(z[:, at, :], ps[:, bank, :], scale).then_inc(z_evac, 1)
                after(s)
                if s_idx["qb0"] <= s < s_idx["vb0"]:
                    load_ada(18 + s - s_idx["qb0"])
                if name in ("qa1", "ka0"):
                    for h in range(4):
                        relu_index(h + 4 * (name == "ka0"))

            def attn_a(h):
                act.wait_ge(s_sb, 4 * NQ + 2 * (h + 1))
                for m in range(2):
                    o = sA[h % 2][:, m * P:P + m * T]
                    nc.scalar.activation(o, o, ACT.Exp, scale=-1.0, bias=nmax[:, h % 2, m:m + 1], accum_out=psum_p[:, h % 2, m:m + 1]).then_inc(p_exp, 1)

            def attn_b1(h):
                act.wait_ge(b_abs, h + 1)
                link(nc.scalar.activation(eb, eb, ACT.Exp))
                nc.scalar.activation(eb, eb, ACT.Ln, bias=1.0).then_inc(b_ln, 1)

            attn_a(0)
            attn_b1(0)
            attn_a(1)
            for h in range(NB_HEADS):
                if h + 1 < NB_HEADS:
                    attn_b1(h + 1)
                act.wait_ge(b_cm, 2 * (h + 1))
                nc.scalar.activation(attb, attb, ACT.Exp).then_inc(b_att, 1)
                if h + 2 < NB_HEADS:
                    attn_a(h + 2)
                keep_gates(h)
                if h % 2:
                    j = h // 2
                    act.wait_ge(o_ps, NQ + 2 * (h + 1))
                    nc.scalar.copy(mix_hi[:, j::4, :], ps[:, 6, :].rearrange("p (e t) -> p e t", e=2)).then_inc(o_hi, 1)
            act.wait_ge(z_evac, 12 + s_idx["sg7"] - s_idx["idx"] + 1)
            for u in range(2):
                g4 = sgate[:, :, 4 * u:4 * u + 4, :]
                nc.scalar.activation(g4, g4, ACT.Sigmoid).then_inc(gates_open, 1)
            nc.scalar.preload_act_table_set("sqrt_and_others")
            for u in range(2):
                after(s_idx[f"upa{u}"])
                after(s_idx[f"upb{u}"])
                act.wait_ge(m_sum, u + 1)
                nc.scalar.copy(h_hi[:, 4 * u:4 * u + 4, :], merged(u)).then_inc(m_hi, 1)
            for i4 in range(4):
                after(s_idx[f"o2{i4}"])
            act.wait_ge(pe_tile, s_idx["o23"] + 1)
            for q in range(4):
                nc.scalar.activation(xn_scratch[:, 0:512], ps[:, q, :], ACT.Square, accum_out=part[:, q:q + 1]).then_inc(sqy, 1)
                act.wait_ge(sqy, q + 1)
            root(4)
            root(5)
            norm_hi(3, lambda k: scl[:, k:k + 1], lambda k: modT[:, 24 + k:25 + k])

            def ff2_step(st, i=0):
                s0 = s_idx[f"fa{st}"]
                act.wait_ge(pe_tile, i * 6 + (s0 + 1))
                if st >= 3:
                    act.wait_ge(hid2_done, i * 3 + (st - 2))
                nc.scalar.activation(ff_act[st % 3], ps[:, 4 + st % 3, :], ACT.Relu).then_inc(relu2_done, 1)
                after(s0, i)
                act.wait_ge(hid2_done, i * 3 + (st + 1))
                if st >= 3:
                    act.wait_ge(pe_tile, i * 6 + (s0 - 4 + 1))
                nc.scalar.copy(hid_hi[st % 3], ff_hid[st % 3].rearrange("p (c t) -> p c t", c=2)).then_inc(hid2hi_done, 1)
                if st >= 1:
                    after(s0 + 1, i)

            for st in range(5):
                ff2_step(st)
            with act.Fori(1, TURNS) as i:
                ff2_step(2, i)
                ff2_step(3, i)
                ff2_step(4, i)
            ff2_step(14)
            ff2_step(15)
            act.wait_ge(pe_tile, s_idx["fb15"] + 1)
            for q in range(4):
                nc.scalar.activation(xn_scratch[:, 0:512], ps[:, q, :], ACT.Square, accum_out=part[:, q:q + 1]).then_inc(sqy, 1)
                act.wait_ge(sqy, 4 + q + 1)
            root(6)

        @block.vector
        def _(dve):
            V = nc.vector
            steps = [0]

            def link(ins):
                steps[0] += 1
                ins.then_inc(dstep, 1)
                dve.wait_ge(dstep, steps[0])

            def split(s, name, i=0):
                dve.wait_ge(hi_ready, i * 6 + (s + 1))
                w = tile_width(name)
                V.tensor_tensor(w_lo[:, s % RING, 0:w], raw[:, n_of[name] % RAW, 0:w],
                                w_hi[:, s % RING, 0:w].bitcast(F32), ALU.subtract).then_inc(w_ready, 1)

            def after(s, i=0):
                if s + RING < NSPLIT:
                    split(s + RING, s_name[s + RING], i)

            roots = [0]

            def rstd():
                V.tensor_scalar(msum, msum, EPS, None, ALU.add).then_inc(ms_ready, 1)
                roots[0] += 1
                dve.wait_ge(sq_ready, roots[0])
                link(V.reciprocal(rst, sqv))
                newton(rst, msum, nwt)

            def newton(r, v, t):
                link(V.tensor_tensor(t, r, r, ALU.mult))
                link(V.tensor_tensor(t, t, v, ALU.mult))
                link(V.tensor_scalar(t, t, -0.5, 1.5, ALU.mult, ALU.add))
                link(V.tensor_tensor(r, r, t, ALU.mult))

            def norm_x():
                for m in range(2):
                    link(V.tensor_tensor_reduce(xn_scratch, x[:, m, :], x[:, m, :], 1.0 / D, 0.0, ALU.mult, ALU.add, msum[:, m:m + 1]))
                rstd()

            def norm_scale():
                for m in range(2):
                    V.tensor_scalar(xn[:, m, :], x[:, m, :], rst[:, m:m + 1], None, ALU.mult).then_inc(xn_ready, 1)

            def norm_lo(t, scale, bias=None):
                for k in range(DC):
                    src = ps[:, 4 + k // 2, (k % 2) * T:(k % 2 + 1) * T]
                    dve.wait_ge(hhi_ready, 8 * t + 2 * (k // 2) + 2)
                    hi = h_hi[:, k, :].bitcast(F32)
                    if bias is None:
                        V.scalar_tensor_tensor(h_lo[:, k, :], src, scale(k), hi, ALU.mult, ALU.subtract).then_inc(h_ready, 1)
                    else:
                        link(V.tensor_scalar(htmp[:, k % 2, :], src, scale(k), bias(k), ALU.mult, ALU.add))
                        V.tensor_tensor(h_lo[:, k, :], htmp[:, k % 2, :], hi, ALU.subtract).then_inc(h_ready, 1)

            def diagonals(v):
                for k in range(DC):
                    i = V.tensor_scalar(diag[:, k, :], ident, v[:, k:k + 1], None, ALU.mult)
                i.then_inc(diag_ready, 1)

            def row(t):
                dve.wait_ge(row_ps, t + 1)
                V.tensor_copy(rowb, ps[:, 4:6, :].rearrange("p a n -> p (a n)")).then_inc(row_ready, 1)
                dve.wait_ge(row_ready, t + 1)

            dve.wait_ge(s_x, 32)
            norm_x()
            norm_scale()
            for s in range(RING):
                split(s, s_name[s])
            dve.wait_ge(vec_ps, 1)
            V.tensor_copy(vec[:, :], ps[:, 0, 0:NA_ROWS]).then_inc(vec_ready, 1)
            V.tensor_copy(vec_b[:, :], ps[:, 0, P:P + NB_ROWS]).then_inc(vec_ready, 1)
            dve.wait_ge(vec_ready, 2)
            norm_lo(0, lambda k: col("attn_norm", k))

            taps = [(w, c) for w in range(CONV_W) for c in range(2)]
            base = steps[0]
            def tap(w, c):
                src, wcol = ypad[:, c, w:w + T], vec_b[:, 2 * w + c:2 * w + c + 1]
                if w == 0:
                    i = V.tensor_scalar(conv[:, c, :], src, wcol, col("conv_b", c), ALU.mult, ALU.add)
                else:
                    dve.wait_ge(dstep, steps[0] - 1)
                    i = V.scalar_tensor_tensor(conv[:, c, :], src, wcol, conv[:, c, :], ALU.mult, ALU.add)
                if (w, c) == taps[-1]:
                    i.then_inc(conv_ready, 1)
                else:
                    steps[0] += 1
                    i.then_inc(dstep, 1)

            behind = 8
            for s in range(8):
                after(s)
                if s == s_idx["v"]:
                    dve.wait_ge(z_evac, s + 1)
                    dve.wait_ge(zeroed, 1)
                    link(V.tensor_tensor(ypad[:, :, CONV_W - 1:], zt(U), zt(V_), ALU.mult))
                if s >= s_idx["v"]:
                    a = behind * (s - s_idx["v"])
                    for w, c in taps[a:a + behind]:
                        tap(w, c)
            for w, c in taps[behind * (8 - s_idx["v"]):]:
                tap(w, c)

            def compressor_sum(a):
                dve.wait_ge(cmp_sb, a + 1)
                v = xs_cmp(a).rearrange("p (l f n) -> p l f n", l=2, f=2)
                link(V.tensor_tensor(pebias[:, 2 * a:2 * a + 2].rearrange("p (f o) -> p f o", o=1), v[:, 0, :, 64:65], v[:, 1, :, 65:66], ALU.add))
                for f in range(2):
                    lo = v[:, 0, f, 0:64].rearrange("p (g c) -> p g c", g=NKV)[:, :, 0:15]
                    hi = v[:, 1, f, 0:64].rearrange("p (g c) -> p g c", g=NKV)[:, :, 1:16]
                    i = V.tensor_tensor(cmp_hidden(a)[:, f], lo, hi, ALU.add)
                    if f == 0:
                        link(i)
                i.then_inc(cmp_sum, 1)

            compressor_sum(0)
            dve.wait_ge(conv_ready, 1)
            dve.wait_ge(conv_mean, 1)
            link(V.tensor_tensor(lnd, conv, ps[:, 3:4, 0:T].to_broadcast([P, 2, T]), ALU.subtract))
            V.tensor_tensor(lnq, lnd, lnd, ALU.mult).then_inc(convd_ready, 1)
            after(8)
            compressor_sum(1)
            dve.wait_ge(conv_var, 1)
            V.tensor_scalar(lnv[:, 0, :], ps[:, 3, T:2 * T], EPS, None, ALU.add).then_inc(lnv_ready, 1)
            dve.wait_ge(zeroed, 2)
            dve.wait_ge(cmp2_ps, 2)
            for h in range(NQ):
                g = h // 3
                V.tensor_copy(vblk[32 * (h % 4):32 * (h % 4 + 1), h, :], ps[32 * g:32 * (g + 1), 7, 0:HD]).then_inc(vblk_ready, 1)
            dve.wait_ge(lnsq_ready, 1)
            link(V.reciprocal(lnq[:, 0, :], lnv[:, 1, :]))
            newton(lnq[:, 0, :], lnv[:, 0, :], lnq[:, 1, :])
            V.tensor_tensor(lnd, lnd, lnq[:, 0:1, :].to_broadcast([P, 2, T]), ALU.mult).then_inc(lnn_ready, 1)
            after(9)
            dve.wait_ge(sc_ps, 1)
            for e in range(2):
                half = lambda a: a.rearrange("p (a e n) -> p a e n", a=4, e=2)[:, :, e, :]
                link(V.tensor_tensor(half(scmp_flat), ps[:, 4 + e, 0:192].rearrange("p (a n) -> p a n", a=4),
                                     half(shared[:, 256:640]), ALU.add))
            mx, sm = st24
            link(V.tensor_reduce(mx, scmp, AX.X, ALU.max))
            link(V.tensor_scalar(mx, mx, -1.0e20, None, ALU.max))
            V.tensor_tensor(scmp, scmp, wide(mx), ALU.subtract).then_inc(sc_sb, 1)
            for c in range(2):
                dve.wait_ge(chi_ready, c + 1)
                V.tensor_tensor(mix_lo[:, c, :], conv[:, c, :], mix_hi[:, c, :].bitcast(F32), ALU.subtract).then_inc(clo_ready, 1)
            dve.wait_ge(pc_exp, 1)
            link(V.tensor_reduce(sm, scmp, AX.X, ALU.add))
            link(V.tensor_scalar(sm, sm, 1.0e-30, None, ALU.max))
            link(V.reciprocal(mx, sm))
            dve.wait_ge(z_evac, s_idx["g"] + 1)
            link(V.tensor_tensor(mx, mx, gates[:, :, :, 0], ALU.mult))
            dve.wait_ge(zeroed, 5)
            V.tensor_tensor(pcmp[:, :, :, 0:CMP_SLOT], scmp, wide(mx), ALU.mult).then_inc(pc_ready, 1)
            after(10)

            order = [6 * p + r + 3 * e for p in range(2) for r in range(3) for e in range(2)]

            def masked(n):
                h = order[n]
                dve.wait_ge(s_ps, n + 1)
                dve.wait_ge(alibi_ready, NQ)
                for br in range(2):
                    for m in range(2):
                        at = (2 * (n % 2) + br) * 384
                        c = 2 * br + m
                        bias = alibi[:, T * h:T * (h + 1)] if m else alibi[:, T * h + P:T * (h + 1)]
                        V.tensor_tensor_reduce(soft[:, at + m * P:at + P + m * T], ps[:, 2 * (n % 2) + br, m * P:P + m * T], bias,
                                               -1.0, 3.0e38, ALU.add, ALU.min, nmax[:, n % 2, c:c + 1]).then_inc(s_sb, 1)

            def normal(n):
                h = order[n]
                dve.wait_ge(p_exp, 4 * (n + 1))
                link(V.reciprocal(coef[:, n % 2, :], psum_p[:, n % 2, :]))
                cf = coef[:, n % 2, :].rearrange("p (b m) -> p b m", b=2)
                gt = gates[:, :, h, 1:3].rearrange("p m b -> p b m")
                link(V.tensor_tensor(cf, cf, gt, ALU.mult))
                for br in range(2):
                    for m in range(2):
                        o = soft[:, (2 * (n % 2) + br) * 384 + m * P:(2 * (n % 2) + br) * 384 + P + m * T]
                        V.tensor_scalar(o, o, coef[:, n % 2, 2 * br + m:2 * br + m + 1], None, ALU.mult).then_inc(p_ready, 1)

            def nsa_lo(j):
                dve.wait_ge(o_hi, j + 1)
                V.tensor_tensor(mix_lo[:, 2 + j, :], ps[:, 6, 0:T], mix_hi[:, 2 + j, :].bitcast(F32), ALU.subtract).then_inc(o_lo, 1)

            masked(0)
            dve.wait_ge(pcT_ps, 1)
            for c in range(3):
                V.tensor_copy(pcT[:, c, :], ps[:, 4 + c // 2, (c % 2) * T:(c % 2 + 1) * T]).then_inc(pcT_ready, 1)
            masked(1)
            normal(0)
            after(11)
            for n in range(NQ):
                dve.wait_ge(pT_ps, 2 * n + 1)
                if n >= 1:
                    dve.wait_ge(o_ps, n)
                V.tensor_copy(turned[:, 0:384], ps[:, 4, 0:384]).then_inc(pT_ready, 1)
                if n + 1 < NQ:
                    normal(n + 1)
                if n + 2 < NQ:
                    dve.wait_ge(pT_ps, 2 * (n + 1))
                    masked(n + 2)
                if n % 2 == 0 and n >= 2:
                    nsa_lo(n // 2 - 1)
            nsa_lo(5)

            def sum_ada(t, i=0):
                dve.wait_ge(s_ada[t % 2], i * 32 + 16 * (t // 2 + 1))
                dve.wait_ge(ada_used, i * 4 + (t + 1 if t >= 16 else max(t, 1)))
                k = t - 16 if t >= 16 else i * 2 + t // 2
                acc = mod_tail[:, :] if t >= 16 else mod_part[:, (t % 2) * TW:(t % 2 + 1) * TW]
                V.scalar_tensor_tensor(acc, ada[:, t % 2, :], silu_c[:, bass.ds(k, 1)], acc, ALU.mult, ALU.add).then_inc(ada_used, 1)

            def modulation(t, a, n):
                dve.wait_ge(mod_ps, t)
                b = VEC_A["b_ada"][0]
                V.tensor_tensor(modT[:, a:a + n], ps[:, 6, a:a + n], vec[:, b + a:b + a + n], ALU.add).then_inc(mod_ready, 1)
                dve.wait_ge(mod_ready, t)

            for i4 in range(4):
                after(s_idx[f"out{i4}"])
            dve.wait_ge(pe_tile, s_idx["out3"] + 1)
            for q in range(4):
                xs = x[:, q // 2, (q % 2) * 512:(q % 2 + 1) * 512]
                V.tensor_tensor(xs, xs, ps[:, q, :], ALU.add).then_inc(x_new, 1)
            dve.wait_ge(x_new, 4)
            norm_x()
            norm_scale()
            norm_lo(1, lambda k: col("ffn_norm", k))
            V.memset(mod_tail[:, :], 0.0).then_inc(ada_used, 1)
            dve.wait_ge(silu_c_ready, 1)
            dve.wait_ge(mod_zeroed, 1)

            def ff1_step(st, i=0):
                s0 = s_idx[f"gate{st}"]
                after(s0, i)
                dve.wait_ge(pe_tile, i * 6 + (s0 + 2))
                dve.wait_ge(silu_done, i * 2 + (st + 1))
                if st >= 2:
                    dve.wait_ge(hidlo_done, i * 2 + (st - 1))
                V.tensor_tensor(ff_hid[st % 2], ff_act[st % 2], ps[:, 5 + 2 * (st % 2), :], ALU.mult).then_inc(hid_done, 1)
                after(s0 + 1, i)
                dve.wait_ge(hidhi_done, i * 2 + (st + 1))
                V.tensor_tensor(hid_lo[st % 2], ff_hid[st % 2].rearrange("p (c t) -> p c t", c=2),
                                hid_hi[st % 2].bitcast(F32), ALU.subtract).then_inc(hidlo_done, 1)
                if st >= 1:
                    after(s0 + 2, i)
                if 2 <= st <= 9:
                    sum_ada(2 * (st - 2), i)
                    sum_ada(2 * (st - 2) + 1, i)

            ff1_step(0)
            ff1_step(1)
            with dve.Fori(0, TURNS) as i:
                ff1_step(2, i)
                ff1_step(3, i)
            ff1_step(10)
            after(s_idx["down10"])
            diagonals(vec[:, VEC_A["final"][0]:VEC_A["final"][0] + 8])
            dve.wait_ge(pe_tile, s_idx["down10"] + 1)
            for q in range(4):
                xs = x[:, q // 2, (q % 2) * 512:(q % 2 + 1) * 512]
                V.tensor_tensor(xs, xs, ps[:, q, :], ALU.add).then_inc(x_new, 1)
            dve.wait_ge(x_new, 8)
            norm_x()
            row(0)
            for m in range(2):
                V.scalar_tensor_tensor(x[:, m, :], x[:, m, :], rst[:, m:m + 1], rowb, ALU.mult, ALU.mult).then_inc(x_new, 1)
            dve.wait_ge(x_new, 10)

            def modulated(g, i):
                link(V.tensor_scalar(scl, modT[:, i:i + 8], 1.0, None, ALU.add))
                link(V.tensor_tensor(scl, scl, vec[:, VEC_A[g][0]:VEC_A[g][0] + 8], ALU.mult))

            norm_x()
            modulation(1, 0, 32)
            modulated("g_pre_mix", 8)
            norm_scale()
            norm_lo(2, lambda k: scl[:, k:k + 1], lambda k: modT[:, k:k + 1])

            cos, sin = shared[:, 0:T], shared[:, T:2 * T]
            rots = [0]

            def rotate(view, groups):
                n = groups * T
                dve.wait_ge(rot_ps, rots[0] + 1)
                t = rtmp[:, 0:n].rearrange("p (g t) -> p g t", g=groups)
                s = ps[:, 3, 0:n].rearrange("p (g t) -> p g t", g=groups)
                v = view.rearrange("p (g t) -> p g t", g=groups)
                bc = lambda a: a.rearrange("p (g t) -> p g t", g=1).to_broadcast([P, groups, T])
                link(V.tensor_tensor(t, s, bc(sin), ALU.mult))
                link(V.tensor_tensor(v, v, bc(cos), ALU.mult))
                V.tensor_tensor(v, v, t, ALU.add).then_inc(rot_done, 1)
                rots[0] += 1

            def index_sum(h):
                dve.wait_ge(relu_done, h + 1)
                if h >= 1:
                    dve.wait_ge(ix_acc, 2 * h)
                for m in range(2):
                    o = isc[:, m * P:P + m * T]
                    base_ = (cst("causal") if m else cst("causal")[:, P:T]) if h == 0 else o
                    V.scalar_tensor_tensor(o, relu_b[h % 2][:, m * P:P + m * T], wi_s[:, m, h:h + 1], base_,
                                           ALU.mult, ALU.add).then_inc(ix_acc, 1)

            def take8(m):
                o = isc[:, m * P:P + m * T]
                link(V.max(top8, o))
                link(V.match_replace(o, top8, o, TAKEN))

            takes = [m for _ in range(TOPK // 8) for m in range(2)]
            for s in range(s_idx["idx"], s_idx["vb1"] + 1):
                name = s_name[s]
                after(s)
                if s >= s_idx["qb0"]:
                    sum_ada(16 + s - s_idx["qb0"])
                if name == "qa0":
                    rotate(kiT, 1)
                    rotate(z[:, QI, :], 2)
                    rotate(z[:, QI + 1, :], 2)
                if name == "qa1":
                    for h in range(4):
                        index_sum(h)
                    rotate(z[:, QA, :], 2)
                if name == "ka0":
                    for h in range(4, 8):
                        index_sum(h)
                    rotate(z[:, QA + 1, :], 2)
                    dve.wait_ge(ix_acc, 16)
                if name == "ka1":
                    rotate(z[:, KA, :], 2)
                if name == "qb0":
                    rotate(z[:, KA + 1, :], 2)
                if s > s_idx["ka0"] and takes:
                    for m in takes[:2]:
                        take8(m)
                    takes = takes[2:]
            assert not takes
            link(V.tensor_scalar(abias, isc, TAKEN, NEG, ALU.not_equal, ALU.mult))
            for m in range(2):
                o = abias[:, m * P:P + m * T]
                V.tensor_tensor(o, o, cst("causal") if m else cst("causal")[:, P:T], ALU.add).then_inc(bias_ready, 1)
            dve.wait_ge(bias_ready, 2)

            def a_masked(h):
                dve.wait_ge(s_ps, NQ + h + 1)
                for m in range(2):
                    V.tensor_tensor_reduce(sA[h % 2][:, m * P:P + m * T], ps[:, h % 2, m * P:P + m * T], abias[:, m * P:P + m * T],
                                           -1.0, 3.0e38, ALU.add, ALU.min, nmax[:, h % 2, m:m + 1]).then_inc(s_sb, 1)

            def diag_masked(dst, bank, inc):
                two = lambda a: a.rearrange("p (k n) -> p k n", n=P)[:, 0:3:2, :]
                link(V.tensor_tensor(two(dst), two(ps[:, bank, 0:384]), cst("strict").rearrange("p (o n) -> p o n", o=1).to_broadcast([P, 2, P]), ALU.add))
                V.tensor_copy(dst[:, P:T], ps[:, bank, P:T]).then_inc(inc, 1)

            def b_front(h):
                dve.wait_ge(b_z, h + 1)
                diag_masked(zm[h % 2], 3 + h % 2, b_zm)
                dve.wait_ge(b_zm, h + 1)
                if h >= 1:
                    dve.wait_ge(b_sp, h)
                V.scalar_tensor_tensor(eb, zm[h % 2], -1.0, zm[h % 2], ALU.mult, ALU.min).then_inc(b_abs, 1)

            def softplus(h):
                dve.wait_ge(b_ln, h + 1)
                if h >= 1:
                    dve.wait_ge(b_c, h)
                V.scalar_tensor_tensor(spb, zm[h % 2], 0.0, eb, ALU.max, ALU.add).then_inc(b_sp, 1)

            def a_normal(h):
                dve.wait_ge(p_exp, 4 * NQ + 2 * (h + 1))
                link(V.reciprocal(coef[:, h % 2, 0:2], psum_p[:, h % 2, 0:2]))
                for m in range(2):
                    o = sA[h % 2][:, m * P:P + m * T]
                    V.tensor_scalar(o, o, coef[:, h % 2, m:m + 1], None, ALU.mult).then_inc(p_ready, 1)

            def mixed_lo(j):
                dve.wait_ge(o_hi, 6 + j + 1)
                V.tensor_tensor(mix_lo[:, j::4, :], ps[:, 6, :].rearrange("p (e t) -> p e t", e=2),
                                mix_hi[:, j::4, :].bitcast(F32), ALU.subtract).then_inc(o_lo, 1)

            a_masked(0)
            b_front(0)
            a_masked(1)
            softplus(0)
            a_normal(0)
            for h in range(NB_HEADS):
                if h + 1 < NB_HEADS:
                    b_front(h + 1)
                dve.wait_ge(pT_ps, 2 * NQ + h + 1)
                if h >= 1:
                    dve.wait_ge(o_ps, NQ + 2 * h)
                V.tensor_copy(pTA, ps[:, 2, 0:384]).then_inc(pT_ready, 1)
                dve.wait_ge(b_c, h + 1)
                two = lambda a: a.rearrange("p (k n) -> p k n", n=P)[:, 0:3:2, :]
                V.tensor_tensor(two(attb), two(ps[:, 5, 0:384]), cst("strict").rearrange("p (o n) -> p o n", o=1).to_broadcast([P, 2, P]),
                                ALU.add).then_inc(b_cm, 1)
                V.tensor_copy(attb[:, P:T], ps[:, 5, P:T]).then_inc(b_cm, 1)
                if h + 2 < NB_HEADS:
                    a_masked(h + 2)
                if h + 1 < NB_HEADS:
                    softplus(h + 1)
                    a_normal(h + 1)
                if h % 2 == 0 and h >= 2:
                    mixed_lo(h // 2 - 1)
                after(s_idx[f"sg{h}"])
            mixed_lo(3)

            for u in range(2):
                after(s_idx[f"upa{u}"])
                dve.wait_ge(pe_tile, s_idx[f"upa{u}"] + 1)
                dve.wait_ge(gates_open, u + 1)
                ga, gb = sgate[:, 0, 4 * u:4 * u + 4, :], sgate[:, 1, 4 * u:4 * u + 4, :]
                pa = ps[:, 4 * u:4 * u + 2, :].rearrange("p a (c t) -> p (a c) t", c=2)
                pb = ps[:, 4 * u + 2:4 * u + 4, :].rearrange("p a (c t) -> p (a c) t", c=2)
                V.tensor_tensor(ga, pa, ga, ALU.mult).then_inc(up_a, 1)
                after(s_idx[f"upb{u}"])
                dve.wait_ge(pe_tile, s_idx[f"upb{u}"] + 1)
                link(V.tensor_tensor(gb, pb, gb, ALU.mult))
                dve.wait_ge(up_a, u + 1)
                V.tensor_tensor(merged(u), ga, gb, ALU.add).then_inc(m_sum, 1)
                dve.wait_ge(m_hi, u + 1)
                V.tensor_tensor(h_lo[:, 4 * u:4 * u + 4, :], merged(u), h_hi[:, 4 * u:4 * u + 4, :].bitcast(F32), ALU.subtract).then_inc(m_lo, 1)
            for i4 in range(4):
                after(s_idx[f"o2{i4}"])

            def post_norm(t, g, i, target):
                link(V.tensor_tensor(scl, modT[:, i:i + 8], vec[:, VEC_A[g][0]:VEC_A[g][0] + 8], ALU.mult))
                diagonals(scl)
                dve.wait_ge(sqy, 4 * t)
                halves = part.rearrange("p (m n) -> p m n", m=2)
                link(V.tensor_reduce(msum, halves, AX.X, ALU.add))
                link(V.tensor_scalar(msum, msum, 1.0 / D, None, ALU.mult))
                rstd()
                row(t)
                for q in range(4):
                    xs = x[:, q // 2, (q % 2) * 512:(q % 2 + 1) * 512]
                    t_ = xn_scratch[:, 512 * (q % 2):512 * (q % 2 + 1)]
                    link(V.scalar_tensor_tensor(t_, ps[:, q, :], rst[:, q // 2:q // 2 + 1], rowb[:, (q % 2) * 512:(q % 2 + 1) * 512], ALU.mult, ALU.mult))
                    V.tensor_tensor(xs, xs, t_, ALU.add).then_inc(y_res, 1)
                dve.wait_ge(y_res, 4 * t)

            post_norm(1, "g_post_mix", 16, None)
            norm_x()
            modulation(2, 32, 16)
            modulated("g_pre_ffn", 32)
            norm_scale()
            norm_lo(3, lambda k: scl[:, k:k + 1], lambda k: modT[:, 24 + k:25 + k])

            def ff2_step(st, i=0):
                s0 = s_idx[f"fa{st}"]
                after(s0, i)
                dve.wait_ge(relu2_done, i * 3 + (st + 1))
                if st >= 3:
                    dve.wait_ge(hid2lo_done, i * 3 + (st - 2))
                V.tensor_tensor(ff_hid[st % 3], ff_act[st % 3], ff_act[st % 3], ALU.mult).then_inc(hid2_done, 1)
                dve.wait_ge(hid2hi_done, i * 3 + (st + 1))
                V.tensor_tensor(hid_lo[st % 3], ff_hid[st % 3].rearrange("p (c t) -> p c t", c=2),
                                hid_hi[st % 3].bitcast(F32), ALU.subtract).then_inc(hid2lo_done, 1)
                if st >= 1:
                    after(s0 + 1, i)

            for st in range(5):
                ff2_step(st)
            with dve.Fori(1, TURNS) as i:
                ff2_step(2, i)
                ff2_step(3, i)
                ff2_step(4, i)
            ff2_step(14)
            ff2_step(15)
            post_norm(2, "g_post_ffn", 40, None)


def _cols(w):
    k, n = w.shape[0] // 128, w.shape[1] // 256
    return w.reshape(k, 128, n, 256).transpose(2, 1, 0, 3).reshape(n, 128, k * 256)


def _rows(w):
    return w.reshape(-1, 2, 128, 1024).transpose(0, 2, 1, 3).reshape(-1, 128, 2048)


def _narrow(w):
    return np.ascontiguousarray(w.reshape(8, 128, -1).transpose(1, 0, 2).reshape(128, -1))


def _pair_heads(w, axis):
    s = w.shape
    shape = s[:axis] + (2, 2, 3, 64) + s[axis + 1:]
    order = list(range(len(shape)))
    order[axis + 1], order[axis + 2] = axis + 2, axis + 1
    return w.reshape(shape).transpose(order).reshape(s)


def _layout(a):
    f = lambda n: np.asarray(a[n])[0]
    w_in, w_out, gu, down = f("w_in"), f("w_out"), f("w_gate_up"), f("w_down")
    q = _pair_heads(w_in[:, 512:1280], 1)
    kv = lambda i: w_in[:, 1280 + 256 * i:1536 + 256 * i]
    first = _cols(np.concatenate([w_in[:, 0:512], kv(0), kv(1), q, kv(2), kv(4), kv(3), kv(5)], 1))
    w_g = _narrow(w_in[:, 2816:2852])
    cmp1 = [f(n).reshape(2, 8, 128, 256).transpose(0, 2, 1, 3).reshape(2, 128, 2048) for n in ("cmp_k_w1", "cmp_v_w1")]
    out1 = np.concatenate([w_out[:256], _pair_heads(w_out[256:], 0)], 0)
    gate, up, dn = _cols(gu[:, :2816]), _cols(gu[:, 2816:]), _rows(down)
    ffn1 = [gate[0:1], up[0:1]]
    for i in range(1, FF1_STEPS):
        ffn1 += [gate[i:i + 1], up[i:i + 1], dn[i - 1:i]]
    ffn1 += [dn[-1:]]
    w2 = f("w_in_2")
    qa, ka, va, qb, kb, vb, qi = (w2[:, 512 * i:512 * (i + 1)] for i in range(7))
    ki, wi, sg = w2[:, 3584:3648], w2[:, 3648:3656], w2[:, 3656:]
    w_idx = _narrow(np.concatenate([ki, ki, wi], 1))
    ups = [f(n).reshape(4, 128, 2, 512).transpose(2, 1, 0, 3).reshape(2, 128, 2048) for n in ("w_up_a_2", "w_up_b_2")]
    fa, fb = _cols(f("w_ff1_2")), _rows(f("w_ff2_2"))
    ffn2 = [fa[0:1]]
    for i in range(1, FF2_STEPS):
        ffn2 += [fa[i:i + 1], fb[i - 1:i]]
    ffn2 += [fb[-1:]]
    stream = [first[:-1], *cmp1, first[-1:], _rows(out1), *ffn1,
              _cols(np.concatenate([qi, qa, ka, qb, kb, va, vb, sg], 1)),
              ups[0][0:1], ups[1][0:1], ups[0][1:2], ups[1][1:2], _rows(f("w_out_2")), *ffn2]
    wts = np.concatenate(stream, 0)
    vecs = {"attn_norm": f("attn_norm"), "ffn_norm": f("ffn_norm"), "g_pre_mix": f("g_pre_mix_2"), "g_pre_ffn": f("g_pre_ffn_2"),
            "c": f("c_2"), "b_ada": f("b_ada_2"), "conv_b": f("conv_b"), "ln_g": f("conv_ln_g"), "ln_b": f("conv_ln_b"),
            "g_post_mix": f("g_post_mix_2"), "g_post_ffn": f("g_post_ffn_2"), "final": np.asarray(a["final_norm"])}
    rows_a = np.concatenate([vecs[n].reshape(-1, 128) for n in VEC_A], 0)
    rows_b = np.concatenate([f("conv_w").reshape(-1, 128), f("cmp_k_pe").reshape(-1, 128), f("cmp_v_pe").reshape(-1, 128)], 0)
    w2c = np.concatenate([f(n).reshape(2, 128, 64).transpose(1, 0, 2).reshape(128, 128) for n in ("cmp_k_w2", "cmp_v_w2")], 1)
    ada = f("w_ada_2").reshape(8, 128, 3, 2048).transpose(0, 2, 1, 3)
    w_ada = np.concatenate([ada[:, 0:2].reshape(16, 128, 2048), ada[:, 2]], 0)
    return {"x": np.asarray(a["x"])[0], "wts": wts, "w_ada": w_ada, "w_g": w_g, "w_idx": w_idx, "rows_a": rows_a, "rows_b": rows_b, "cmp_w2": w2c}


def _constants():
    p, t = np.arange(128), np.arange(256)
    c = {"ident": np.eye(128), "tri": -(p[:, None] >= p[None, :]).astype(np.float32), "negones": -np.ones((128, 128)),
         "strict": np.where(p[:, None] < p[None, :], 0.0, NEG), "mean": np.full((128, 128), 1.0 / 256), "ones": np.ones((128, 128))}
    dist = t[None, :] - (p[:, None] + 128)
    c["causal"] = np.where(dist <= 0, 0.0, NEG)
    const = np.concatenate([c[n] for n in CONST], 1).astype(np.float32)
    sl = np.asarray(slopes())
    tt = np.arange(256).reshape(2, 128)
    n = np.arange(16)
    center, end = n * 16 + 15.5, n * 16 + 31
    valid = (end[None, None, :] <= tt[:, :, None]) & (n < 15)
    cb = np.where(valid[:, :, None, :], -sl[None, None, :, None] * (tt[:, :, None, None] - center), NEG)
    shared_1 = np.concatenate([np.where(dist <= 0, dist, -1.0e33), cb.transpose(1, 0, 2, 3).reshape(128, -1)], 1).astype(np.float32)
    ang = np.arange(256, dtype=np.float32)[:, None] * (500000.0 ** (-np.arange(0, 16, 2, dtype=np.float32) / 16)).astype(np.float32)
    cos, sin, swap = np.ones((128, 256)), np.zeros((128, 256)), np.zeros((128, 128))
    for b in (0, 64):
        for i in range(8):
            cos[b + i] = cos[b + 8 + i] = np.cos(ang[:, i])
            sin[b + i] = sin[b + 8 + i] = np.sin(ang[:, i])
            swap[b + 8 + i, b + i] = -1.0
            swap[b + i, b + 8 + i] = 1.0
    shared_2 = np.concatenate([cos, sin, swap], 1).astype(np.float32)
    return {"const": const, "shared_1": shared_1, "shared_2": shared_2}


def kernel(**inputs):
    import concourse.bacc as _bacc
    from concourse.bass_utils import run_bass_kernel_spmd as _run

    nc = _bacc.Bacc("TRN2", target_bir_lowering=False, num_devices=1)
    arrays = {n: np.ascontiguousarray(v) for n, v in {**_layout(inputs), **_constants()}.items()}
    ap = {n: nc.dram_tensor(n, v.shape, mybir.dt.from_np(v.dtype), kind="ExternalInput").ap() for n, v in arrays.items()}
    out = nc.dram_tensor("out", (T, D), F32, kind="ExternalOutput").ap()
    build(nc, ap["x"], ap["wts"], ap["w_ada"], ap["w_g"], ap["w_idx"], ap["rows_a"], ap["rows_b"], ap["cmp_w2"], ap["const"],
          ap["shared_1"], ap["shared_2"], out)
    r = _run(nc, [arrays], core_ids=[0])
    return r.results[0]["out"].reshape(1, T, D)
```

```python
import math
from contextlib import ExitStack

import numpy as np

import concourse.bass as bass
from concourse import mybir

F32 = mybir.dt.float32
F32R = mybir.dt.float32r
ALU = mybir.AluOpType
ACT = mybir.ActivationFunctionType
AX = mybir.AxisListType

P = 128
T = 256
D = 1024
DC = D // P
HD = 64
EPS = 1e-6
CONV_W = 31
NQ, NKV = 12, 4
NB_HEADS = 8
TOPK = T // 4
N_CMP = 15
CMP_SLOT = 16
FF1_STEPS = 11
FF2_STEPS = 16
NEG = -1.0e30
TAKEN = -3.0e38

TW = 2048
RAW, RING = 3, 3
TURN = 6

def plan():
    tiles = [("s", n) for n in ("u", "v", "kc", "vc", "q0", "q1", "q2", "ks", "kw", "g", "vs")]
    tiles += [("d", f"cmp{i}") for i in range(4)] + [("s", "vw")]
    tiles += [("s", f"out{i}") for i in range(3)]
    tiles += [("s", "out3"), ("s", "gate0"), ("s", "up0")]
    for i in range(1, FF1_STEPS):
        tiles += [("s", f"gate{i}"), ("s", f"up{i}"), ("s", f"down{i - 1}")]
    tiles += [("s", f"down{FF1_STEPS - 1}")]
    tiles += [("s", n) for n in ("idx", "qi0", "qi1", "qa0", "qa1", "ka0", "ka1", "qb0", "qb1", "kb0", "kb1",
                                 "va0", "va1", "vb0", "vb1")]
    tiles += [("s", f"sg{i}") for i in range(8)]
    tiles += [("s", n) for n in ("upa0", "upb0", "upa1", "upb1")] + [("s", f"o2{i}") for i in range(4)]
    tiles += [("s", "fa0")]
    for i in range(1, FF2_STEPS):
        tiles += [("s", f"fa{i}"), ("s", f"fb{i - 1}")]
    tiles += [("s", f"fb{FF2_STEPS - 1}")]
    return tiles


TILES = plan()
G_COLS = 36
IDX_COLS = 136

VEC_A = {}
for _name, _rows in (("attn_norm", 8), ("ffn_norm", 8), ("g_pre_mix", 8), ("g_pre_ffn", 8), ("b_ada", 48),
                     ("conv_b", 2), ("ln_g", 2), ("ln_b", 2), ("g_post_mix", 8), ("g_post_ffn", 8)):
    VEC_A[_name] = (sum(r for _, r in VEC_A.values()), _rows)
NA_ROWS = sum(r for _, r in VEC_A.values())
NB_ROWS = 2 * CONV_W + 32

CONST = {}
for _name, _w in (("ident", 128), ("causal", 256), ("tri", 128), ("negones", 128), ("strict", 128), ("mean", 128),
                  ("ones", 128)):
    CONST[_name] = (sum(w for _, w in CONST.values()), _w)
NCONST = sum(w for _, w in CONST.values())
NSHARED = 640


def slopes():
    def pow2(m):
        return [(2.0 ** (-8.0 / m)) ** (i + 1) for i in range(m)]
    return [float(s) for s in np.asarray(pow2(8) + pow2(16)[0::2][:NQ - 8], np.float32)]


def build(nc, x_in, wts, w_ada, w_g, w_idx, rows_a, rows_b, rows_wide, cmp_w2, const_in, shared_1, shared_2, out):
    ctx = ExitStack()
    with ctx:
        def sb(name, shape, dt=F32):
            return ctx.enter_context(nc.sbuf_tensor(name, shape, dt))

        def sem(name):
            return ctx.enter_context(nc.semaphore(name))

        raw = sb("raw", [P, RAW, TW])
        w_hi = sb("w_hi", [P, RING, TW], F32R)
        w_lo = sb("w_lo", [P, RING, TW], F32R)
        x = sb("resid", [P, 2, D])
        h_hi = sb("h_hi", [P, DC, T], F32R)
        h_lo = sb("h_lo", [P, DC, T], F32R)
        mix_hi = sb("mix_hi", [P, DC, T], F32R)
        mix_lo = sb("mix_lo", [P, DC, T], F32R)
        const = sb("consts", [P, NCONST])
        shared = sb("shared", [P, NSHARED])
        vec = sb("vec", [P, NA_ROWS])
        vec_b = sb("vec_b", [P, NB_ROWS])
        z = sb("z", [P, 14, 2 * T])
        alibi = sb("alibi", [P, 4096])
        soft = sb("soft", [P, 1536])
        turned = sb("turned", [P, 768])
        misc = sb("misc", [P, 2048])
        small = sb("small", [P, 224])
        modT = sb("modT", [P, 48])
        ada = sb("ada", [P, 2, TW])
        rows_ga = sb("rows_ga", [P, 2, D])
        ps = ctx.enter_context(nc.psum_tensor("ps", [P, 8, 512], F32))

        def cst(name):
            a, w = CONST[name]
            return const[:, a:a + w]

        def col(name, i):
            return vec[:, VEC_A[name][0] + i:VEC_A[name][0] + i + 1]

        ident = cst("ident")

        def zt(i):
            return z[:, i, :].rearrange("p (c t) -> p c t", c=2)
        U, V_, Q0, KC, VC, KS, KW, VS, VW = 0, 1, 2, 5, 6, 7, 8, 9, 10
        z_at = {"u": U, "v": V_, "q0": Q0, "q1": Q0 + 1, "q2": Q0 + 2, "kc": KC, "vc": VC, "ks": KS, "kw": KW, "vs": VS, "vw": VW}
        zflat = z[:, :, :].rearrange("p a b -> p (a b)")
        tail = zflat[:, 11 * 512:14 * 512]
        kr = [tail[:, 528 * i:528 * (i + 1)].rearrange("p (j n) -> p j n", j=8) for i in range(2)]
        hcmp = [tail[:, 1056:1312].rearrange("p (f n) -> p f n", f=2), misc[:, 1536:1792].rearrange("p (f n) -> p f n", f=2)]
        kcmp = tail[:, 1312:1376]
        vblk = misc[:, 0:768].rearrange("p (h d) -> p h d", h=NQ)
        pcT = misc[:, 768:1536].rearrange("p (c t) -> p c t", c=3)
        w2 = misc[:, 1792:2048].rearrange("p (a f d) -> p a f d", a=2, f=2)
        early = ada[:, :, :].rearrange("p a w -> p (a w)")
        ypad = early[:, 0:572].rearrange("p (c t) -> p c t", c=2)
        conv = early[:, 572:1084].rearrange("p (c t) -> p c t", c=2)
        lnv = early[:, 1084:1596].rearrange("p (a t) -> p a t", a=2)
        lnd = z[:, U, :].rearrange("p (c t) -> p c t", c=2)
        lnq = z[:, V_, :].rearrange("p (c t) -> p c t", c=2)
        scmp_flat = early[:, 2364:2748]
        scmp = scmp_flat.rearrange("p (m h n) -> p m h n", m=2, h=NQ)
        pcmp = early[:, 2748:3516].rearrange("p (m h n) -> p m h n", m=2, h=NQ)
        gT = early[0:G_COLS, 3516:3772]
        wiT = misc[0:NB_HEADS, 1536:1792]
        probs = [soft[:, 0:768], soft[:, 768:1536], early[:, 0:768]]
        gates = small[:, 0:72].rearrange("p (m h b) -> p m h b", m=2, h=NQ)
        st24 = [small[:, 72 + 24 * i:96 + 24 * i].rearrange("p (m h) -> p m h", m=2) for i in range(2)]
        msum, rst, nwt, sqv, part = (small[:, 192 + 4 * i:196 + 4 * i] for i in range(5))
        nmax = small[:, 128:136].rearrange("p (a b) -> p a b", a=2)
        psum_p = small[:, 136:144].rearrange("p (a b) -> p a b", a=2)
        coef = small[:, 144:152].rearrange("p (a b) -> p a b", a=2)
        pebias = small[:, 152:156]
        gcol = small[:, 160:168]
        mod_turn = small[:, 212:220]
        scl = small[:, 168:176]
        wi_s = small[:, 176:192].rearrange("p (m h) -> p m h", m=2)
        top8 = small[:, 72:80]
        xn = zflat[:, 0:2048].rearrange("p (m d) -> p m d", m=2)
        y_norm = zflat[:, 2048:4096].rearrange("p (q n) -> p q n", q=4)
        sq_full, sq_half, sq_last = soft[:, 0:1024], soft[:, 1024:1536], turned[:, 0:512]
        h_full = misc[:, 0:1024]
        ff_act = [z[:, i, :] for i in range(3)]
        ff_hid = [z[:, 3 + i, :] for i in range(3)]
        hid_hi = [mix_hi[:, 2 * i:2 * i + 2, :] for i in range(3)]
        hid_lo = [mix_lo[:, 2 * i:2 * i + 2, :] for i in range(3)]
        final_row, c_row = rows_ga[:, 0, :], rows_ga[:, 1, :]
        diag = alibi[:, 2 * D:3 * D].rearrange("p (k n) -> p k n", k=8)
        QI, QA, KA, QB, KB, VA, VB = 0, 2, 4, 6, 8, 10, 12

        def wide(v):
            return v.rearrange("p m (h o) -> p m h o", o=1).to_broadcast([P, 2, NQ, CMP_SLOT])

        def xs_cmp(a):
            return early[:, 1596 + 264 * a:1860 + 264 * a]

        def cmp_hidden(a):
            return early[:, 2124 + 120 * a:2244 + 120 * a].rearrange("p (f g n) -> p f g n", f=2, g=NKV)

        def merged(u):
            return zflat[:, 1024 * u:1024 * (u + 1)].rearrange("p (c t) -> p c t", c=4)
        sgate = alibi[:, :].rearrange("p (a k t) -> p a k t", a=2, k=8)
        kiT = turned[:, 0:256]
        rtmp = soft[:, 0:512]
        isc = misc[:, 0:384]
        abias = misc[:, 384:768]
        relu_b = [soft[:, 768 + 384 * i:1152 + 384 * i] for i in range(2)]
        sA = [soft[:, 384 * i:384 * (i + 1)] for i in range(2)]
        pTA = turned[:, 0:384]
        zm = [soft[:, 768 + 384 * i:1152 + 384 * i] for i in range(2)]
        eb = turned[:, 384:768]
        spb = misc[:, 768:1152]
        attb = misc[:, 1152:1536]

        s_raw = [sem(f"raw{i}_landed") for i in range(RAW)]
        s_ada = [sem(f"ada{i}_landed") for i in range(2)]
        ada_used, mod_kept, c_ready, s_wide, xf_new, hf_ready = (sem(n) for n in ("ada_used", "mod_kept", "c_ready", "wide_landed", "x_final_new", "h_full_ready"))
        s_x = [sem(f"x{m}_landed") for m in range(2)]
        s_const, s_rows, s_shared, s_w2, s_out = (sem(n) for n in (
            "const_landed", "rows_landed", "shared_landed", "w2_landed", "out_written"))
        hi_ready = sem("hi_ready")
        w_ready = sem("w_ready")
        pe_tile = sem("pe_tile")
        direct_done = sem("direct_done")
        z_evac = sem("z_evac")
        vec_ps, vec_ready = sem("vec_ps"), sem("vec_ready")
        ms_ready, sq_ready = sem("ms_ready"), sem("sq_ready")
        xn_ready, xT_ready, hhi_ready, h_ready = sem("xn_ready"), sem("xT_ready"), sem("hhi_ready"), sem("h_ready")
        dstep, astep = sem("dve_step"), sem("act_step")
        zeroed, alibi_ready = sem("zeroed"), sem("alibi_ready")
        conv_ready, conv_mean, convd_ready, conv_var = (sem(n) for n in ("conv_ready", "conv_mean", "convd_ready", "conv_var"))
        lnv_ready, lnsq_ready, lnn_ready, chi_ready, clo_ready = (sem(n) for n in (
            "lnv_ready", "lnsq_ready", "lnn_ready", "conv_hi_ready", "conv_lo_ready"))
        kr_ready, cmp_ps, cmp_sb, cmp_sum, cmp_h, cmp2_ps, cmp2_sb, vblk_ready = (sem(n) for n in (
            "kr_ready", "cmp_ps", "cmp_sb", "cmp_sum", "cmp_h", "cmp2_ps", "cmp_keys_ready", "cmp_values_ready"))
        narrow_sb, narrow_ps, wi_ready = sem("narrow_sb"), sem("narrow_ps"), sem("wi_ready")
        sc_ps, sc_sb, pc_exp, pc_ready, pcT_ps, pcT_ready = (sem(n) for n in (
            "cmp_scores_ps", "cmp_scores_sb", "cmp_probs_exp", "cmp_probs_ready", "cmp_probsT_ps", "cmp_probsT_ready"))
        s_ps, s_sb, p_exp, p_ready, pT_ps, pT_ready, pTn_ready, o_ps, o_hi, o_lo = (sem(n) for n in (
            "scores_ps", "scores_sb", "probs_exp", "probs_ready", "probsT_ps", "probsT_ready", "nsa_probsT_ready", "o_ps", "o_hi", "o_lo"))
        acc_ps, x_new = sem("acc_ps"), sem("x_new")
        silu_done, hid_done, hidhi_done, hidlo_done = (sem(n) for n in ("silu_done", "hid_done", "hid_hi_done", "hid_lo_done"))
        relu2_done, hid2_done, hid2hi_done, hid2lo_done = (sem(n) for n in ("relu2_done", "hid2_done", "hid2_hi_done", "hid2_lo_done"))
        diag_ready, row_ps, row_ready = sem("diag_ready"), sem("row_ps"), sem("row_ready")
        rot_ps, rot_done, ix_ps, relu_done, ix_acc = (sem(n) for n in ("rot_ps", "rot_done", "ix_ps", "relu_done", "ix_acc"))
        bias_ready, gates_open = sem("bias_ready"), sem("gates_open")
        b_z, b_zm, b_abs, b_ln, b_sp, b_c, b_cm, b_att = (sem(n) for n in (
            "b_scores_ps", "b_masked", "b_abs", "b_ln", "b_softplus", "b_sum_ps", "b_sum_masked", "b_att"))
        up_ps, up_a, m_sum, m_hi, m_lo = (sem(n) for n in ("up_ps", "up_used", "merged", "merged_hi", "merged_lo"))
        sqy, y_gain, y_res = sem("squares"), sem("y_gained"), sem("y_residual")

        n_of = {name: n for n, (_, name) in enumerate(TILES)}
        s_idx, d_idx = {}, {}
        for kind, name in TILES:
            (s_idx if kind == "s" else d_idx)[name] = len(s_idx) if kind == "s" else len(d_idx)
        s_name = {v: k for k, v in s_idx.items()}
        NSPLIT = len(s_idx)
        FF1_LOOP, FF2_LOOP, LOOPED, TURNS = s_idx["gate2"], s_idx["fa2"], 24, 4
        ff1_tiles, ff2_tiles = range(FF1_LOOP, FF1_LOOP + LOOPED), range(FF2_LOOP, FF2_LOOP + LOOPED)

        def tile_width(name):
            return {"g": DC * G_COLS, "idx": DC * IDX_COLS}.get(name, TW)

        def raw_of(name):
            return raw[:, n_of[name] % RAW, 0:tile_width(name)]

        def landed(eng, name):
            n = n_of[name]
            eng.wait_ge(s_raw[n % RAW], 16 * (n // RAW + 1))

        block = ctx.enter_context(nc.Block())

        @block.sync
        def _(sp):
            for m in range(2):
                sp.dma_start(x[:, m, :], x_in[m * P:(m + 1) * P, :]).then_inc(s_x[m], 16)
            sp.dma_start(const[:, :], const_in).then_inc(s_const, 16)
            sp.dma_start(raw[0:NA_ROWS, RAW - 1, 0:P], rows_a).then_inc(s_rows, 16)
            sp.dma_start(raw[0:NB_ROWS, RAW - 1, P:2 * P], rows_b).then_inc(s_rows, 16)

            def load(name):
                n = n_of[name]
                if n >= RAW:
                    kind, old = TILES[n - RAW]
                    if kind == "s":
                        sp.wait_ge(w_ready, s_idx[old] + 1)
                    else:
                        sp.wait_ge(direct_done, d_idx[old] + 1)
                if n == RAW - 1:
                    sp.wait_ge(vec_ps, 1)
                src = {"g": w_g, "idx": w_idx}.get(name)
                if src is None:
                    src = wts[n - (n > n_of["g"]) - (n > n_of["idx"]), :, :]
                sp.dma_start(raw_of(name), src).then_inc(s_raw[n % RAW], 16)

            def load_loop(first):
                n0, s0 = n_of[s_name[first]], first
                w0 = n0 - (n0 > n_of["g"]) - (n0 > n_of["idx"])
                with sp.Fori(0, TURNS) as i:
                    for j in range(TURN):
                        sp.wait_ge(w_ready, i * TURN + (s0 + j - RAW + 1))
                        src = wts[bass.ds(i * TURN + (w0 + j), 1), :, :].rearrange("a p w -> (a p) w")
                        sp.dma_start(raw[:, (n0 + j) % RAW, :], src).then_inc(s_raw[(n0 + j) % RAW], 16)

            for kind, name in TILES:
                if kind == "s" and s_idx[name] in ff1_tiles:
                    if s_idx[name] == FF1_LOOP:
                        load_loop(FF1_LOOP)
                elif kind == "s" and s_idx[name] in ff2_tiles:
                    if s_idx[name] == FF2_LOOP:
                        load_loop(FF2_LOOP)
                else:
                    load(name)
                if name == "u":
                    sp.dma_start(shared[:, :], shared_1).then_inc(s_shared, 16)
                    sp.dma_start(w2.rearrange("p a f d -> p (a f d)"), cmp_w2).then_inc(s_w2, 16)
                if name == "down0":
                    sp.wait_ge(x_new, 4)
                    sp.dma_start(shared[:, :], shared_2).then_inc(s_shared, 16)
                    sp.dma_start(rows_ga[:, :, :].rearrange("p a n -> p (a n)"), rows_wide.to_broadcast([P, 2 * D])).then_inc(s_wide, 16)
            for q in range(4):
                sp.wait_ge(y_res, 4 + q + 1)
                m, ns = q // 2, slice((q % 2) * 512, (q % 2 + 1) * 512)
                sp.dma_start(out[m * P:(m + 1) * P, ns], x[:, m, ns]).then_inc(s_out, 16)
            sp.wait_ge(s_out, 64)

        @block.gpsimd
        def _(pool):
            nc.gpsimd.memset(ypad[:, :, 0:CONV_W - 1], 0.0).then_inc(zeroed, 1)
            nc.gpsimd.memset(vblk, 0.0).then_inc(zeroed, 1)
            for i in range(2):
                nc.gpsimd.memset(hcmp[i], 0.0).then_inc(zeroed, 1)
            nc.gpsimd.memset(pcmp, 0.0).then_inc(zeroed, 1)
            pool.wait_ge(s_shared, 16)
            for h, s in enumerate(slopes()):
                nc.gpsimd.tensor_scalar(alibi[:, T * h:T * (h + 1)], shared[:, 0:T], s, None, ALU.mult).then_inc(alibi_ready, 1)
            pool.wait_ge(vec_ready, 2)
            pool.wait_ge(zeroed, 5)
            pool.wait_ge(alibi_ready, NQ)
            copies = 0
            for i, (src, name) in enumerate(((KC, "kc"), (VC, "vc"))):
                pool.wait_ge(z_evac, s_idx[name] + 1)
                for g in range(NKV):
                    view = zt(src)[(g % 2) * HD:(g % 2 + 1) * HD, g // 2, :].rearrange("p (c j l) -> p l j c", c=16, j=8)
                    for l in range(2):
                        if copies:
                            pool.wait_ge(kr_ready, copies)
                        copies += 1
                        nc.gpsimd.tensor_copy(kr[i][l * HD:(l + 1) * HD, :, g * 16:(g + 1) * 16], view[:, l]).then_inc(kr_ready, 1)
                for half in range(2):
                    a = 2 * CONV_W + 16 * i + 8 * half
                    pool.wait_ge(kr_ready, copies)
                    copies += 1
                    nc.gpsimd.tensor_copy(kr[i][:, :, 64 + half:65 + half],
                                          vec_b[:, a:a + 8].rearrange("p (j o) -> p j o", o=1)).then_inc(kr_ready, 1)
        @block.tensor
        def _(pe):
            def mm3(o, lh, ll, rh, rl, start, stop):
                nc.tensor.matmul(o, lh, rh, start=start, stop=False)
                nc.tensor.matmul(o, lh, rl, start=False, stop=False)
                return nc.tensor.matmul(o, ll, rh, start=False, stop=stop)

            def w3(slot, k, n=TW):
                return (w_hi[:, slot, 0:n].rearrange("p (k c) -> p k c", k=k), w_lo[:, slot, 0:n].rearrange("p (k c) -> p k c", k=k))

            def feature_tile(slot, bank, hi, lo, ready=None):
                wh, wl = w3(slot, DC)
                for c in range(2):
                    cs = slice(c * P, (c + 1) * P)
                    for k in range(DC):
                        if ready is not None and c == 0:
                            pe.wait_ge(h_ready, ready + k + 1)
                        i = mm3(ps[:, bank, c * T:(c + 1) * T], wh[:, k, cs], wl[:, k, cs], hi[:, k, :], lo[:, k, :],
                                k == 0, k == DC - 1)
                return i

            def token_tile(slot, bank, hi, lo, a, n, cols):
                wh, wl = w3(slot, DC, DC * cols)
                for m in range(2):
                    ms = slice(m * P, (m + 1) * P)
                    for k in range(DC):
                        i = mm3(ps[:, bank, m * T:m * T + n], hi[:, k, ms], lo[:, k, ms], wh[:, k, a:a + n], wl[:, k, a:a + n],
                                k == 0, k == DC - 1)
                return i

            def narrow_tile(slot, o, a, n, cols):
                wh, wl = w3(slot, DC, DC * cols)
                for k in range(DC):
                    i = mm3(o, wh[:, k, a:a + n], wl[:, k, a:a + n], h_hi[:, k, :], h_lo[:, k, :], k == 0, k == DC - 1)
                return i

            def acc_tile(slot, hi, lo, k0, first, last):
                wh, wl = w3(slot, 2)
                for kk, m in ((0, 0), (1, 0), (0, 1), (1, 1)) if last else ((0, 0), (0, 1), (1, 0), (1, 1)):
                    ms = slice(m * P, (m + 1) * P)
                    for n in range(2):
                        ns = slice(n * 512, (n + 1) * 512)
                        i = mm3(ps[:, 2 * m + n, :], hi[:, k0 + kk, ms], lo[:, k0 + kk, ms], wh[:, kk, ns], wl[:, kk, ns],
                                first and kk == 0, last and kk == 1)
                    if last and (kk, m) == (1, 0):
                        i.then_inc(acc_ps, 1)
                return i

            def keep_warm(n, bank=7):
                for _ in range(n):
                    nc.tensor.matmul(ps[:, bank, 0:T], ident, const[:, 0:T], start=True, stop=True)

            def norm_turn(t):
                for m in range(2):
                    pe.wait_ge(xn_ready, 2 * t + m + 1)
                    for k in range(DC):
                        o = ps[:, 4 + k // 2, (k % 2) * T + m * P:(k % 2) * T + (m + 1) * P]
                        i = nc.tensor.transpose(o, xn[:, m, k * P:(k + 1) * P], ident)
                        if m and k % 2:
                            i.then_inc(xT_ready, 1)

            def spread(t, n):
                pe.wait_ge(diag_ready, t + 1)
                if n:
                    pe.wait_ge(row_ready, 2 * t + 1)
                nc.tensor.matmul(ps[:, 7, :], cst("ones"), diag[:, 4 * n:4 * n + 4, :].rearrange("p k n -> p (k n)"),
                                 start=True, stop=True).then_inc(row_ps, 1)

            pe.wait_ge(s_const, 16)
            pe.wait_ge(s_rows, 32)
            nc.tensor.transpose(ps[:, 0, 0:NA_ROWS], raw[0:NA_ROWS, RAW - 1, 0:P], ident[0:NA_ROWS, 0:NA_ROWS])
            nc.tensor.transpose(ps[:, 0, P:P + NB_ROWS], raw[0:NB_ROWS, RAW - 1, P:2 * P], ident[0:NB_ROWS, 0:NB_ROWS]).then_inc(vec_ps, 1)
            norm_turn(0)
            keep_warm(3, 3)

            pe.wait_ge(vec_ready, 2)

            def project_1(s):
                pe.wait_ge(w_ready, s + 1)
                if s >= 3:
                    pe.wait_ge(z_evac, s - 2)
                return s % RING, s % 3
            for s in range(3):
                feature_tile(*project_1(s), h_hi, h_lo, 0 if s == 0 else None).then_inc(pe_tile, 1)
            with pe.Fori(0, 2) as i:
                for j in range(3):
                    pe.wait_ge(w_ready, i * 3 + (3 + j + 1))
                    pe.wait_ge(z_evac, i * 3 + (3 + j - 2))
                    feature_tile(j, j, h_hi, h_lo).then_inc(pe_tile, 1)
            def compress(a):
                pe.wait_ge(kr_ready, 10 * (a + 1))
                for half in range(2):
                    name = f"cmp{2 * a + half}"
                    landed(pe, name)
                    wc = raw_of(name).rearrange("p (j h) -> p j h", j=8)
                    for f in range(2):
                        for j in range(8):
                            i = nc.tensor.matmul(ps[:, 4 + a, (2 * half + f) * 66:(2 * half + f + 1) * 66], wc[:, j, f * P:(f + 1) * P],
                                                 kr[a][:, j, :], start=(j == 0), stop=(j == 7))
                    i.then_inc(direct_done, 1)

            compress(0)
            pe.wait_ge(conv_ready, 1)
            for c in range(2):
                i = nc.tensor.matmul(ps[:, 3, 0:T], cst("mean"), conv[:, c, :], start=(c == 0), stop=(c == 1))
            i.then_inc(conv_mean, 1)
            compress(1)
            pe.wait_ge(convd_ready, 1)
            for c in range(2):
                i = nc.tensor.matmul(ps[:, 3, T:2 * T], cst("mean"), lnq[:, c, :], start=(c == 0), stop=(c == 1))
            i.then_inc(conv_var, 1)
            slot, bank = project_1(s_idx["g"])
            narrow_tile(slot, ps[0:G_COLS, bank, 0:T], 0, G_COLS, G_COLS).then_inc(pe_tile, 1)
            pe.wait_ge(s_w2, 16)
            pe.wait_ge(cmp_h, 2)
            for f in range(2):
                i = nc.tensor.matmul(ps[0:HD, 6, 0:P], w2[:, 0, f, :], hcmp[0][:, f, :], start=(f == 0), stop=(f == 1))
            i.then_inc(cmp2_ps, 1)
            pe.wait_ge(cmp_h, 4)
            for f in range(2):
                i = nc.tensor.matmul(ps[:, 7, 0:HD], hcmp[1][:, f, :], w2[:, 1, f, :], start=(f == 0), stop=(f == 1))
            i.then_inc(cmp2_ps, 1)
            pe.wait_ge(narrow_sb, 1)
            for m in range(2):
                i = nc.tensor.transpose(ps[:, s_idx["g"] % 3, T + m * HD:T + m * HD + G_COLS], gT[:, m * P:(m + 1) * P], ident[0:G_COLS, 0:G_COLS])
            i.then_inc(narrow_ps, 1)
            slot, bank = project_1(s_idx["vs"])
            token_tile(slot, bank, h_hi, h_lo, 0, T, T).then_inc(pe_tile, 1)

            def head_at(h):
                pair, in_pair = h // 6, h % 6
                return 3 * pair + in_pair % 3, HD * (in_pair // 3), pair

            def qT(h):
                j, b, _ = head_at(h)
                return z[b:b + HD, Q0 + j // 2, (j % 2) * T:(j % 2 + 1) * T]

            pe.wait_ge(cmp2_sb, 2)
            for m in range(2):
                for h in range(NQ):
                    _, b, _ = head_at(h)
                    g = h // 3
                    at = ((2 * m + h // 6) * 3 + h % 3) * CMP_SLOT
                    i = nc.tensor.matmul(ps[:, 4 + b // HD, at:at + CMP_SLOT], qT(h)[:, m * P:(m + 1) * P],
                                         kcmp[b:b + HD, g * CMP_SLOT:(g + 1) * CMP_SLOT], start=True, stop=True)
            i.then_inc(sc_ps, 1)

            order = [6 * p + r + 3 * e for p in range(2) for r in range(3) for e in range(2)]

            def scores(n):
                h = order[n]
                _, b, pair = head_at(h)
                for br, k_tile in enumerate((KS, KW)):
                    bank = 2 * (n % 2) + br
                    kT = z[b:b + HD, k_tile, pair * T:(pair + 1) * T]
                    nc.tensor.matmul(ps[:, bank, 0:P], qT(h)[:, 0:P], kT[:, 0:P], start=True, stop=True)
                    i = nc.tensor.matmul(ps[:, bank, P:P + T], qT(h)[:, P:T], kT, start=True, stop=True)
                i.then_inc(s_ps, 1)

            pe.wait_ge(z_evac, s_idx["vw"])
            scores(0)
            slot, bank = project_1(s_idx["vw"])
            token_tile(slot, bank, h_hi, h_lo, 0, T, T).then_inc(pe_tile, 1)
            pe.wait_ge(z_evac, s_idx["vw"] + 1)
            pe.wait_ge(lnv_ready, 1)
            scores(1)
            pe.wait_ge(pc_ready, 1)
            for c in range(3):
                for m in range(2):
                    i = nc.tensor.transpose(ps[:, 4 + c // 2, (c % 2) * T + m * P:(c % 2) * T + (m + 1) * P],
                                            pcmp[:, m, 4 * c:4 * c + 4, :].rearrange("p h n -> p (h n)"), ident)
            i.then_inc(pcT_ps, 1)

            pe.wait_ge(vblk_ready, NQ)
            pe.wait_ge(pcT_ready, 3)
            for n in range(NQ):
                h = order[n]
                j, b, _ = head_at(h)
                g = h // 3
                if n + 2 < NQ:
                    pe.wait_ge(s_sb, 4 * (n + 1))
                    scores(n + 2)
                for br in range(2):
                    pe.wait_ge(p_ready, 4 * n + 2 * (br + 1))
                    if n >= 1:
                        pe.wait_ge(pTn_ready, 2 * n + br - 1)
                    for c in range(3):
                        i = nc.tensor.transpose(ps[:, 4 + br, c * P:(c + 1) * P],
                                                probs[n % 3][:, br * 384 + c * P:br * 384 + (c + 1) * P], ident)
                    i.then_inc(pT_ps, 1)
                if n % 2 == 0 and n >= 4:
                    pe.wait_ge(o_lo, n // 2 - 1)
                bank = 6 + n // 2 % 2
                nc.tensor.matmul(ps[b:b + HD, bank, 0:T], vblk[:, h, :], pcT[:, h // 4, :], start=True, stop=False)
                for br, v_tile in enumerate((VS, VW)):
                    pe.wait_ge(pTn_ready, 2 * n + br + 1)
                    for kt in range(2):
                        lhs = z[:, v_tile, kt * T + g * HD:kt * T + (g + 1) * HD]
                        pt = turned[:, br * 384:br * 384 + T] if kt == 0 else turned[:, br * 384 + T:(br + 1) * 384]
                        i = nc.tensor.matmul(ps[b:b + HD, bank, kt * P:T], lhs, pt, start=False, stop=(br == 1 and kt == 1))
                i.then_inc(o_ps, 1)

            pe.wait_ge(clo_ready, 2)
            for i4 in range(4):
                s = s_idx[f"out{i4}"]
                pe.wait_ge(w_ready, s + 1)
                if i4 == 0:
                    pe.wait_ge(s_sb, 4 * NQ)
                if i4 >= 1:
                    pe.wait_ge(o_lo, 2 * i4)
                i = acc_tile(s % RING, mix_hi, mix_lo, 2 * i4, i4 == 0, i4 == 3)
                i.then_inc(pe_tile, 1)
            keep_warm(7)
            norm_turn(1)

            def down(slot, buf, first, last):
                return acc_tile(slot, hid_hi[buf], hid_lo[buf], 0, first, last)

            def ff1_step(st, i=0, first=False):
                s0 = s_idx[f"gate{st}"]
                for c in range(2):
                    pe.wait_ge(w_ready, i * 6 + (s0 + c + 1))
                    if c == 0 and st >= 2:
                        pe.wait_ge(hid_done, i * 2 + (st - 1))
                    feature_tile((s0 + c) % RING, 4 + 2 * (st % 2) + c, h_hi, h_lo, DC if (st, c) == (0, 0) else None).then_inc(pe_tile, 1)
                if st >= 1:
                    pe.wait_ge(w_ready, i * 6 + (s0 + 3))
                    pe.wait_ge(hidlo_done, i * 2 + st)
                    down((s0 + 2) % RING, (st - 1) % 2, first, False).then_inc(pe_tile, 1)

            pe.wait_ge(h_ready, DC + 2)
            ff1_step(0)
            pe.wait_ge(x_new, 4)
            ff1_step(1, first=True)
            with pe.Fori(0, TURNS) as i:
                ff1_step(2, i)
                ff1_step(3, i)
            ff1_step(10)
            s = s_idx["down10"]
            pe.wait_ge(w_ready, s + 1)
            pe.wait_ge(hidlo_done, FF1_STEPS)
            down(s % RING, 0, False, True).then_inc(pe_tile, 1)
            keep_warm(10)
            norm_turn(2)

            def evac_no(s):
                return 12 + s - s_idx["idx"]

            def project_2(name):
                s = s_idx[name]
                pe.wait_ge(w_ready, s + 1)
                pe.wait_ge(z_evac, evac_no(s) - 2)
                return s % RING, s % 3

            slot, bank = project_2("idx")
            wh, wl = w3(slot, DC, DC * IDX_COLS)
            for k in range(DC):
                pe.wait_ge(h_ready, 2 * DC + k + 1)
                mm3(ps[:, bank, 0:T], wh[:, k, 0:P], wl[:, k, 0:P], h_hi[:, k, :], h_lo[:, k, :], k == 0, k == DC - 1)
            narrow_tile(slot, ps[0:NB_HEADS, bank, T:2 * T], P, NB_HEADS, IDX_COLS).then_inc(pe_tile, 1)

            def feature_2(name):
                feature_tile(*project_2(name), h_hi, h_lo).then_inc(pe_tile, 1)

            rots = [0]

            def swap(src, n, name):
                pe.wait_ge(z_evac, evac_no(s_idx[name]) + 1)
                if rots[0]:
                    pe.wait_ge(rot_done, rots[0])
                nc.tensor.matmul(ps[:, 3, 0:n], shared[:, 512:640], src, start=True, stop=True).then_inc(rot_ps, 1)
                rots[0] += 1

            def index_scores(h):
                b, j = HD * (h % 2), h // 2
                if h == 0:
                    pe.wait_ge(rot_done, 2)
                    pe.wait_ge(wi_ready, 1)
                if h >= 4:
                    pe.wait_ge(rot_done, 3)
                    pe.wait_ge(relu_done, h - 3)
                q = z[b:b + HD, QI + j // 2, (j % 2) * T:(j % 2 + 1) * T]
                nc.tensor.matmul(ps[:, 4 + h % 4, 0:P], q[:, 0:P], kiT[b:b + HD, 0:P], start=True, stop=True)
                nc.tensor.matmul(ps[:, 4 + h % 4, P:P + T], q[:, P:T], kiT[b:b + HD, :], start=True, stop=True).then_inc(ix_ps, 1)

            pe.wait_ge(s_shared, 32)
            feature_2("qi0")
            pe.wait_ge(narrow_sb, 2)
            for m in range(2):
                i = nc.tensor.transpose(ps[:, 7, m * NB_HEADS:(m + 1) * NB_HEADS], wiT[:, m * P:(m + 1) * P], ident[0:NB_HEADS, 0:NB_HEADS])
            i.then_inc(narrow_ps, 1)
            feature_2("qi1")
            swap(kiT, T, "idx")
            feature_2("qa0")
            swap(z[:, QI, :], 512, "qi0")
            feature_2("qa1")
            swap(z[:, QI + 1, :], 512, "qi1")
            feature_2("ka0")
            for h in range(4):
                index_scores(h)
            swap(z[:, QA, :], 512, "qa0")
            feature_2("ka1")
            for h in range(4, 8):
                index_scores(h)
            swap(z[:, QA + 1, :], 512, "qa1")
            feature_2("qb0")
            swap(z[:, KA, :], 512, "ka0")
            feature_2("qb1")
            swap(z[:, KA + 1, :], 512, "ka1")
            feature_2("kb0")
            feature_2("kb1")
            def gate_half(h, c):
                s = s_idx[f"sg{h}"]
                if c == 0:
                    pe.wait_ge(w_ready, s + 1)
                    pe.wait_ge(z_evac, evac_no(s))
                wh, wl = w3(s % RING, DC)
                cs = slice(c * P, (c + 1) * P)
                for k in range(DC):
                    i = mm3(ps[:, 7, c * T:(c + 1) * T], wh[:, k, cs], wl[:, k, cs], h_hi[:, k, :], h_lo[:, k, :], k == 0, k == DC - 1)
                if c:
                    i.then_inc(pe_tile, 1)

            def zhead(base, h):
                b, j = HD * (h % 2), h // 2
                return z[b:b + HD, base + j // 2, (j % 2) * T:(j % 2 + 1) * T]

            def scores_a(h):
                if h == 0:
                    pe.wait_ge(z_evac, evac_no(s_idx["vb1"]) + 1)
                if h >= 2:
                    pe.wait_ge(s_sb, 4 * NQ + 2 * (h - 1))
                q, k = zhead(QA, h), zhead(KA, h)
                nc.tensor.matmul(ps[:, h % 2, 0:P], q[:, 0:P], k[:, 0:P], start=True, stop=True)
                nc.tensor.matmul(ps[:, h % 2, P:P + T], q[:, P:T], k, start=True, stop=True).then_inc(s_ps, 1)

            def scores_b(h):
                if h == 0:
                    pe.wait_ge(z_evac, evac_no(s_idx["kb1"]) + 1)
                    pe.wait_ge(rot_done, 7)
                if h >= 2:
                    pe.wait_ge(b_zm, h - 1)
                q, k = zhead(QB, h), zhead(KB, h)
                nc.tensor.matmul(ps[:, 3 + h % 2, 0:T], k[:, 0:P], q, start=True, stop=True)
                nc.tensor.matmul(ps[:, 3 + h % 2, T:T + P], k[:, P:T], q[:, P:T], start=True, stop=True).then_inc(b_z, 1)

            for name in ("va0", "va1", "vb0", "vb1"):
                if name == "vb1":
                    for h in range(2):
                        scores_b(h)
                token_tile(*project_2(name), h_hi, h_lo, 0, T, T).then_inc(pe_tile, 1)
                if name == "va1":
                    pe.wait_ge(relu_done, 8)
                    spread(0, 0)
                if name == "vb0":
                    spread(0, 1)
            pe.wait_ge(rot_done, 7)
            for h in range(2):
                scores_a(h)

            def sums_b(h):
                pe.wait_ge(b_sp, h + 1)
                if h >= 1:
                    pe.wait_ge(b_cm, h)
                nc.tensor.matmul(ps[:, 5, 0:T], cst("tri"), spb[:, 0:T], start=True, stop=False)
                nc.tensor.matmul(ps[:, 5, P:T], cst("negones"), spb[:, T:T + P], start=False, stop=True)
                nc.tensor.matmul(ps[:, 5, T:T + P], cst("tri"), spb[:, T:T + P], start=True, stop=True).then_inc(b_c, 1)

            sums_b(0)
            for h in range(NB_HEADS):
                b, j = HD * (h % 2), h // 2
                pe.wait_ge(p_ready, 4 * NQ + 2 * (h + 1))
                if h >= 1:
                    pe.wait_ge(pT_ready, h)
                for c in range(3):
                    i = nc.tensor.transpose(ps[:, 2, c * P:(c + 1) * P], sA[h % 2][:, c * P:(c + 1) * P], ident)
                i.then_inc(pT_ps, 1)
                if h >= 1:
                    sums_b(h)
                if h + 2 < NB_HEADS:
                    scores_a(h + 2)
                    scores_b(h + 2)
                gate_half(h, 0)
                if h + 1 < NB_HEADS:
                    gate_half(h, 1)
                if h % 2 == 0 and h >= 2:
                    pe.wait_ge(o_lo, 6 + h // 2)
                va = z[:, VA + h // 4, :].rearrange("p (m d) -> p m d", m=2)[:, :, (h % 4) * HD:(h % 4 + 1) * HD]
                vb = z[:, VB + h // 4, :].rearrange("p (m d) -> p m d", m=2)[:, :, (h % 4) * HD:(h % 4 + 1) * HD]
                pe.wait_ge(pT_ready, h + 1)
                nc.tensor.matmul(ps[b:b + HD, 6, 0:T], va[:, 0, :], pTA[:, 0:T], start=True, stop=False)
                nc.tensor.matmul(ps[b:b + HD, 6, P:T], va[:, 1, :], pTA[:, T:T + P], start=False, stop=True).then_inc(o_ps, 1)
                pe.wait_ge(b_att, h + 1)
                nc.tensor.matmul(ps[b:b + HD, 6, T:2 * T], vb[:, 0, :], attb[:, 0:T], start=True, stop=False)
                nc.tensor.matmul(ps[b:b + HD, 6, T + P:2 * T], vb[:, 1, :], attb[:, T:T + P], start=False, stop=True).then_inc(o_ps, 1)
            gate_half(NB_HEADS - 1, 1)

            for u, name in enumerate(("upa0", "upb0", "upa1", "upb1")):
                s = s_idx[name]
                pe.wait_ge(w_ready, s + 1)
                pe.wait_ge(o_lo, 10)
                wh, wl = w3(s % RING, 4)
                for c in range(4):
                    for k in range(4):
                        kk = 4 * (u % 2) + k
                        cs = slice(c * P, (c + 1) * P)
                        i = mm3(ps[:, 2 * u + c // 2, (c % 2) * T:(c % 2 + 1) * T], wh[:, k, cs], wl[:, k, cs], mix_hi[:, kk, :], mix_lo[:, kk, :],
                                k == 0, k == 3)
                i.then_inc(pe_tile, 1)
            for i4 in range(4):
                s = s_idx[f"o2{i4}"]
                pe.wait_ge(w_ready, s + 1)
                pe.wait_ge(m_lo, i4 // 2 + 1)
                acc_tile(s % RING, h_hi, h_lo, 2 * i4, i4 == 0, i4 == 3).then_inc(pe_tile, 1)
            pe.wait_ge(m_sum, 2)
            keep_warm(14)
            norm_turn(3)

            def ff2_step(st, i=0, first=False):
                s0 = s_idx[f"fa{st}"]
                pe.wait_ge(w_ready, i * 6 + (s0 + 1))
                if st >= 3:
                    pe.wait_ge(relu2_done, i * 3 + (st - 2))
                feature_tile(s0 % RING, 4 + st % 3, h_hi, h_lo, 3 * DC if st == 0 else None).then_inc(pe_tile, 1)
                if st >= 1:
                    pe.wait_ge(w_ready, i * 6 + (s0 + 2))
                    pe.wait_ge(hid2lo_done, i * 3 + st)
                    down((s0 + 1) % RING, (st - 1) % 3, first, False).then_inc(pe_tile, 1)

            pe.wait_ge(hf_ready, DC + 2)
            ff2_step(0)
            pe.wait_ge(y_res, 4)
            ff2_step(1, first=True)
            ff2_step(2)
            ff2_step(3)
            ff2_step(4)
            with pe.Fori(1, TURNS) as i:
                ff2_step(2, i)
                ff2_step(3, i)
                ff2_step(4, i)
            ff2_step(14)
            spread(1, 0)
            ff2_step(15)
            spread(1, 1)
            s = s_idx["fb15"]
            pe.wait_ge(w_ready, s + 1)
            pe.wait_ge(hid2lo_done, FF2_STEPS)
            down(s % RING, 15 % 3, False, True).then_inc(pe_tile, 1)

        @block.scalar
        def _(act):
            def load_ada(t, i=0):
                act.wait_ge(ada_used, i * 4 + max(t, 1))
                src = w_ada[bass.ds(i * 4 + t, 1), :, :].rearrange("a p w -> (a p) w")
                act.dma_start(ada[:, t % 2, :], src).then_inc(s_ada[t % 2], 16)

            def split(s, name, i=0):
                n = n_of[name]
                act.wait_ge(s_raw[n % RAW], i * (16 * TURN // RAW) + 16 * (n // RAW + 1))
                if s >= RING:
                    act.wait_ge(pe_tile, i * 6 + (s - RING + 1))
                w = tile_width(name)
                nc.scalar.copy(w_hi[:, s % RING, 0:w], raw[:, n % RAW, 0:w]).then_inc(hi_ready, 1)

            def after(s, i=0):
                if s + RING < NSPLIT:
                    split(s + RING, s_name[s + RING], i)

            steps = [0]

            def link(ins):
                steps[0] += 1
                ins.then_inc(astep, 1)
                act.wait_ge(astep, steps[0])

            def square(o, src, sum_):
                nc.scalar.activation(o, src, ACT.Square, accum_out=sum_).then_inc(sqy, 1)

            def squares(src, sem_a, a, sem_b, b):
                act.wait_ge(sem_a, a)
                square(sq_full, src[:, 0, :], msum[:, 0:1])
                act.wait_ge(sem_b, b)
                square(sq_half, src[:, 1, 0:512], part[:, 0:1])

            def root(t, w=2):
                act.wait_ge(ms_ready, t + 1)
                nc.scalar.activation(sqv[:, 0:w], msum[:, 0:w], ACT.Sqrt).then_inc(sq_ready, 1)

            def norm_hi(t, scale):
                for k in range(DC):
                    act.wait_ge(xT_ready, 4 * t + k // 2 + 1)
                    src = ps[:, 4 + k // 2, (k % 2) * T:(k % 2 + 1) * T]
                    nc.scalar.activation(h_hi[:, k, :], src, ACT.Identity, scale=scale(k)).then_inc(hhi_ready, 1)

            def norm_full(t, scale, bias):
                for k in range(DC):
                    act.wait_ge(xT_ready, 4 * (t + 2) + k // 2 + 1)
                    if k >= 4:
                        act.wait_ge(h_ready, 8 * (t + 2) + 2 * (k // 2) - 2)
                    src = ps[:, 4 + k // 2, (k % 2) * T:(k % 2 + 1) * T]
                    nc.scalar.activation(h_full[:, (k % 4) * T:(k % 4 + 1) * T], src, ACT.Identity, scale=scale(k),
                                         bias=bias(k)).then_inc(hf_ready, 1)

            nc.scalar.preload_act_table_set("sqrt_and_others")
            squares(x, s_x[0], 16, s_x[1], 16)
            root(0)
            nc.scalar.preload_act_table_set("sigmoid_and_others")
            split(0, s_name[0])
            act.wait_ge(vec_ready, 1)
            norm_hi(0, lambda k: col("attn_norm", k))
            for s in range(1, RING):
                split(s, s_name[s])

            def copy_out(s):
                act.wait_ge(pe_tile, s + 1)
                bank, name = s % 3, s_name[s]
                if name == "g":
                    nc.scalar.copy(gT, ps[0:G_COLS, bank, 0:T]).then_inc(narrow_sb, 1)
                elif name == "v":
                    nc.scalar.activation(z[:, V_, :], ps[:, bank, :], ACT.Sigmoid).then_inc(z_evac, 1)
                elif name[0] == "q":
                    nc.scalar.mul(z[:, z_at[name], :], ps[:, bank, :], HD ** -0.5).then_inc(z_evac, 1)
                else:
                    nc.scalar.copy(z[:, z_at[name], :], ps[:, bank, :]).then_inc(z_evac, 1)

            for s in range(9):
                copy_out(s)
                if s < 8:
                    after(s)
            act.wait_ge(direct_done, 2)
            nc.scalar.copy(xs_cmp(0), ps[:, 4, 0:264]).then_inc(cmp_sb, 1)
            after(8)
            act.wait_ge(direct_done, 4)
            nc.scalar.copy(xs_cmp(1), ps[:, 5, 0:264]).then_inc(cmp_sb, 1)
            for a in range(2):
                act.wait_ge(cmp_sum, a + 1)
                for f in range(2):
                    dst = hcmp[a][:, f, :].rearrange("p (g n) -> p g n", g=NKV)[:, :, 0:N_CMP]
                    nc.scalar.activation(dst, cmp_hidden(a)[:, f], ACT.Silu, bias=pebias[:, 2 * a + f:2 * a + f + 1]).then_inc(cmp_h, 1)
            copy_out(s_idx["g"])
            act.wait_ge(cmp2_ps, 1)
            for b in range(2):
                nc.scalar.copy(kcmp[b * HD:(b + 1) * HD, :].rearrange("p (g n) -> p g n", g=NKV),
                               ps[0:HD, 6, 0:P].rearrange("p (g n) -> p g n", g=NKV)[:, :, 0:CMP_SLOT]).then_inc(cmp2_sb, 1)
            act.wait_ge(narrow_ps, 1)
            nc.scalar.activation(gates, ps[:, s_idx["g"] % 3, T:T + 2 * HD].rearrange("p (m c) -> p m c", m=2)[:, :, 0:G_COLS].rearrange(
                "p m (h b) -> p m h b", b=3), ACT.Sigmoid).then_inc(z_evac, 1)
            act.wait_ge(lnv_ready, 1)
            nc.scalar.activation(lnv[:, 1, :], lnv[:, 0, :], ACT.Sqrt).then_inc(lnsq_ready, 1)
            after(9)
            copy_out(s_idx["vs"])
            act.wait_ge(lnn_ready, 1)
            for c in range(2):
                link(nc.scalar.activation(conv[:, c, :], lnd[:, c, :], ACT.Silu, scale=col("ln_g", c), bias=col("ln_b", c)))
                nc.scalar.copy(mix_hi[:, c, :], conv[:, c, :]).then_inc(chi_ready, 1)
            act.wait_ge(sc_sb, 1)
            nc.scalar.activation(scmp, scmp, ACT.Exp).then_inc(pc_exp, 1)

            def attn(n):
                act.wait_ge(s_sb, 4 * (n + 1))
                for br in range(2):
                    for m in range(2):
                        o = probs[n % 3][:, br * 384 + m * P:br * 384 + P + m * T]
                        c = 2 * br + m
                        nc.scalar.activation(o, o, ACT.Exp, scale=-1.0, bias=nmax[:, n % 2, c:c + 1],
                                             accum_out=psum_p[:, n % 2, c:c + 1]).then_inc(p_exp, 1)

            attn(0)
            copy_out(s_idx["vw"])

            for n in range(NQ):
                if n >= 1:
                    act.wait_ge(o_ps, n)
                for br in range(2):
                    act.wait_ge(pT_ps, 2 * n + br + 1)
                    nc.scalar.copy(turned[:, 384 * br:384 * (br + 1)], ps[:, 4 + br, 0:384]).then_inc(pTn_ready, 1)
                if n == 0:
                    attn(1)
                if n + 2 < NQ:
                    attn(n + 2)
                if n in (4, 8):
                    after(9 + n // 4)
                if n % 2:
                    j = n // 2
                    act.wait_ge(o_ps, n + 1)
                    nc.scalar.copy(mix_hi[:, 2 + j, :], ps[:, 6 + j % 2, 0:T]).then_inc(o_hi, 1)
            nc.scalar.preload_act_table_set("sqrt_and_others")
            for i4 in range(2):
                after(s_idx[f"out{i4}"])
            squares(x, x_new, 2, x_new, 3)
            root(1)
            nc.scalar.preload_act_table_set("silu_and_others")
            norm_hi(1, lambda k: col("ffn_norm", k))
            after(s_idx["out2"])
            after(s_idx["out3"])

            def ff1_step(st, i=0):
                s0 = s_idx[f"gate{st}"]
                if 2 <= st <= 9:
                    load_ada(2 * (st - 2), i)
                    load_ada(2 * (st - 2) + 1, i)
                act.wait_ge(pe_tile, i * 6 + (s0 + 1))
                if st >= 2:
                    act.wait_ge(hid_done, i * 2 + (st - 1))
                nc.scalar.activation(ff_act[st % 2], ps[:, 4 + 2 * (st % 2), :], ACT.Silu).then_inc(silu_done, 1)
                after(s0, i)
                after(s0 + 1, i)
                act.wait_ge(hid_done, i * 2 + (st + 1))
                if st >= 2:
                    act.wait_ge(pe_tile, i * 6 + (s0 - 1 + 1))
                nc.scalar.copy(hid_hi[st % 2], ff_hid[st % 2].rearrange("p (c t) -> p c t", c=2)).then_inc(hidhi_done, 1)
                if 1 <= st < FF1_STEPS - 1:
                    after(s0 + 2, i)

            ff1_step(0)
            ff1_step(1)
            act.wait_ge(s_wide, 16)
            nc.scalar.activation(c_row, c_row, ACT.Silu).then_inc(c_ready, 1)
            with act.Fori(0, TURNS) as i:
                ff1_step(2, i)
                ff1_step(3, i)
            ff1_step(10)
            nc.scalar.preload_act_table_set("sqrt_and_others")
            act.wait_ge(x_new, 6)
            square(sq_full, x[:, 0, :], msum[:, 0:1])
            act.wait_ge(xf_new, 1)
            act.wait_ge(sqy, 5)
            square(sq_full, xn[:, 0, :], msum[:, 2:3])
            act.wait_ge(x_new, 8)
            act.wait_ge(sqy, 6)
            square(sq_full, x[:, 1, :], msum[:, 1:2])
            act.wait_ge(sqy, 7)
            for n in range(2):
                act.wait_ge(xf_new, n + 2)
                square((sq_full[:, 0:512], sq_half)[n], xn[:, 1, n * 512:(n + 1) * 512], part[:, n:n + 1])
            root(2, 4)
            nc.scalar.preload_act_table_set("natural_log_exp_and_others")
            norm_full(0, lambda k: scl[:, k:k + 1], lambda k: modT[:, k:k + 1])
            after(s_idx["down9"])
            after(s_idx["down10"])

            def relu_index(h):
                act.wait_ge(ix_ps, h + 1)
                if h >= 2:
                    act.wait_ge(ix_acc, 2 * (h - 1))
                nc.scalar.activation(relu_b[h % 2], ps[:, 4 + h % 4, 0:384], ACT.Relu).then_inc(relu_done, 1)

            def copy_row(t, n):
                act.wait_ge(row_ps, 2 * t + n + 1)
                nc.scalar.copy(rows_ga[:, t, n * 512:(n + 1) * 512], ps[:, 7, :]).then_inc(row_ready, 1)

            def keep_gates(h):
                s = s_idx[f"sg{h}"]
                act.wait_ge(pe_tile, s + 1)
                dst = sgate[:, h // 4, 2 * (h % 4):2 * (h % 4) + 2, :].rearrange("p c t -> p (c t)")
                nc.scalar.copy(dst, ps[:, 7, :]).then_inc(z_evac, 1)
                after(s)

            def attn_a(h):
                act.wait_ge(s_sb, 4 * NQ + 2 * (h + 1))
                for m in range(2):
                    o = sA[h % 2][:, m * P:P + m * T]
                    nc.scalar.activation(o, o, ACT.Exp, scale=-1.0, bias=nmax[:, h % 2, m:m + 1], accum_out=psum_p[:, h % 2, m:m + 1]).then_inc(p_exp, 1)

            def attn_b1(h):
                act.wait_ge(b_abs, h + 1)
                link(nc.scalar.activation(eb, eb, ACT.Exp))
                nc.scalar.activation(eb, eb, ACT.Ln, bias=1.0).then_inc(b_ln, 1)

            for s in range(s_idx["idx"], s_idx["vb1"] + 1):
                name = s_name[s]
                act.wait_ge(pe_tile, s + 1)
                bank = s % 3
                if name == "idx":
                    nc.scalar.copy(wiT, ps[0:NB_HEADS, bank, T:2 * T]).then_inc(narrow_sb, 1)
                    nc.scalar.copy(kiT, ps[:, bank, 0:T]).then_inc(z_evac, 1)
                else:
                    at = {"qi": QI, "qa": QA, "ka": KA, "qb": QB, "kb": KB, "va": VA, "vb": VB}[name[:2]] + int(name[2])
                    scale = HD ** -0.5 if name[:2] in ("qa", "qb") else 1.0
                    nc.scalar.mul(z[:, at, :], ps[:, bank, :], scale).then_inc(z_evac, 1)
                if name == "qi0":
                    act.wait_ge(narrow_ps, 2)
                    nc.scalar.copy(wi_s, ps[:, 7, 0:2 * NB_HEADS].rearrange("p (m h) -> p m h", m=2)).then_inc(wi_ready, 1)
                if name == "vb1":
                    attn_b1(0)
                    attn_a(0)
                    attn_a(1)
                after(s)
                if name in ("va1", "vb0"):
                    copy_row(0, int(name == "vb0"))
                if name in ("ka0", "ka1"):
                    for h in range(4):
                        relu_index(h + 4 * (name == "ka1"))

            load_ada(16)
            load_ada(17)
            for h in range(NB_HEADS):
                act.wait_ge(pT_ps, 2 * NQ + h + 1)
                if h >= 1:
                    act.wait_ge(o_ps, NQ + 2 * h)
                nc.scalar.copy(pTA, ps[:, 2, 0:384]).then_inc(pT_ready, 1)
                act.wait_ge(b_cm, h + 1)
                nc.scalar.activation(attb, attb, ACT.Exp).then_inc(b_att, 1)
                if h + 1 < NB_HEADS:
                    attn_b1(h + 1)
                if h + 2 < NB_HEADS:
                    attn_a(h + 2)
                if h + 1 < NB_HEADS:
                    keep_gates(h)
                if h % 2:
                    j = h // 2
                    act.wait_ge(o_ps, NQ + 2 * (h + 1))
                    nc.scalar.copy(mix_hi[:, j::4, :], ps[:, 6, :].rearrange("p (e t) -> p e t", e=2)).then_inc(o_hi, 1)
                if h < 4:
                    load_ada(18 + h)
            keep_gates(NB_HEADS - 1)
            act.wait_ge(z_evac, 12 + s_idx["sg7"] - s_idx["idx"] + 1)

            def open_gates(u):
                g4 = sgate[:, :, 4 * u:4 * u + 4, :]
                nc.scalar.activation(g4, g4, ACT.Sigmoid).then_inc(gates_open, 1)

            open_gates(0)
            for u in range(2):
                after(s_idx[f"upa{u}"])
                if u == 0:
                    open_gates(1)
                    nc.scalar.preload_act_table_set("sqrt_and_others")
                after(s_idx[f"upb{u}"])
                act.wait_ge(m_sum, u + 1)
                nc.scalar.copy(h_hi[:, 4 * u:4 * u + 4, :], merged(u)).then_inc(m_hi, 1)
            for i4 in range(2):
                after(s_idx[f"o2{i4}"])
            def squares_y(a, s):
                act.wait_ge(acc_ps, a)
                square(sq_full, ps[:, 0:2, :].rearrange("p a n -> p (a n)"), msum[:, 0:1])
                act.wait_ge(pe_tile, s + 1)
                for n in range(2):
                    square((sq_half, sq_last)[n], ps[:, 2 + n, :], part[:, n:n + 1])

            act.wait_ge(sqy, 9)
            squares_y(3, s_idx["o23"])
            root(3)
            squares(x, y_res, 2, y_res, 3)
            root(4)
            norm_full(1, lambda k: scl[:, k:k + 1], lambda k: modT[:, 24 + k:25 + k])
            after(s_idx["o22"])
            after(s_idx["o23"])

            def ff2_step(st, i=0):
                s0 = s_idx[f"fa{st}"]
                act.wait_ge(pe_tile, i * 6 + (s0 + 1))
                if st >= 3:
                    act.wait_ge(hid2_done, i * 3 + (st - 2))
                nc.scalar.activation(ff_act[st % 3], ps[:, 4 + st % 3, :], ACT.Relu).then_inc(relu2_done, 1)
                act.wait_ge(hid2_done, i * 3 + (st + 1))
                if st >= 3:
                    act.wait_ge(pe_tile, i * 6 + (s0 - 4 + 1))
                nc.scalar.copy(hid_hi[st % 3], ff_hid[st % 3].rearrange("p (c t) -> p c t", c=2)).then_inc(hid2hi_done, 1)
                after(s0, i)
                if st >= 1:
                    after(s0 + 1, i)

            for st in range(5):
                ff2_step(st)
                if st < 2:
                    load_ada(22 + st)
            with act.Fori(1, TURNS) as i:
                ff2_step(2, i)
                ff2_step(3, i)
                ff2_step(4, i)
            ff2_step(14)
            copy_row(1, 0)
            ff2_step(15)
            copy_row(1, 1)
            squares_y(4, s_idx["fb15"])
            root(5)

        @block.vector
        def _(dve):
            V = nc.vector
            steps = [0]

            def link(ins):
                steps[0] += 1
                ins.then_inc(dstep, 1)
                dve.wait_ge(dstep, steps[0])

            def split(s, name, i=0):
                dve.wait_ge(hi_ready, i * 6 + (s + 1))
                w = tile_width(name)
                V.tensor_tensor(w_lo[:, s % RING, 0:w], raw[:, n_of[name] % RAW, 0:w],
                                w_hi[:, s % RING, 0:w].bitcast(F32), ALU.subtract).then_inc(w_ready, 1)

            def after(s, i=0):
                if s + RING < NSPLIT:
                    split(s + RING, s_name[s + RING], i)

            roots = [0]

            def rstd(w=2):
                roots[0] += 1
                dve.wait_ge(sq_ready, roots[0])
                link(V.reciprocal(rst[:, 0:w], sqv[:, 0:w]))
                newton(rst[:, 0:w], msum[:, 0:w], nwt[:, 0:w])

            def newton(r, v, t):
                link(V.scalar_tensor_tensor(t, r, -0.5, r, ALU.mult, ALU.mult))
                link(V.tensor_tensor(t, t, v, ALU.mult))
                link(V.scalar_tensor_tensor(r, t, 1.5, r, ALU.add, ALU.mult))

            def mean_squares(src, done):
                link(V.tensor_tensor_reduce(sq_last, src, src, 1.0, 0.0, ALU.mult, ALU.add, part[:, 1:2]))
                dve.wait_ge(sqy, done)
                link(V.tensor_tensor(msum[:, 1:2], part[:, 0:1], part[:, 1:2], ALU.add))
                V.tensor_scalar(msum[:, 0:2], msum[:, 0:2], 1.0 / D, EPS, ALU.mult, ALU.add).then_inc(ms_ready, 1)

            def norm_x(done):
                mean_squares(x[:, 1, 512:1024], done)
                rstd()
                norm_scale()

            def norm_scale():
                for m in range(2):
                    V.tensor_scalar(xn[:, m, :], x[:, m, :], rst[:, m:m + 1], None, ALU.mult).then_inc(xn_ready, 1)

            def norm_lo(t, scale):
                for k in range(DC):
                    src = ps[:, 4 + k // 2, (k % 2) * T:(k % 2 + 1) * T]
                    dve.wait_ge(hhi_ready, 8 * t + 2 * (k // 2) + 2)
                    V.scalar_tensor_tensor(h_lo[:, k, :], src, scale(k), h_hi[:, k, :].bitcast(F32), ALU.mult, ALU.subtract).then_inc(h_ready, 1)

            def norm_split(t):
                for k in range(0, DC, 2):
                    dve.wait_ge(hf_ready, 8 * t + k + 2)
                    full = h_full[:, (k % 4) * T:(k % 4 + 2) * T].rearrange("p (a t) -> p a t", a=2)
                    link(V.tensor_copy(h_hi[:, k:k + 2, :], full))
                    V.tensor_tensor(h_lo[:, k:k + 2, :], full, h_hi[:, k:k + 2, :].bitcast(F32), ALU.subtract).then_inc(h_ready, 2)

            def add_out(s, a):
                for q in range(4):
                    if q == 0:
                        dve.wait_ge(acc_ps, a)
                    if q == 2:
                        dve.wait_ge(pe_tile, s + 1)
                    xs = x[:, q // 2, (q % 2) * 512:(q % 2 + 1) * 512]
                    V.tensor_tensor(xs, xs, ps[:, q, :], ALU.add).then_inc(x_new, 1)
                    if q % 2:
                        yield q // 2

            def diagonals(v):
                for k in range(DC):
                    i = V.tensor_scalar(diag[:, k, :], ident, v[:, k:k + 1], None, ALU.mult)
                i.then_inc(diag_ready, 1)

            for m in range(2):
                dve.wait_ge(s_x[m], 16)
            norm_x(2)
            dve.wait_ge(vec_ps, 1)
            V.tensor_copy(vec[:, :], ps[:, 0, 0:NA_ROWS]).then_inc(vec_ready, 1)
            V.tensor_copy(vec_b[:, :], ps[:, 0, P:P + NB_ROWS]).then_inc(vec_ready, 1)
            split(0, s_name[0])
            dve.wait_ge(vec_ready, 2)
            norm_lo(0, lambda k: col("attn_norm", k))
            for s in range(1, RING):
                split(s, s_name[s])

            taps = [(w, c) for w in range(CONV_W) for c in range(2)]
            base = steps[0]
            def tap(w, c):
                src, wcol = ypad[:, c, w:w + T], vec_b[:, 2 * w + c:2 * w + c + 1]
                if w == 0:
                    i = V.tensor_scalar(conv[:, c, :], src, wcol, col("conv_b", c), ALU.mult, ALU.add)
                else:
                    dve.wait_ge(dstep, steps[0] - 1)
                    i = V.scalar_tensor_tensor(conv[:, c, :], src, wcol, conv[:, c, :], ALU.mult, ALU.add)
                if (w, c) == taps[-1]:
                    i.then_inc(conv_ready, 1)
                else:
                    steps[0] += 1
                    i.then_inc(dstep, 1)

            behind = 8
            for s in range(8):
                after(s)
                if s == s_idx["v"]:
                    dve.wait_ge(z_evac, s + 1)
                    dve.wait_ge(zeroed, 1)
                    link(V.tensor_tensor(ypad[:, :, CONV_W - 1:], zt(U), zt(V_), ALU.mult))
                if s >= s_idx["v"]:
                    a = behind * (s - s_idx["v"])
                    for w, c in taps[a:a + behind]:
                        tap(w, c)
            for w, c in taps[behind * (8 - s_idx["v"]):]:
                tap(w, c)

            def compressor_sum(a):
                dve.wait_ge(cmp_sb, a + 1)
                v = xs_cmp(a).rearrange("p (l f n) -> p l f n", l=2, f=2)
                link(V.tensor_tensor(pebias[:, 2 * a:2 * a + 2].rearrange("p (f o) -> p f o", o=1), v[:, 0, :, 64:65], v[:, 1, :, 65:66], ALU.add))
                for f in range(2):
                    lo = v[:, 0, f, 0:64].rearrange("p (g c) -> p g c", g=NKV)[:, :, 0:15]
                    hi = v[:, 1, f, 0:64].rearrange("p (g c) -> p g c", g=NKV)[:, :, 1:16]
                    i = V.tensor_tensor(cmp_hidden(a)[:, f], lo, hi, ALU.add)
                    if f == 0:
                        link(i)
                i.then_inc(cmp_sum, 1)

            compressor_sum(0)
            dve.wait_ge(conv_ready, 1)
            dve.wait_ge(conv_mean, 1)
            link(V.tensor_tensor(lnd, conv, ps[:, 3:4, 0:T].to_broadcast([P, 2, T]), ALU.subtract))
            V.tensor_tensor(lnq, lnd, lnd, ALU.mult).then_inc(convd_ready, 1)
            after(8)
            compressor_sum(1)
            dve.wait_ge(conv_var, 1)
            V.tensor_scalar(lnv[:, 0, :], ps[:, 3, T:2 * T], EPS, None, ALU.add).then_inc(lnv_ready, 1)
            dve.wait_ge(zeroed, 2)
            dve.wait_ge(cmp2_ps, 2)
            for h in range(NQ):
                g = h // 3
                V.tensor_copy(vblk[32 * (h % 4):32 * (h % 4 + 1), h, :], ps[32 * g:32 * (g + 1), 7, 0:HD]).then_inc(vblk_ready, 1)
            dve.wait_ge(lnsq_ready, 1)
            link(V.reciprocal(lnq[:, 0, :], lnv[:, 1, :]))
            newton(lnq[:, 0, :], lnv[:, 0, :], lnq[:, 1, :])
            V.tensor_tensor(lnd, lnd, lnq[:, 0:1, :].to_broadcast([P, 2, T]), ALU.mult).then_inc(lnn_ready, 1)
            after(9)
            order = [6 * p + r + 3 * e for p in range(2) for r in range(3) for e in range(2)]

            def masked(n):
                h = order[n]
                dve.wait_ge(s_ps, n + 1)
                dve.wait_ge(alibi_ready, NQ)
                for br in range(2):
                    for m in range(2):
                        at = br * 384
                        c = 2 * br + m
                        bias = alibi[:, T * h:T * (h + 1)] if m else alibi[:, T * h + P:T * (h + 1)]
                        V.tensor_tensor_reduce(probs[n % 3][:, at + m * P:at + P + m * T], ps[:, 2 * (n % 2) + br, m * P:P + m * T], bias,
                                               -1.0, 3.0e38, ALU.add, ALU.min, nmax[:, n % 2, c:c + 1]).then_inc(s_sb, 1)

            def normal(n):
                h = order[n]
                dve.wait_ge(p_exp, 4 * (n + 1))
                link(V.reciprocal(coef[:, n % 2, :], psum_p[:, n % 2, :]))
                cf = coef[:, n % 2, :].rearrange("p (b m) -> p b m", b=2)
                gt = gates[:, :, h, 1:3].rearrange("p m b -> p b m")
                link(V.tensor_tensor(cf, cf, gt, ALU.mult))
                for br in range(2):
                    for m in range(2):
                        o = probs[n % 3][:, br * 384 + m * P:br * 384 + P + m * T]
                        V.tensor_scalar(o, o, coef[:, n % 2, 2 * br + m:2 * br + m + 1], None, ALU.mult).then_inc(p_ready, 1)

            def nsa_lo(j):
                dve.wait_ge(o_hi, j + 1)
                V.tensor_tensor(mix_lo[:, 2 + j, :], ps[:, 6 + j % 2, 0:T], mix_hi[:, 2 + j, :].bitcast(F32), ALU.subtract).then_inc(o_lo, 1)

            dve.wait_ge(sc_ps, 1)
            for e in range(2):
                half = lambda a: a.rearrange("p (a e n) -> p a e n", a=4, e=2)[:, :, e, :]
                link(V.tensor_tensor(half(scmp_flat), ps[:, 4 + e, 0:192].rearrange("p (a n) -> p a n", a=4),
                                     half(shared[:, 256:640]), ALU.add))
            mx, sm = st24
            link(V.tensor_reduce(mx, scmp, AX.X, ALU.max))
            link(V.tensor_scalar(mx, mx, -1.0e20, None, ALU.max))
            V.tensor_tensor(scmp, scmp, wide(mx), ALU.subtract).then_inc(sc_sb, 1)
            masked(0)
            for c in range(2):
                dve.wait_ge(chi_ready, c + 1)
                V.tensor_tensor(mix_lo[:, c, :], conv[:, c, :], mix_hi[:, c, :].bitcast(F32), ALU.subtract).then_inc(clo_ready, 1)
            dve.wait_ge(pc_exp, 1)
            link(V.tensor_reduce(sm, scmp, AX.X, ALU.add))
            link(V.tensor_scalar(sm, sm, 1.0e-30, None, ALU.max))
            link(V.reciprocal(mx, sm))
            dve.wait_ge(z_evac, s_idx["g"] + 1)
            link(V.tensor_tensor(mx, mx, gates[:, :, :, 0], ALU.mult))
            dve.wait_ge(zeroed, 5)
            V.tensor_tensor(pcmp[:, :, :, 0:CMP_SLOT], scmp, wide(mx), ALU.mult).then_inc(pc_ready, 1)
            normal(0)

            dve.wait_ge(pcT_ps, 1)
            for c in range(3):
                V.tensor_copy(pcT[:, c, :], ps[:, 4 + c // 2, (c % 2) * T:(c % 2 + 1) * T]).then_inc(pcT_ready, 1)
            masked(1)
            for n in range(NQ):
                if n + 2 < NQ:
                    if n >= 1:
                        dve.wait_ge(pT_ps, 2 * n)
                    masked(n + 2)
                if n + 1 < NQ:
                    normal(n + 1)
                if n % 2 == 0 and n >= 2:
                    nsa_lo(n // 2 - 1)
                if n in (5, 9):
                    after(9 + n // 4)
            nsa_lo(5)

            def sum_ada(t, i=0, halves=(0, 1)):
                dve.wait_ge(s_ada[t % 2], i * 32 + 16 * (t // 2 + 1))
                if t == 0:
                    dve.wait_ge(mod_kept, i + 1)
                for e in halves:
                    w = ada[:, t % 2, e * D:(e + 1) * D]
                    at = 2 * t + e
                    sum_ = modT[:, at:at + 1] if t >= 16 else mod_turn[:, at:at + 1]
                    ins = V.tensor_tensor_reduce(w, w, c_row, 1.0, 0.0, ALU.mult, ALU.add, sum_)
                if halves[-1]:
                    ins.then_inc(ada_used, 1)
                if t == 3:
                    dve.wait_ge(ada_used, i * 4 + 5)
                    V.tensor_copy(modT[:, bass.ds(i * 8, 8)], mod_turn).then_inc(mod_kept, 1)

            def modulation(a, n, tiles):
                dve.wait_ge(ada_used, tiles + 1)
                b = VEC_A["b_ada"][0]
                link(V.tensor_tensor(modT[:, a:a + n], modT[:, a:a + n], vec[:, b + a:b + a + n], ALU.add))

            for i4 in range(2):
                after(s_idx[f"out{i4}"])
            list(add_out(s_idx["out3"], 1))
            dve.wait_ge(x_new, 4)
            norm_x(4)
            norm_lo(1, lambda k: col("ffn_norm", k))
            after(s_idx["out2"])
            after(s_idx["out3"])

            def ff1_step(st, i=0):
                s0 = s_idx[f"gate{st}"]
                after(s0, i)
                dve.wait_ge(pe_tile, i * 6 + (s0 + 2))
                dve.wait_ge(silu_done, i * 2 + (st + 1))
                if st >= 2:
                    dve.wait_ge(hidlo_done, i * 2 + (st - 1))
                V.tensor_tensor(ff_hid[st % 2], ff_act[st % 2], ps[:, 5 + 2 * (st % 2), :], ALU.mult).then_inc(hid_done, 1)
                after(s0 + 1, i)
                dve.wait_ge(hidhi_done, i * 2 + (st + 1))
                V.tensor_tensor(hid_lo[st % 2], ff_hid[st % 2].rearrange("p (c t) -> p c t", c=2),
                                hid_hi[st % 2].bitcast(F32), ALU.subtract).then_inc(hidlo_done, 1)
                if 1 <= st < FF1_STEPS - 1:
                    after(s0 + 2, i)
                if 2 <= st <= 9:
                    sum_ada(2 * (st - 2), i)
                    sum_ada(2 * (st - 2) + 1, i)

            ff1_step(0)
            ff1_step(1)
            dve.wait_ge(c_ready, 1)
            V.memset(mod_turn[:, 0:4], 0.0).then_inc(ada_used, 1)
            V.memset(mod_turn[:, 4:8], 0.0).then_inc(mod_kept, 1)
            dve.wait_ge(ada_used, 1)
            with dve.Fori(0, TURNS) as i:
                ff1_step(2, i)
                ff1_step(3, i)
            def modulated(g, i):
                link(V.tensor_scalar(scl, modT[:, i:i + 8], 1.0, None, ALU.add))
                link(V.tensor_tensor(scl, scl, vec[:, VEC_A[g][0]:VEC_A[g][0] + 8], ALU.mult))

            dve.wait_ge(mod_kept, TURNS + 1)
            modulation(0, 32, 16)
            modulated("g_pre_mix", 8)
            ff1_step(10)
            for m in add_out(s_idx["down10"], 2):
                dve.wait_ge(x_new, 6 + 2 * m)
                for n in range(m + 1):
                    ns = slice(n * 512, (n + 1) * 512) if m else slice(0, D)
                    V.tensor_tensor(xn[:, m, ns], x[:, m, ns], final_row[:, ns], ALU.mult).then_inc(xf_new, 1)
            dve.wait_ge(sqy, 7)
            link(V.tensor_scalar(msum[:, 0:2], msum[:, 0:2], 1.0 / D, EPS, ALU.mult, ALU.add))
            link(V.tensor_scalar(part[:, 2:4], msum[:, 0:2], EPS, None, ALU.mult))
            dve.wait_ge(sqy, 9)
            link(V.tensor_tensor(msum[:, 3:4], part[:, 0:1], part[:, 1:2], ALU.add))
            V.scalar_tensor_tensor(msum[:, 2:4], msum[:, 2:4], 1.0 / D, part[:, 2:4], ALU.mult, ALU.add).then_inc(ms_ready, 1)
            rstd(4)
            for m in range(2):
                V.tensor_scalar(xn[:, m, :], xn[:, m, :], rst[:, 2 + m:3 + m], None, ALU.mult).then_inc(xn_ready, 1)
            norm_split(0)
            after(s_idx["down9"])
            after(s_idx["down10"])
            for m in range(2):
                V.scalar_tensor_tensor(x[:, m, :], x[:, m, :], rst[:, m:m + 1], final_row, ALU.mult, ALU.mult).then_inc(x_new, 1)

            cos, sin = shared[:, 0:T], shared[:, T:2 * T]
            rots = [0]

            def rotate(view, groups):
                n = groups * T
                dve.wait_ge(rot_ps, rots[0] + 1)
                t = rtmp[:, 0:n].rearrange("p (g t) -> p g t", g=groups)
                s = ps[:, 3, 0:n].rearrange("p (g t) -> p g t", g=groups)
                v = view.rearrange("p (g t) -> p g t", g=groups)
                bc = lambda a: a.rearrange("p (g t) -> p g t", g=1).to_broadcast([P, groups, T])
                link(V.tensor_tensor(t, s, bc(sin), ALU.mult))
                link(V.tensor_tensor(v, v, bc(cos), ALU.mult))
                V.tensor_tensor(v, v, t, ALU.add).then_inc(rot_done, 1)
                rots[0] += 1

            def index_sum(h):
                dve.wait_ge(relu_done, h + 1)
                if h >= 1:
                    dve.wait_ge(ix_acc, 2 * h)
                for m in range(2):
                    o = isc[:, m * P:P + m * T]
                    base_ = (cst("causal") if m else cst("causal")[:, P:T]) if h == 0 else o
                    V.scalar_tensor_tensor(o, relu_b[h % 2][:, m * P:P + m * T], wi_s[:, m, h:h + 1], base_,
                                           ALU.mult, ALU.add).then_inc(ix_acc, 1)

            def take8(m):
                o = isc[:, m * P:P + m * T]
                link(V.max(top8, o))
                link(V.match_replace(o, top8, o, TAKEN))

            def post_gain(g, i):
                link(V.tensor_tensor(gcol, modT[:, i:i + 8], vec[:, VEC_A[g][0]:VEC_A[g][0] + 8], ALU.mult))
                diagonals(gcol)

            takes = [m for _ in range(TOPK // 8) for m in range(2)]
            def key_bias():
                link(V.tensor_scalar(abias, isc, TAKEN, NEG, ALU.not_equal, ALU.mult))
                for m in range(2):
                    o = abias[:, m * P:P + m * T]
                    V.tensor_tensor(o, o, cst("causal") if m else cst("causal")[:, P:T], ALU.add).then_inc(bias_ready, 1)
                dve.wait_ge(bias_ready, 2)

            def a_masked(h):
                dve.wait_ge(s_ps, NQ + h + 1)
                for m in range(2):
                    V.tensor_tensor_reduce(sA[h % 2][:, m * P:P + m * T], ps[:, h % 2, m * P:P + m * T], abias[:, m * P:P + m * T],
                                           -1.0, 3.0e38, ALU.add, ALU.min, nmax[:, h % 2, m:m + 1]).then_inc(s_sb, 1)

            def diag_masked(dst, bank, inc):
                two = lambda a: a.rearrange("p (k n) -> p k n", n=P)[:, 0:3:2, :]
                link(V.tensor_tensor(two(dst), two(ps[:, bank, 0:384]), cst("strict").rearrange("p (o n) -> p o n", o=1).to_broadcast([P, 2, P]), ALU.add))
                V.tensor_copy(dst[:, P:T], ps[:, bank, P:T]).then_inc(inc, 1)

            def b_front(h):
                dve.wait_ge(b_z, h + 1)
                diag_masked(zm[h % 2], 3 + h % 2, b_zm)
                dve.wait_ge(b_zm, h + 1)
                if h >= 1:
                    dve.wait_ge(b_sp, h)
                V.scalar_tensor_tensor(eb, zm[h % 2], -1.0, zm[h % 2], ALU.mult, ALU.min).then_inc(b_abs, 1)

            def softplus(h):
                dve.wait_ge(b_ln, h + 1)
                if h >= 1:
                    dve.wait_ge(b_c, h)
                V.scalar_tensor_tensor(spb, zm[h % 2], 0.0, eb, ALU.max, ALU.add).then_inc(b_sp, 1)

            def a_normal(h):
                dve.wait_ge(p_exp, 4 * NQ + 2 * (h + 1))
                link(V.reciprocal(coef[:, h % 2, 0:2], psum_p[:, h % 2, 0:2]))
                for m in range(2):
                    o = sA[h % 2][:, m * P:P + m * T]
                    V.tensor_scalar(o, o, coef[:, h % 2, m:m + 1], None, ALU.mult).then_inc(p_ready, 1)

            def mixed_lo(j):
                dve.wait_ge(o_hi, 6 + j + 1)
                V.tensor_tensor(mix_lo[:, j::4, :], ps[:, 6, :].rearrange("p (e t) -> p e t", e=2),
                                mix_hi[:, j::4, :].bitcast(F32), ALU.subtract).then_inc(o_lo, 1)

            rotated = {"qa0": (kiT, 1), "qa1": (z[:, QI, :], 2), "ka0": (z[:, QI + 1, :], 2), "ka1": (z[:, QA, :], 2),
                       "qb0": (z[:, QA + 1, :], 2), "qb1": (z[:, KA, :], 2), "kb0": (z[:, KA + 1, :], 2)}
            for s in range(s_idx["idx"], s_idx["vb1"] + 1):
                name = s_name[s]
                if name in rotated:
                    rotate(*rotated[name])
                if name == "vb1":
                    b_front(0)
                    softplus(0)
                    a_masked(0)
                    a_masked(1)
                    a_normal(0)
                after(s)
                if name == "va1":
                    key_bias()
                if name in ("ka0", "ka1"):
                    for h in range(4):
                        index_sum(h + 4 * (name == "ka1"))
                if name == "ka1":
                    dve.wait_ge(ix_acc, 16)
                if name == "kb1":
                    post_gain("g_post_mix", 16)
                if s > s_idx["ka1"]:
                    for m in takes[:2 if name == "qb0" else 4]:
                        take8(m)
                    takes = takes[2 if name == "qb0" else 4:]
            assert not takes
            for h in range(NB_HEADS):
                dve.wait_ge(b_c, h + 1)
                if h >= 1:
                    dve.wait_ge(o_ps, NQ + 2 * h)
                V.tensor_tensor(attb, ps[:, 5, 0:384], zm[h % 2], ALU.add).then_inc(b_cm, 1)
                if h % 2 == 0 and h >= 2:
                    mixed_lo(h // 2 - 1)
                if h + 1 < NB_HEADS:
                    b_front(h + 1)
                if h + 2 < NB_HEADS:
                    dve.wait_ge(pT_ps, 2 * NQ + h + 1)
                    a_masked(h + 2)
                if h < 4:
                    sum_ada(16 + h, halves=(0,))
                if h + 1 < NB_HEADS:
                    softplus(h + 1)
                    a_normal(h + 1)
                if h < 4:
                    sum_ada(16 + h, halves=(1,))
                if h == NB_HEADS - 1:
                    mixed_lo(3)
                after(s_idx[f"sg{h}"])

            for u in range(2):
                after(s_idx[f"upa{u}"])
                dve.wait_ge(pe_tile, s_idx[f"upa{u}"] + 1)
                dve.wait_ge(gates_open, u + 1)
                ga, gb = sgate[:, 0, 4 * u:4 * u + 4, :], sgate[:, 1, 4 * u:4 * u + 4, :]
                pa = ps[:, 4 * u:4 * u + 2, :].rearrange("p a (c t) -> p (a c) t", c=2)
                pb = ps[:, 4 * u + 2:4 * u + 4, :].rearrange("p a (c t) -> p (a c) t", c=2)
                V.tensor_tensor(ga, pa, ga, ALU.mult).then_inc(up_a, 1)
                after(s_idx[f"upb{u}"])
                dve.wait_ge(pe_tile, s_idx[f"upb{u}"] + 1)
                link(V.tensor_tensor(gb, pb, gb, ALU.mult))
                dve.wait_ge(up_a, u + 1)
                V.tensor_tensor(merged(u), ga, gb, ALU.add).then_inc(m_sum, 1)
                dve.wait_ge(m_hi, u + 1)
                V.tensor_tensor(h_lo[:, 4 * u:4 * u + 4, :], merged(u), h_hi[:, 4 * u:4 * u + 4, :].bitcast(F32), ALU.subtract).then_inc(m_lo, 1)
            for i4 in range(2):
                after(s_idx[f"o2{i4}"])

            def post_norm(t, done):
                dve.wait_ge(row_ready, 2 * t + 2)
                for q in range(4):
                    dve.wait_ge(sqy, done - 2 + max(q - 1, 0))
                    V.tensor_tensor(y_norm[:, q, :], ps[:, q, :], rows_ga[:, t, (q % 2) * 512:(q % 2 + 1) * 512], ALU.mult).then_inc(y_gain, 1)
                link(V.tensor_tensor(msum[:, 1:2], part[:, 0:1], part[:, 1:2], ALU.add))
                V.tensor_scalar(msum[:, 0:2], msum[:, 0:2], 1.0 / D, EPS, ALU.mult, ALU.add).then_inc(ms_ready, 1)
                rstd()
                dve.wait_ge(y_gain, 4 * (t + 1))
                for q in range(4):
                    xs = x[:, q // 2, (q % 2) * 512:(q % 2 + 1) * 512]
                    V.scalar_tensor_tensor(xs, y_norm[:, q, :], rst[:, q // 2:q // 2 + 1], xs, ALU.mult, ALU.add).then_inc(y_res, 1)
                dve.wait_ge(y_res, 4 * (t + 1))

            modulation(32, 8, 20)
            modulated("g_pre_ffn", 32)
            dve.wait_ge(x_new, 10)
            post_norm(0, 12)
            norm_x(14)
            norm_split(1)
            after(s_idx["o22"])
            after(s_idx["o23"])
            def ff2_step(st, i=0):
                s0 = s_idx[f"fa{st}"]
                dve.wait_ge(relu2_done, i * 3 + (st + 1))
                if st >= 3:
                    dve.wait_ge(hid2lo_done, i * 3 + (st - 2))
                V.tensor_tensor(ff_hid[st % 3], ff_act[st % 3], ff_act[st % 3], ALU.mult).then_inc(hid2_done, 1)
                dve.wait_ge(hid2hi_done, i * 3 + (st + 1))
                V.tensor_tensor(hid_lo[st % 3], ff_hid[st % 3].rearrange("p (c t) -> p c t", c=2),
                                hid_hi[st % 3].bitcast(F32), ALU.subtract).then_inc(hid2lo_done, 1)
                after(s0, i)
                if st >= 1:
                    after(s0 + 1, i)

            for st in range(5):
                ff2_step(st)
                if st < 4:
                    sum_ada(20 + st)
            modulation(40, 8, 24)
            post_gain("g_post_ffn", 40)
            with dve.Fori(1, TURNS) as i:
                ff2_step(2, i)
                ff2_step(3, i)
                ff2_step(4, i)
            ff2_step(14)
            ff2_step(15)
            post_norm(1, 17)


def _cols(w):
    k, n = w.shape[0] // 128, w.shape[1] // 256
    return w.reshape(k, 128, n, 256).transpose(2, 1, 0, 3).reshape(n, 128, k * 256)


def _rows(w):
    return w.reshape(-1, 2, 128, 1024).transpose(0, 2, 1, 3).reshape(-1, 128, 2048)


def _narrow(w):
    return np.ascontiguousarray(w.reshape(8, 128, -1).transpose(1, 0, 2).reshape(128, -1))


def _pair_heads(w, axis):
    s = w.shape
    shape = s[:axis] + (2, 2, 3, 64) + s[axis + 1:]
    order = list(range(len(shape)))
    order[axis + 1], order[axis + 2] = axis + 2, axis + 1
    return w.reshape(shape).transpose(order).reshape(s)


def _layout(a):
    f = lambda n: np.asarray(a[n])[0]
    w_in, w_out, gu, down = f("w_in"), f("w_out"), f("w_gate_up"), f("w_down")
    q = _pair_heads(w_in[:, 512:1280], 1)
    kv = lambda i: w_in[:, 1280 + 256 * i:1536 + 256 * i]
    first = _cols(np.concatenate([w_in[:, 0:512], kv(0), kv(1), q, kv(2), kv(4), kv(3), kv(5)], 1))
    w_g = _narrow(w_in[:, 2816:2852])
    cmp1 = [f(n).reshape(2, 8, 128, 256).transpose(0, 2, 1, 3).reshape(2, 128, 2048) for n in ("cmp_k_w1", "cmp_v_w1")]
    out1 = np.concatenate([w_out[:256], _pair_heads(w_out[256:], 0)], 0)
    gate, up, dn = _cols(gu[:, :2816]), _cols(gu[:, 2816:]), _rows(down)
    ffn1 = [gate[0:1], up[0:1]]
    for i in range(1, FF1_STEPS):
        ffn1 += [gate[i:i + 1], up[i:i + 1], dn[i - 1:i]]
    ffn1 += [dn[-1:]]
    w2 = f("w_in_2")
    qa, ka, va, qb, kb, vb, qi = (w2[:, 512 * i:512 * (i + 1)] for i in range(7))
    ki, wi, sg = w2[:, 3584:3648], w2[:, 3648:3656], w2[:, 3656:]
    w_idx = _narrow(np.concatenate([ki, ki, wi], 1))
    ups = [f(n).reshape(4, 128, 2, 512).transpose(2, 1, 0, 3).reshape(2, 128, 2048) for n in ("w_up_a_2", "w_up_b_2")]
    fa, fb = _cols(f("w_ff1_2")), _rows(f("w_ff2_2"))
    ffn2 = [fa[0:1]]
    for i in range(1, FF2_STEPS):
        ffn2 += [fa[i:i + 1], fb[i - 1:i]]
    ffn2 += [fb[-1:]]
    stream = [first[:-1], *cmp1, first[-1:], _rows(out1), *ffn1,
              _cols(np.concatenate([qi, qa, ka, qb, kb, va, vb, sg], 1)),
              ups[0][0:1], ups[1][0:1], ups[0][1:2], ups[1][1:2], _rows(f("w_out_2")), *ffn2]
    wts = np.concatenate(stream, 0)
    vecs = {"attn_norm": f("attn_norm"), "ffn_norm": f("ffn_norm"), "g_pre_mix": f("g_pre_mix_2"), "g_pre_ffn": f("g_pre_ffn_2"),
            "b_ada": f("b_ada_2"), "conv_b": f("conv_b"), "ln_g": f("conv_ln_g"), "ln_b": f("conv_ln_b"),
            "g_post_mix": f("g_post_mix_2"), "g_post_ffn": f("g_post_ffn_2")}
    rows_a = np.concatenate([vecs[n].reshape(-1, 128) for n in VEC_A], 0)
    rows_b = np.concatenate([f("conv_w").reshape(-1, 128), f("cmp_k_pe").reshape(-1, 128), f("cmp_v_pe").reshape(-1, 128)], 0)
    w2c = np.concatenate([f(n).reshape(2, 128, 64).transpose(1, 0, 2).reshape(128, 128) for n in ("cmp_k_w2", "cmp_v_w2")], 1)
    w_ada = f("w_ada_2").reshape(1024, 24, 2, 128).transpose(1, 3, 2, 0).reshape(24, 128, 2048)
    rows_wide = np.concatenate([np.asarray(a["final_norm"]).reshape(-1), f("c_2").reshape(-1)]).reshape(1, -1)
    return {"x": np.asarray(a["x"])[0], "wts": wts, "w_ada": w_ada, "w_g": w_g, "w_idx": w_idx, "rows_a": rows_a, "rows_b": rows_b, "rows_wide": rows_wide, "cmp_w2": w2c}


def _constants():
    p, t = np.arange(128), np.arange(256)
    c = {"ident": np.eye(128), "tri": -(p[:, None] >= p[None, :]).astype(np.float32), "negones": -np.ones((128, 128)),
         "strict": np.where(p[:, None] < p[None, :], 0.0, NEG), "mean": np.full((128, 128), 1.0 / 256), "ones": np.ones((128, 128))}
    dist = t[None, :] - (p[:, None] + 128)
    c["causal"] = np.where(dist <= 0, 0.0, NEG)
    const = np.concatenate([c[n] for n in CONST], 1).astype(np.float32)
    sl = np.asarray(slopes())
    tt = np.arange(256).reshape(2, 128)
    n = np.arange(16)
    center, end = n * 16 + 15.5, n * 16 + 31
    valid = (end[None, None, :] <= tt[:, :, None]) & (n < 15)
    cb = np.where(valid[:, :, None, :], -sl[None, None, :, None] * (tt[:, :, None, None] - center), NEG)
    shared_1 = np.concatenate([np.where(dist <= 0, dist, -1.0e33), cb.transpose(1, 0, 2, 3).reshape(128, -1)], 1).astype(np.float32)
    ang = np.arange(256, dtype=np.float32)[:, None] * (500000.0 ** (-np.arange(0, 16, 2, dtype=np.float32) / 16)).astype(np.float32)
    cos, sin, swap = np.ones((128, 256)), np.zeros((128, 256)), np.zeros((128, 128))
    for b in (0, 64):
        for i in range(8):
            cos[b + i] = cos[b + 8 + i] = np.cos(ang[:, i])
            sin[b + i] = sin[b + 8 + i] = np.sin(ang[:, i])
            swap[b + 8 + i, b + i] = -1.0
            swap[b + i, b + 8 + i] = 1.0
    shared_2 = np.concatenate([cos, sin, swap], 1).astype(np.float32)
    return {"const": const, "shared_1": shared_1, "shared_2": shared_2}


def kernel(**inputs):
    import concourse.bacc as _bacc
    from concourse.bass_utils import run_bass_kernel_spmd as _run

    nc = _bacc.Bacc("TRN2", target_bir_lowering=False, num_devices=1)
    arrays = {n: np.ascontiguousarray(v) for n, v in {**_layout(inputs), **_constants()}.items()}
    ap = {n: nc.dram_tensor(n, v.shape, mybir.dt.from_np(v.dtype), kind="ExternalInput").ap() for n, v in arrays.items()}
    out = nc.dram_tensor("out", (T, D), F32, kind="ExternalOutput").ap()
    build(nc, ap["x"], ap["wts"], ap["w_ada"], ap["w_g"], ap["w_idx"], ap["rows_a"], ap["rows_b"], ap["rows_wide"], ap["cmp_w2"], ap["const"],
          ap["shared_1"], ap["shared_2"], out)
    r = _run(nc, [arrays], core_ids=[0])
    return r.results[0]["out"].reshape(1, T, D)
```
